# Optimizing a Trainium2 kernel written in Bass

```python
import math
import jax, jax.numpy as jnp
from jax import lax
import numpy as np

D_MODEL = 1024
BATCH = 1
SEQ = 512
DEPTH = 2

PLE_DIM = 256
EPS = 1e-6
BLOCK = 128
SB_HEADS = 8
SB_DIM = 64
SB_WIDTH = SB_HEADS * SB_DIM
HG_HEADS = 4
HG_DK = 128
HG_DV = 128
HG_QK = HG_HEADS * HG_DK
HG_V = HG_HEADS * HG_DV
HG_CHUNK = 64
AB_SPLITS = [SB_WIDTH] * 3 + [HG_QK] * 2 + [HG_V] * 2
AB_IN = sum(AB_SPLITS)
AB_OUT = SB_WIDTH + HG_V
SW_HEADS = 16
SW_KV_HEADS = 4
SW_DIM = 64
SW_GROUP = SW_HEADS // SW_KV_HEADS
WINDOW = 128
C_IN = (SW_HEADS + 2 * SW_KV_HEADS) * SW_DIM
C_OUT = SW_HEADS * SW_DIM
N_BUCKETS = 32
MAX_DISTANCE = 128
D_FF = 2816
CONV_W = 3
N_EVEN = (DEPTH + 1) // 2
N_ODD = DEPTH // 2


def rmsnorm(x, g):
    xf = x.astype(jnp.float32)
    y = xf * lax.rsqrt(jnp.mean(xf * xf, axis=-1, keepdims=True) + EPS)
    return (y * g.astype(jnp.float32)).astype(x.dtype)

def stick_breaking_attention(q, k, v):
    S = q.shape[1]
    qf = jnp.swapaxes(q, 1, 2).astype(jnp.float32)
    kf = jnp.swapaxes(k, 1, 2).astype(jnp.float32)
    vf = jnp.swapaxes(v, 1, 2).astype(jnp.float32)
    scale = SB_DIM ** -0.5
    outs = []
    for n in range(S // BLOCK):
        t0 = n * BLOCK
        kn = t0 + BLOCK
        z = jnp.einsum('bhtd,bhsd->bhts', qf[:, :, t0:kn], kf[:, :, :kn]) * scale
        t_pos = t0 + jnp.arange(BLOCK)[:, None]
        s_pos = jnp.arange(kn)[None, :]
        mask = s_pos < t_pos
        log_keep = jnp.where(mask, jax.nn.log_sigmoid(-z), 0.0)
        later = lax.cumsum(log_keep, axis=3, reverse=True) - log_keep
        w = jnp.where(mask, jnp.exp(jax.nn.log_sigmoid(z) + later), 0.0)
        outs.append(jnp.einsum('bhts,bhsd->bhtd', w, vf[:, :, :kn]))
    o = jnp.concatenate(outs, axis=2)
    return jnp.swapaxes(o, 1, 2)

def hgrn2(q, f_pre, i, lb):
    B, S = q.shape[:2]
    lb = lb.reshape(HG_HEADS, HG_DK).astype(jnp.float32)
    fp = f_pre.astype(jnp.float32)
    log_f = jnp.log(lb + (1.0 - lb) * jax.nn.sigmoid(fp))
    kk = (1.0 - lb) * jax.nn.sigmoid(-fp)
    qf = jax.nn.silu(q.astype(jnp.float32))
    nc = S // HG_CHUNK

    def to_chunks(a):
        return a.reshape(B, nc, HG_CHUNK, HG_HEADS, a.shape[-1]).transpose(1, 0, 3, 2, 4)

    causal = jnp.tril(jnp.ones((HG_CHUNK, HG_CHUNK), dtype=bool))

    def step(state, xs):
        qc, kc, lfc, ic = xs
        b = jnp.cumsum(lfc, axis=2)
        o_inter = jnp.einsum('bhtk,bhkv->bhtv', qc * jnp.exp(b), state)
        rel = jnp.where(causal[:, :, None], b[:, :, :, None, :] - b[:, :, None, :, :], -jnp.inf)
        scores = jnp.einsum('bhtk,bhsk,bhtsk->bhts', qc, kc, jnp.exp(rel))
        o = o_inter + jnp.einsum('bhts,bhsv->bhtv', scores, ic)
        b_last = b[:, :, -1:, :]
        state = jnp.exp(b_last[:, :, 0, :, None]) * state + jnp.einsum('bhsk,bhsv->bhkv', kc * jnp.exp(b_last - b), ic)
        return state, o

    s0 = jnp.zeros((B, HG_HEADS, HG_DK, HG_DV), jnp.float32)
    _, o = lax.scan(step, s0, (to_chunks(qf), to_chunks(kk), to_chunks(log_f), to_chunks(i.astype(jnp.float32))))
    return o.transpose(1, 0, 3, 2, 4).reshape(B, S, HG_HEADS, HG_DV)

def t5_band_buckets():
    t = np.arange(WINDOW)[:, None]
    s = np.arange(2 * WINDOW)[None, :]
    dist = t + WINDOW - s
    band = (dist >= 0) & (dist < WINDOW)
    max_exact = N_BUCKETS // 2
    large = max_exact + (np.log(np.maximum(dist, max_exact) / max_exact) / math.log(MAX_DISTANCE / max_exact) * (N_BUCKETS - max_exact)).astype(np.int32)
    large = np.minimum(large, N_BUCKETS - 1)
    bucket = np.where(dist < max_exact, np.maximum(dist, 0), large).astype(np.int32)
    return bucket, band

def sliding_window_attention(q, k, v, sinks, rel_bias):
    B, S = q.shape[:2]
    nb = S // WINDOW
    bucket, band = t5_band_buckets()
    bias = rel_bias.astype(jnp.float32)[bucket]
    bias = bias.transpose(2, 0, 1).reshape(SW_KV_HEADS, SW_GROUP, WINDOW, 2 * WINDOW)
    key_pos = np.arange(nb)[:, None] * WINDOW - WINDOW + np.arange(2 * WINDOW)[None, :]
    mask = jnp.asarray(band[None] & (key_pos >= 0)[:, None, :])
    qb = q.astype(jnp.float32).reshape(B, nb, WINDOW, SW_KV_HEADS, SW_GROUP, SW_DIM).transpose(1, 0, 2, 3, 4, 5)

    def band_keys(a):
        ap = jnp.pad(a.astype(jnp.float32), ((0, 0), (WINDOW, 0), (0, 0), (0, 0)))
        ap = ap.reshape(B, nb + 1, WINDOW, SW_KV_HEADS, SW_DIM)
        return jnp.concatenate([ap[:, :-1], ap[:, 1:]], axis=2).transpose(1, 0, 2, 3, 4)

    kb, vb = band_keys(k), band_keys(v)
    sink = sinks.astype(jnp.float32).reshape(SW_KV_HEADS, SW_GROUP, 1, 1)
    scale = SW_DIM ** -0.5

    def block_attn(args):
        qn, kn, vn, mn = args
        logits = jnp.einsum('bqhgd,bkhd->bhgqk', qn, kn) * scale + bias
        logits = jnp.where(mn, logits, -jnp.inf)
        m = jnp.maximum(jnp.max(logits, axis=-1, keepdims=True), sink)
        e = jnp.exp(logits - m)
        w = e / (jnp.sum(e, axis=-1, keepdims=True) + jnp.exp(sink - m))
        return jnp.einsum('bhgqk,bkhd->bqhgd', w, vn)

    o = lax.map(block_attn, (qb, kb, vb, mask))
    return o.transpose(1, 0, 2, 3, 4, 5).reshape(B, S, SW_HEADS, SW_DIM)

def mixer_ab(h, w_in, lb, hg_norm, w_out):
    B, S, _ = h.shape
    proj = h @ w_in
    qa, ka, va, qb, fb, ib, gb = jnp.split(proj, np.cumsum(AB_SPLITS)[:-1].tolist(), axis=-1)
    sb_shape = (B, S, SB_HEADS, SB_DIM)
    o_a = stick_breaking_attention(qa.reshape(sb_shape), ka.reshape(sb_shape), va.reshape(sb_shape))
    o_a = o_a.astype(h.dtype).reshape(B, S, SB_WIDTH)
    o_b = hgrn2(qb.reshape(B, S, HG_HEADS, HG_DK), fb.reshape(B, S, HG_HEADS, HG_DK), ib.reshape(B, S, HG_HEADS, HG_DV), lb)
    o_b = rmsnorm(o_b.astype(h.dtype), hg_norm) * jax.nn.silu(gb.reshape(B, S, HG_HEADS, HG_DV))
    o_b = o_b.reshape(B, S, HG_V)
    return jnp.concatenate([o_a, o_b], axis=-1) @ w_out

def mixer_c(h, w_in, q_norm, k_norm, sinks, rel_bias, w_out):
    B, S, _ = h.shape
    proj = h @ w_in
    q, k, v = jnp.split(proj, [SW_HEADS * SW_DIM, (SW_HEADS + SW_KV_HEADS) * SW_DIM], axis=-1)
    q = rmsnorm(q.reshape(B, S, SW_HEADS, SW_DIM), q_norm)
    k = rmsnorm(k.reshape(B, S, SW_KV_HEADS, SW_DIM), k_norm)
    v = v.reshape(B, S, SW_KV_HEADS, SW_DIM)
    o = sliding_window_attention(q, k, v, sinks, rel_bias).astype(h.dtype)
    return o.reshape(B, S, C_OUT) @ w_out

def conv_glu_ffn(h, w_up, conv_w, conv_b, w_down):
    u = h @ w_up
    u = lax.conv_general_dilated(u, conv_w[:, None, :], window_strides=(1,), padding=[(CONV_W - 1, 0)],
                                 dimension_numbers=('NWC', 'WIO', 'NWC'), feature_group_count=2 * D_FF) + conv_b
    gate, up = jnp.split(u, 2, axis=-1)
    return (jax.nn.silu(gate) * up) @ w_down

def first_inputs(seed: int = 0) -> dict:
    key = jax.random.key(seed)
    ks = jax.random.split(key, 21)

    def nrm(k, shape):
        return jax.random.normal(k, shape, jnp.float32)

    def w(k, shape, fan_in):
        return nrm(k, shape) * fan_in ** -0.5

    def gain(k, shape):
        return 1.0 + 0.02 * nrm(k, shape)

    F2 = 2 * D_FF
    return {
        'x': nrm(ks[0], (BATCH, SEQ, D_MODEL)),
        'p': nrm(ks[1], (DEPTH, BATCH, SEQ, PLE_DIM)),
        'mix_norm': gain(ks[2], (DEPTH, D_MODEL)),
        'ab_w_in': w(ks[3], (N_EVEN, D_MODEL, AB_IN), D_MODEL),
        'hg_lb_logits': 0.5 * nrm(ks[4], (N_EVEN, HG_QK)),
        'hg_out_norm': gain(ks[5], (N_EVEN, HG_DV)),
        'ab_w_out': w(ks[6], (N_EVEN, AB_OUT, D_MODEL), AB_OUT),
        'c_w_in': w(ks[7], (N_ODD, D_MODEL, C_IN), D_MODEL),
        'q_norm': gain(ks[8], (N_ODD, SW_DIM)),
        'k_norm': gain(ks[9], (N_ODD, SW_DIM)),
        'sinks': 0.5 * nrm(ks[10], (N_ODD, SW_HEADS)),
        'rel_bias': 0.5 * nrm(ks[11], (N_BUCKETS, SW_HEADS)),
        'c_w_out': w(ks[12], (N_ODD, C_OUT, D_MODEL), C_OUT),
        'ffn_norm': gain(ks[13], (DEPTH, D_MODEL)),
        'ffn_up': w(ks[14], (DEPTH, D_MODEL, F2), D_MODEL),
        'ffn_conv': w(ks[15], (DEPTH, CONV_W, F2), CONV_W),
        'ffn_conv_b': 0.02 * nrm(ks[16], (DEPTH, F2)),
        'ffn_down': w(ks[17], (DEPTH, D_FF, D_MODEL), D_FF),
        'ple_norm': gain(ks[18], (DEPTH, D_MODEL)),
        'ple_gate': w(ks[19], (DEPTH, D_MODEL, D_MODEL), D_MODEL),
        'ple_proj': w(ks[20], (DEPTH, PLE_DIM, D_MODEL), PLE_DIM),
    }

def first_block(x, p, mix_norm, ab_w_in, hg_lb_logits, hg_out_norm, ab_w_out, c_w_in, q_norm, k_norm,
              sinks, rel_bias, c_w_out, ffn_norm, ffn_up, ffn_conv, ffn_conv_b, ffn_down,
              ple_norm, ple_gate, ple_proj):
    lb_cum = jnp.cumsum(jax.nn.softmax(hg_lb_logits.astype(jnp.float32), axis=0), axis=0)
    lower_bounds = lb_cum - lb_cum[0]
    h = x
    for i in range(DEPTH):
        j = i // 2
        hn = rmsnorm(h, mix_norm[i])
        if i % 2 == 0:
            h = h + mixer_ab(hn, ab_w_in[j], lower_bounds[j], hg_out_norm[j], ab_w_out[j])
        else:
            h = h + mixer_c(hn, c_w_in[j], q_norm[j], k_norm[j], sinks[j], rel_bias, c_w_out[j])
        h = h + conv_glu_ffn(rmsnorm(h, ffn_norm[i]), ffn_up[i], ffn_conv[i], ffn_conv_b[i], ffn_down[i])
        gate = jax.nn.sigmoid(rmsnorm(h, ple_norm[i]) @ ple_gate[i])
        h = h + gate * (p[i] @ ple_proj[i])
    return h


DEPTH_2 = 1

CHUNK = 64
Q_BLOCK = 128

DIFF_HEADS = 8
DIFF_DH = 64
DIFF_W = DIFF_HEADS * 2 * DIFF_DH

CH_HEADS = 8
CH_DH = 64
CH_W = CH_HEADS * CH_DH
CH_LEFT = 8
REL_CLIP = 128

PEER_HEADS = 8
PEER_NKEYS = 128
PEER_NEXP = PEER_NKEYS * PEER_NKEYS
PEER_DKEY = 128
PEER_TOPK = 16
PEER_BLOCK = 128

IN_SIZES = (DIFF_W, DIFF_W, DIFF_W, CH_W, CH_W, CH_W, D_MODEL, D_MODEL)
IN_COLS = sum(IN_SIZES)
IN_SPLITS = tuple(int(s) for s in np.cumsum(IN_SIZES)[:-1])


def rmsnorm_2(x, w):
    xf = x.astype(jnp.float32)
    y = xf * lax.rsqrt(jnp.mean(xf * xf, axis=-1, keepdims=True) + EPS)
    return (y * w.astype(jnp.float32)).astype(x.dtype)

def alibi_slopes(n_heads):
    return jnp.exp2(-8.0 * jnp.arange(1, n_heads + 1, dtype=jnp.float32) / n_heads)

def diff_attention(q, k, v, lq1, lk1, lq2, lk2, subln_w, lam_init):
    B, S = q.shape[0], q.shape[1]
    nqb = S // Q_BLOCK
    f32 = jnp.float32
    lam = (jnp.exp(jnp.sum(lq1.astype(f32) * lk1.astype(f32)))
           - jnp.exp(jnp.sum(lq2.astype(f32) * lk2.astype(f32))) + lam_init)
    k1, k2 = k[..., 0, :], k[..., 1, :]
    qb = jnp.moveaxis(q.reshape(B, nqb, Q_BLOCK, DIFF_HEADS, 2, DIFF_DH), 1, 0)
    slopes = alibi_slopes(DIFF_HEADS)
    kpos = jnp.arange(S, dtype=jnp.int32)
    scale = DIFF_DH ** -0.5

    def block(args):
        qblk, bi = args
        qpos = bi * Q_BLOCK + jnp.arange(Q_BLOCK, dtype=jnp.int32)
        dist = jnp.abs(qpos[:, None] - kpos[None, :]).astype(f32)
        bias = -slopes[:, None, None] * dist
        allowed = (kpos[None, :] // CHUNK) <= (qpos[:, None] // CHUNK)

        def probs(qq, kk):
            s = jnp.einsum('bqhd,bkhd->bhqk', qq, kk).astype(f32) * scale + bias
            return jax.nn.softmax(jnp.where(allowed, s, -jnp.inf), axis=-1)

        a = probs(qblk[..., 0, :], k1) - lam * probs(qblk[..., 1, :], k2)
        return jnp.einsum('bhqk,bkhe->bqhe', a.astype(v.dtype), v)

    o = lax.map(block, (qb, jnp.arange(nqb, dtype=jnp.int32)))
    o = jnp.moveaxis(o, 0, 1).reshape(B, S, DIFF_HEADS, 2 * DIFF_DH)
    o = rmsnorm_2(o, subln_w) * (1.0 - lam_init)
    return o.reshape(B, S, DIFF_W)

def chunk_attention(q, k, v, rel_table):
    B, S = q.shape[0], q.shape[1]
    nc = S // CHUNK
    band = (CH_LEFT + 1) * CHUNK
    f32 = jnp.float32
    qc = q.reshape(B, nc, CHUNK, CH_HEADS, CH_DH)
    pad = ((0, 0), (CH_LEFT * CHUNK, 0), (0, 0), (0, 0))
    kp = jnp.pad(k, pad).reshape(B, nc + CH_LEFT, CHUNK, CH_HEADS, CH_DH)
    vp = jnp.pad(v, pad).reshape(B, nc + CH_LEFT, CHUNK, CH_HEADS, CH_DH)
    kb = jnp.concatenate([kp[:, j:j + nc] for j in range(CH_LEFT + 1)], axis=2)
    vb = jnp.concatenate([vp[:, j:j + nc] for j in range(CH_LEFT + 1)], axis=2)
    r = jnp.arange(band, dtype=jnp.int32)
    qi = jnp.arange(CHUNK, dtype=jnp.int32)
    rel = qi[:, None] - r[None, :] + CH_LEFT * CHUNK
    bias = rel_table[:, jnp.clip(rel, -REL_CLIP, REL_CLIP) + REL_CLIP].astype(f32)
    valid = (jnp.arange(nc, dtype=jnp.int32)[:, None] * CHUNK - CH_LEFT * CHUNK + r[None, :]) >= 0
    s = jnp.einsum('bcqhd,bckhd->bhcqk', qc, kb).astype(f32) * (CH_DH ** -0.5) + bias[:, None]
    s = jnp.where(valid[:, None, :], s, -jnp.inf)
    p = jax.nn.softmax(s, axis=-1)
    o = jnp.einsum('bhcqk,bckhd->bcqhd', p.astype(v.dtype), vb)
    return o.reshape(B, S, CH_W)

def peer(xn, wq, keys, u, v):
    B, S, D = xn.shape
    xt = xn.reshape(-1, PEER_BLOCK, D)
    f32 = jnp.float32

    def block(xb):
        q = (xb @ wq).reshape(PEER_BLOCK, PEER_HEADS, 2, PEER_DKEY // 2)
        s1 = jnp.einsum('thd,hnd->thn', q[:, :, 0], keys[:, 0]).astype(f32)
        s2 = jnp.einsum('thd,hnd->thn', q[:, :, 1], keys[:, 1]).astype(f32)
        v1, i1 = lax.top_k(s1, PEER_TOPK)
        v2, i2 = lax.top_k(s2, PEER_TOPK)
        cand = (v1[..., :, None] + v2[..., None, :]).reshape(PEER_BLOCK, PEER_HEADS, PEER_TOPK * PEER_TOPK)
        sc, ci = lax.top_k(cand, PEER_TOPK)
        e = (jnp.take_along_axis(i1, ci // PEER_TOPK, axis=-1) * PEER_NKEYS
             + jnp.take_along_axis(i2, ci % PEER_TOPK, axis=-1))
        g = jax.nn.softmax(sc, axis=-1)
        ue = u[e]
        ve = v[e]
        hid = jnp.einsum('thkd,td->thk', ue, xb).astype(f32)
        a = (jax.nn.gelu(hid, approximate=False) * g).astype(xb.dtype)
        return jnp.einsum('thk,thkd->td', a, ve)

    return lax.map(block, xt).reshape(B, S, D)

def second_inputs(seed: int = 0) -> dict:
    key = jax.random.key(seed)
    ks = jax.random.split(key, 20)
    n = jax.random.normal
    f32 = jnp.float32
    L, D = DEPTH_2, D_MODEL
    return {
        "x": n(ks[0], (BATCH, SEQ, D), f32),
        "norm1_w": 1.0 + 0.02 * n(ks[1], (L, D), f32),
        "w_in": n(ks[2], (L, D, IN_COLS), f32) * D ** -0.5,
        "b_gate": 0.01 * n(ks[3], (L, 2 * D), f32),
        "diff_lq1": 0.1 * n(ks[4], (L, DIFF_DH), f32),
        "diff_lk1": 0.1 * n(ks[5], (L, DIFF_DH), f32),
        "diff_lq2": 0.1 * n(ks[6], (L, DIFF_DH), f32),
        "diff_lk2": 0.1 * n(ks[7], (L, DIFF_DH), f32),
        "diff_subln_w": 1.0 + 0.02 * n(ks[8], (L, 2 * DIFF_DH), f32),
        "chunk_rel_bias": 0.1 * n(ks[9], (L, CH_HEADS, 2 * REL_CLIP + 1), f32),
        "w_branch_diff": n(ks[10], (L, DIFF_W, D), f32) * DIFF_W ** -0.5,
        "w_branch_chunk": n(ks[11], (L, CH_W, D), f32) * CH_W ** -0.5,
        "w_out": n(ks[12], (L, D, D), f32) * D ** -0.5,
        "norm2_w": 1.0 + 0.02 * n(ks[13], (L, D), f32),
        "peer_wq": n(ks[14], (L, D, PEER_HEADS * PEER_DKEY), f32) * D ** -0.5,
        "peer_keys": n(ks[15], (L, PEER_HEADS, 2, PEER_NKEYS, PEER_DKEY // 2), f32) * (PEER_DKEY // 2) ** -0.5,
        "peer_u": n(ks[16], (L, PEER_NEXP, D), f32) * D ** -0.5,
        "peer_v": n(ks[17], (L, PEER_NEXP, D), f32) * D ** -0.5,
        "final_norm_w": 1.0 + 0.02 * n(ks[18], (D,), f32),
    }

def second_block(x, norm1_w, w_in, b_gate, diff_lq1, diff_lk1, diff_lq2, diff_lk2, diff_subln_w,
              chunk_rel_bias, w_branch_diff, w_branch_chunk, w_out, norm2_w, peer_wq, peer_keys,
              peer_u, peer_v, final_norm_w):
    B, S, D = x.shape
    h = x
    for l in range(DEPTH_2):
        lam_init = 0.8 - 0.6 * math.exp(-0.3 * l)
        xn = rmsnorm_2(h, norm1_w[l])
        proj = xn @ w_in[l]
        qd, kd, vd, qc, kc, vc, gd, gc = jnp.split(proj, IN_SPLITS, axis=-1)
        o_d = diff_attention(qd.reshape(B, S, DIFF_HEADS, 2, DIFF_DH),
                             kd.reshape(B, S, DIFF_HEADS, 2, DIFF_DH),
                             vd.reshape(B, S, DIFF_HEADS, 2 * DIFF_DH),
                             diff_lq1[l], diff_lk1[l], diff_lq2[l], diff_lk2[l], diff_subln_w[l], lam_init)
        o_c = chunk_attention(qc.reshape(B, S, CH_HEADS, CH_DH), kc.reshape(B, S, CH_HEADS, CH_DH),
                              vc.reshape(B, S, CH_HEADS, CH_DH), chunk_rel_bias[l])
        g_d = jax.nn.sigmoid(gd + b_gate[l, :D])
        g_c = jax.nn.sigmoid(gc + b_gate[l, D:])
        merged = g_d * (o_d @ w_branch_diff[l]) + g_c * (o_c @ w_branch_chunk[l])
        h = h + merged @ w_out[l]
        h = h + peer(rmsnorm_2(h, norm2_w[l]), peer_wq[l], peer_keys[l], peer_u[l], peer_v[l])
    return rmsnorm_2(h, final_norm_w)


def setup_inputs(seed=0):
    out = dict(first_inputs(seed))
    for name, value in second_inputs(seed + 1).items():
        if name != "x":
            out[name + "_2"] = value
    return out


def reference(
    x, p, mix_norm, ab_w_in, hg_lb_logits, hg_out_norm, ab_w_out, c_w_in, q_norm, k_norm, sinks,
    rel_bias, c_w_out, ffn_norm, ffn_up, ffn_conv, ffn_conv_b, ffn_down, ple_norm, ple_gate,
    ple_proj, norm1_w_2, w_in_2, b_gate_2, diff_lq1_2, diff_lk1_2, diff_lq2_2, diff_lk2_2,
    diff_subln_w_2, chunk_rel_bias_2, w_branch_diff_2, w_branch_chunk_2, w_out_2, norm2_w_2,
    peer_wq_2, peer_keys_2, peer_u_2, peer_v_2, final_norm_w_2,
):
    x = first_block(
        x, p, mix_norm, ab_w_in, hg_lb_logits, hg_out_norm, ab_w_out, c_w_in, q_norm, k_norm,
        sinks, rel_bias, c_w_out, ffn_norm, ffn_up, ffn_conv, ffn_conv_b, ffn_down, ple_norm,
        ple_gate, ple_proj,
    )
    return second_block(
        x, norm1_w_2, w_in_2, b_gate_2, diff_lq1_2, diff_lk1_2, diff_lq2_2, diff_lk2_2,
        diff_subln_w_2, chunk_rel_bias_2, w_branch_diff_2, w_branch_chunk_2, w_out_2, norm2_w_2,
        peer_wq_2, peer_keys_2, peer_u_2, peer_v_2, final_norm_w_2,
    )


_drawn_inputs = setup_inputs


def setup_inputs(seed=0):
    import zlib

    import numpy as np

    out = dict(_drawn_inputs(seed))
    spreads = {}
    factors = {'mix_norm': 3.307,
     'hg_out_norm': 5.742,
     'q_norm': 8.0,
     'k_norm': 8.0,
     'sinks': 8.0,
     'ffn_norm': 3.113,
     'ffn_conv_b': 3.078,
     'ple_norm': 8.0,
     'norm1_w_2': 6.333,
     'b_gate_2': 8.0,
     'diff_lq1_2': 8.0,
     'diff_lk1_2': 5.402,
     'diff_lq2_2': 4.599,
     'diff_lk2_2': 3.41,
     'diff_subln_w_2': 8.0,
     'chunk_rel_bias_2': 8.0,
     'norm2_w_2': 8.0,
     'peer_wq_2': 6.434,
     'peer_keys_2': 6.447,
     'peer_u_2': 7.09,
     'peer_v_2': 6.433,
     'final_norm_w_2': 2.782}
    for name, (base, spread) in spreads.items():
        noise = np.random.default_rng([zlib.crc32(name.encode()), seed]).standard_normal(out[name].shape)
        drawn = base * np.exp(spread * noise) if base else spread * noise
        out[name] = __import__('jax').numpy.asarray(drawn.astype(out[name].dtype))
    for name, factor in factors.items():
        out[name] = (out[name] * factor).astype(out[name].dtype)
    return out
```

```python
import math
from contextlib import ExitStack

import numpy as np

import concourse.bass as bass
import concourse.mybir as mybir

F32 = mybir.dt.float32
U32 = mybir.dt.uint32
I32 = mybir.dt.int32
ACT = mybir.ActivationFunctionType
ALU = mybir.AluOpType
AX = mybir.AxisListType

P = 128
TOKENS = 512
BLOCKS = TOKENS // P
D_MODEL = 1024
D_TILES = D_MODEL // P
EPS = 1e-6

RING = 4
SLOT_TILES = 16
SLOT = SLOT_TILES * P

SB_HEADS, SB_DIM = 8, 64
HG_HEADS = 4
SW_HEADS, SW_KV = 16, 4
BUCKETS, WINDOW, MAX_DISTANCE = 32, 128, 128
FF_TILES = 2816 // P
CONV = 3
PLE_TILES = 2
DIFF_HEADS = 8
CH_HEADS, REL_CLIP = 8, 128
PEER_HEADS, PEER_KEYS, TOPK = 8, 128, 16
GROUP = 8
GROUPS = PEER_KEYS // GROUP
CHUNK_TOKENS = 64
CHUNKS = TOKENS // CHUNK_TOKENS
LAM_INIT = 0.8 - 0.6 * math.exp(-0.3 * 0)
NEG = -1e30

CONST_WIDTHS = dict(ident=P, ones=P, neg_tri=P, neg_ones=P, neg_mask=P, strict=P, head_pair=P, iota=P,
                    distance=TOKENS, restart=TOKENS, level_masks=8 * P, slopes=DIFF_HEADS, eps=1,
                    bucket_rows=2 * WINDOW + P - 1)
COLUMN_WIDTHS = dict(mix0=8, mix1=8, ffn0=8, ffn1=8, ple0=8, ple1=8, norm1=8, norm2=8, final=8,
                     hg_norm=1, q_norm=1, k_norm=1, subln=1, lb=HG_HEADS, b_gate=16,
                     conv0=3 * 44, conv1=3 * 44, conv_b0=44, conv_b1=44,
                     sinks=SW_HEADS, lambdas=4 * 64, rel_bias=SW_HEADS)


def offsets(widths):
    at, out = 0, {}
    for name, width in widths.items():
        out[name] = (at, width)
        at += width
    return out, at


CONST_AT, CONST_N = offsets(CONST_WIDTHS)
COLUMN_AT, COLUMN_N = offsets(COLUMN_WIDTHS)


def t5_bucket(distance):
    exact = BUCKETS // 2
    large = exact + (np.log(np.maximum(distance, exact) / exact) / math.log(MAX_DISTANCE / exact)
                     * (BUCKETS - exact)).astype(np.int32)
    return np.where(distance < exact, np.maximum(distance, 0), np.minimum(large, BUCKETS - 1))


def constants():
    row, col = np.arange(P)[:, None], np.arange(P)[None, :]
    c = {}
    c["ident"] = row == col
    c["ones"] = np.ones((P, P))
    c["neg_tri"] = np.where(row >= col, -1.0, 0.0)
    c["neg_ones"] = -np.ones((P, P))
    c["neg_mask"] = np.where(row >= col, NEG, 0.0)
    c["strict"] = row < col
    c["head_pair"] = (row // 64) == (col // 64)
    c["iota"] = np.broadcast_to(col, (P, P))
    y = np.arange(TOKENS)[None, :]
    c["distance"] = np.where((row < 64) & (y >= 448), 1e32, np.abs(row + 384 - y))
    c["restart"] = np.broadcast_to(y % P != 0, (P, TOKENS))
    levels = [((row // (2 * m)) == (col // (2 * m))) & (row % (2 * m) < m) & (col % (2 * m) >= m)
              for m in (64, 32, 16, 8, 4, 2, 1)]
    c["level_masks"] = np.concatenate(levels + [row == col], axis=1)
    c["slopes"] = np.broadcast_to(-np.exp2(-8.0 * np.arange(1, 9) / DIFF_HEADS), (P, DIFF_HEADS))
    c["eps"] = np.full((P, 1), EPS)
    u = np.arange(2 * WINDOW + P - 1)[None, :]
    distance = 2 * WINDOW - 1 - u
    band = (distance >= 0) & (distance < WINDOW)
    c["bucket_rows"] = np.where(row < BUCKETS, (t5_bucket(distance) == row) & band,
                                np.where((row == BUCKETS) & ~band, NEG, 0.0))
    return np.concatenate([np.broadcast_to(c[n], (P, w)).astype(np.float32)
                           for n, w in CONST_WIDTHS.items()], axis=1)


class Stage:

    def __init__(self, tensor=None, vector=None, scalar=None, gpsimd=None, meet=True):
        self.tensor, self.vector, self.scalar, self.gpsimd, self.meet = tensor, vector, scalar, gpsimd, meet


class Arena:

    def __init__(self, memory, at=0):
        self.memory, self.at = memory, at

    def take(self, columns):
        self.at += columns
        assert self.at <= self.memory.shape[1], (self.at, self.memory.shape)
        return self.memory[:, self.at - columns:self.at]


def cut(ap, start, size):
    return ap[:, bass.ds(start, size)]


def after(signals):
    return signals + 1


def over_slots(eng, first, count, step):
    rounds = count // RING if count >= 2 * RING else 0
    if rounds:
        with eng.Fori(0, rounds) as r:
            for j in range(RING):
                step(j, r * RING + j, (first + j) % RING, r + (first + j) // RING)
    for j in range(RING * rounds, count):
        step(j % RING, j, (first + j) % RING, (first + j) // RING)


class Core:

    def __init__(self, nc, ctx, dram):
        self.nc, self.ctx, self.dram = nc, ctx, dram
        self.period = None
        self.h = self.sbuf("residual", [P, D_TILES * TOKENS])
        self.hn = self.sbuf("normed", [P, D_TILES * TOKENS])
        self.ring = self.sbuf("weight_ring", [P, RING * SLOT])
        self.consts = self.sbuf("constants", [P, CONST_N])
        self.columns = self.sbuf("columns", [P, COLUMN_N])
        self.work = self.sbuf("work", [P, 32256])
        self.banks = ctx.enter_context(nc.psum_tensor("banks", [P, 8, 512], F32))
        self.weights_in = [self.sem(f"weights_in_{i}") for i in range(RING)]
        self.weights_used = [self.sem(f"weights_used_{i}") for i in range(RING)]
        self.meetings = self.sem("meetings")
        self.inputs_in = self.sem("inputs_in")
        self.held = self.sem("held")
        self.slots = 0

    def sbuf(self, name, shape):
        return self.ctx.enter_context(self.nc.sbuf_tensor(name, shape, F32))

    def sem(self, name):
        if self.period is None:
            return self.ctx.enter_context(self.nc.semaphore(name))
        self.period_sems.append(self.period.enter_context(self.nc.semaphore(name)))
        return self.period_sems[-1]

    def sem_from_one(self, name):
        self.from_one.append(self.sem(name))
        return self.from_one[-1]

    def plan(self, periods):
        stages, before = [], []
        for make in periods:
            if len(before) == 2:
                before.pop(0)[0].close()
            self.period, self.period_sems, self.from_one = ExitStack(), [], []
            made = make()
            made.insert(0, Stage(gpsimd=self.opening(before[-1][1] if before else [], self.from_one), meet=False))
            before.append((self.period, self.period_sems))
            stages += made
        for period, _ in before:
            period.close()
        self.period = None
        return stages

    @staticmethod
    def opening(cleared, from_one):
        def gpsimd(pool):
            for sem in cleared:
                pool.sem_clear(sem)
            for sem in from_one:
                pool.sem_inc(sem, 1)
        return gpsimd

    def const(self, name):
        at, width = CONST_AT[name]
        return self.consts[:, at:at + width]

    def column(self, name, index=None):
        at, width = COLUMN_AT[name]
        if index is None:
            return self.columns[:, at:at + width]
        return cut(self.columns, at + index, 1)

    def tile(self, place, n):
        return self.ring[:, place * SLOT + n * P:place * SLOT + (n + 1) * P]

    def hold(self, eng):
        eng.sem_inc(self.held, 1)

    def take_slots(self, count):
        first = self.slots
        self.slots += count
        return first

    def slot_begins(self, pe, place, turn):
        pe.wait_ge(self.weights_in[place], turn * 16 + 16)

    def release_previous(self, matmul, place):
        matmul.then_inc(self.weights_used[(place - 1) % RING], 1)


def projection(k, name, n_tiles, ktiles, source, evacuate, engine="scalar", banks=(0, 1, 2, 3), meet=False):
    slots = n_tiles * ktiles // SLOT_TILES
    per_slot = SLOT_TILES // ktiles
    first = k.take_slots(slots)
    nb = len(banks)
    bank_filled, bank_free = k.sem(name + "_bank_filled"), k.sem(name + "_bank_free")

    def tensor(pe):
        def step(j, slot, place, turn):
            k.slot_begins(pe, place, turn)
            for n in range(per_slot):
                pe.wait_ge(bank_free, slot * per_slot + (n + 1))
                bank = k.banks[:, banks[(j * per_slot + n) % nb], :]
                for kk in range(ktiles):
                    mm = k.nc.tensor.matmul(bank, k.tile(place, n * ktiles + kk), source(kk),
                                            start=kk == 0, stop=kk == ktiles - 1)
                    if n == 0 and kk == 0:
                        k.release_previous(mm, place)
                mm.then_inc(bank_filled, 1)
        over_slots(pe, first, slots, step)

    def reader(eng):
        eng.sem_inc(bank_free, nb)

        def step(j, slot, place, turn):
            for n in range(per_slot):
                tile = slot * per_slot + n
                eng.wait_ge(bank_filled, tile + 1)
                evacuate(eng, k.banks[:, banks[(j * per_slot + n) % nb], :], tile).then_inc(bank_free, 1)
        over_slots(eng, first, slots, step)

    return Stage(tensor=tensor, meet=meet, **{engine: reader})


def token_projection(k, name, slots, source, out, width, meet=False):
    first = k.take_slots(slots)
    filled, free = k.sem(name + "_banks_filled"), k.sem(name + "_banks_free")
    both = [k.banks[:, 4 + 2 * i:6 + 2 * i, :].rearrange("p b (h n) -> p (b h) n", h=2) for i in range(2)]

    def tensor(pe):
        def step(j, slot, place, turn):
            k.slot_begins(pe, place, turn)
            pe.wait_ge(free, slot + 1)
            weights = k.ring[:, place * SLOT:(place + 1) * SLOT].rearrange("p (n k c) -> p n k c", n=2, k=D_TILES)
            for b in range(BLOCKS):
                for kk in range(D_TILES):
                    mm = k.nc.tensor.matmul(both[j % 2][:, b, :], source(kk)[:, b * P:(b + 1) * P],
                                            weights[:, :, kk, :], start=kk == 0, stop=kk == D_TILES - 1)
                    if b == 0 and kk == 0:
                        k.release_previous(mm, place)
            mm.then_inc(filled, 1)
        over_slots(pe, first, slots, step)

    def scalar(act):
        act.sem_inc(free, 2)
        rows = out.rearrange("p (b n) -> p b n", b=BLOCKS)

        def step(j, slot, place, turn):
            act.wait_ge(filled, slot + 1)
            k.nc.scalar.activation(rows[:, :, bass.ds(slot * 256, 256)], both[j % 2][:, :, :],
                                   ACT.Copy).then_inc(free, 1)
        over_slots(act, first, slots, step)

    return Stage(tensor=tensor, scalar=scalar, meet=meet)


def tile_of(memory):
    return lambda n: cut(memory, n * TOKENS, TOKENS)


def copy_into(k, memory, scale=1.0):
    def evacuate(act, bank, tile):
        return k.nc.scalar.activation(cut(memory, tile * TOKENS, TOKENS), bank, ACT.Copy, scale=scale)
    return evacuate


def add_to_residual(k):
    def evacuate(dve, bank, tile):
        h = cut(k.h, tile * TOKENS, TOKENS)
        return k.nc.vector.tensor_tensor(h, bank, h, ALU.add)
    return evacuate


def norm(k, name, gain, temp, out=None):
    out = k.hn if out is None else out
    squares, total, deviation, rstd = temp[:, 0:8 * 512], temp[:, 4096:4608], temp[:, 4608:5120], temp[:, 5120:5632]
    squared, summed, totalled, rooted, ready = (k.sem(f"{name}_{s}") for s in
                                                ("squared", "summed", "totalled", "rooted", "ready"))

    def scalar(act):
        for i in range(D_TILES):
            k.nc.scalar.activation(cut(squares, i * 512, 512), cut(k.h, i * 512, 512), ACT.Square).then_inc(squared, 1)
        act.wait_ge(totalled, 1)
        k.nc.scalar.activation(deviation, k.banks[:, 0, :], ACT.Sqrt, bias=k.const("eps"),
                               scale=1.0 / D_MODEL).then_inc(rooted, 1)

    def vector(dve):
        for i in range(1, D_TILES):
            dve.wait_ge(squared, i + 1)
            if i > 1:
                dve.wait_ge(summed, i - 1)
            other = cut(squares, 0, 512) if i == 1 else total
            k.nc.vector.tensor_tensor(total, other, cut(squares, i * 512, 512), ALU.add).then_inc(summed, 1)
        dve.wait_ge(rooted, 1)
        k.nc.vector.reciprocal(rstd, deviation).then_inc(ready, 1)
        dve.wait_ge(ready, 1)
        for i in range(D_TILES):
            k.nc.vector.scalar_tensor_tensor(out=cut(out, i * 512, 512), in0=cut(k.h, i * 512, 512),
                                             scalar=k.column(gain, i), in1=rstd, op0=ALU.mult, op1=ALU.mult)

    def tensor(pe):
        pe.wait_ge(summed, D_TILES - 1)
        k.nc.tensor.matmul(k.banks[:, 0, :], k.const("ones"), total, start=True, stop=True).then_inc(totalled, 1)

    return Stage(tensor=tensor, vector=vector, scalar=scalar)


def feed_forward(k, layer):
    name = f"ffn{layer}"
    arena = Arena(k.work)
    act_in = arena.take(FF_TILES * TOKENS)
    gate, up, silu = arena.take(2 * 512), arena.take(2 * 512), arena.take(2 * 512)
    filled, free = k.sem(name + "_pair_filled"), k.sem(name + "_pair_free")
    conv_done, silu_done, multiplied, dve_order = (k.sem(f"{name}_{s}") for s in
                                                   ("conv_done", "silu_done", "multiplied", "vector_order"))
    first = k.take_slots(FF_TILES)
    taps, bias = f"conv{layer}", f"conv_b{layer}"

    def tensor(pe):
        def step(j, slot, place, turn):
            k.slot_begins(pe, place, turn)
            pe.wait_ge(free, slot + 1)
            for n in range(2):
                for kk in range(D_TILES):
                    mm = k.nc.tensor.matmul(k.banks[:, 2 * (j % 2) + n, :], k.tile(place, n * D_TILES + kk),
                                            cut(k.hn, kk * 512, 512), start=kk == 0, stop=kk == D_TILES - 1)
                    if n == 0 and kk == 0:
                        k.release_previous(mm, place)
            mm.then_inc(filled, 1)
        over_slots(pe, first, FF_TILES, step)

    def vector(dve):
        dve.sem_inc(free, 2)
        dve.sem_inc(silu_done, 2)

        def step(j, slot, place, turn):
            dve.wait_ge(filled, slot + 1)
            dve.wait_ge(silu_done, slot + 1)
            p = j % 2
            for tap in (2, 1, 0):
                s = CONV - 1 - tap
                for half, (buffer, at) in enumerate(((gate, 0), (up, FF_TILES))):
                    bank = k.banks[:, 2 * p + half, :]
                    y = buffer[:, p * 512 + s:(p + 1) * 512]
                    weight = k.column(taps, slot + (tap * 2 * FF_TILES + at))
                    if s == 0:
                        ins = k.nc.vector.tensor_scalar(y, bank, weight, k.column(bias, slot + at), ALU.mult, ALU.add)
                    else:
                        ins = k.nc.vector.scalar_tensor_tensor(out=y, in0=bank[:, 0:512 - s], scalar=weight, in1=y,
                                                               op0=ALU.mult, op1=ALU.add)
                    if s < 2:
                        ins.then_inc(dve_order, 1)
                    elif half == 1:
                        ins.then_inc(conv_done, 1)
                if s < 2:
                    dve.wait_ge(dve_order, slot * 4 + (2 * s + 2))
            dve.wait_ge(conv_done, slot + 1)
            dve.sem_inc(free, 1)
            dve.wait_ge(silu_done, slot + 3)
            k.nc.vector.tensor_tensor(cut(act_in, slot * 512, 512), silu[:, p * 512:(p + 1) * 512],
                                      up[:, p * 512:(p + 1) * 512], ALU.mult).then_inc(multiplied, 1)
            dve.wait_ge(multiplied, slot + 1)
        over_slots(dve, first, FF_TILES, step)

    def scalar(act):
        def step(j, slot, place, turn):
            p = j % 2
            act.wait_ge(conv_done, slot + 1)
            k.nc.scalar.activation(silu[:, p * 512:(p + 1) * 512], gate[:, p * 512:(p + 1) * 512],
                                   ACT.Silu).then_inc(silu_done, 1)
        over_slots(act, first, FF_TILES, step)

    up_stage = Stage(tensor=tensor, vector=vector, scalar=scalar)

    down_first = k.take_slots(FF_TILES // 2)
    down_filled = k.sem(name + "_down_filled")

    def down_tensor(pe):
        def step(j, slot, place, turn, last=False):
            k.slot_begins(pe, place, turn)
            for kk in range(2):
                for n in range(D_TILES):
                    mm = k.nc.tensor.matmul(k.banks[:, n, :], k.tile(place, kk * D_TILES + n),
                                            cut(act_in, (slot * 2 + kk) * 512, 512),
                                            start=(kk == 0 and first_slot), stop=(kk == 1 and last),
                                            skip_group_check=True)
                    if kk == 0 and n == 0:
                        k.release_previous(mm, place)
                    if kk == 1 and last:
                        mm.then_inc(down_filled, 1)
        count = FF_TILES // 2
        first_slot = True
        step(0, 0, down_first % RING, down_first // RING)
        first_slot = False
        rounds = (count - 2) // RING
        with pe.Fori(0, rounds) as r:
            for j in range(RING):
                g = down_first + 1 + j
                step(j, r * RING + (1 + j), g % RING, r + g // RING)
        for s in range(1 + rounds * RING, count):
            g = down_first + s
            step(0, s, g % RING, g // RING, last=s == count - 1)

    def down_vector(dve):
        for n in range(D_TILES):
            dve.wait_ge(down_filled, n + 1)
            add_to_residual(k)(dve, k.banks[:, n, :], n)

    return [up_stage, Stage(tensor=down_tensor, vector=down_vector)]


def layer_embedding(k, layer):
    name = f"ple{layer}"
    arena = Arena(k.work, 11 * 512)
    embedding, gates = arena.take(PLE_TILES * 512), arena.take(D_TILES * 512)
    product = arena.take(2 * 512)
    loaded, order = k.sem(name + "_embedding_in"), k.sem(name + "_product_order")

    def load(act):
        act.dma_start(embedding.rearrange("p (c t) -> p c t", c=PLE_TILES), k.dram["p"][layer]).then_inc(loaded, 16)

    def gate(act, bank, tile):
        return k.nc.scalar.activation(cut(gates, tile * 512, 512), bank, ACT.Sigmoid)

    def add(dve, bank, tile):
        if tile == 0:
            dve.wait_ge(loaded, 16)
        if tile >= 1:
            dve.wait_ge(order, 2 * tile)
        k.nc.vector.tensor_tensor(product[:, 0:512], bank, cut(gates, tile * 512, 512), ALU.mult).then_inc(order, 1)
        dve.wait_ge(order, 2 * tile + 1)
        h = cut(k.h, tile * 512, 512)
        k.nc.vector.tensor_tensor(h, product[:, 0:512], h, ALU.add).then_inc(order, 1)
        return dve.drain()

    normed = norm(k, name + "_norm", f"ple{layer}", k.work)
    scalar_norm = normed.scalar
    normed.scalar = lambda act: (load(act), scalar_norm(act))
    gated = projection(k, name + "_gate", D_TILES, D_TILES, tile_of(k.hn), gate, meet=True)
    mixed = projection(k, name + "_mix", D_TILES, PLE_TILES, tile_of(embedding), add, engine="vector", meet=True)
    mixed_tensor = mixed.tensor
    mixed.tensor = lambda pe: (pe.wait_ge(loaded, 16), mixed_tensor(pe))
    return [normed, gated, mixed]


def turn(k, name, source, width, tiles, finish, engine="scalar"):
    filled, free = k.sem(name + "_turned"), k.sem(name + "_turn_free")

    def tensor(pe):
        for n, tile in enumerate(tiles):
            if n >= 4:
                pe.wait_ge(free, n - 3)
            for b in range(BLOCKS):
                mm = k.nc.tensor.transpose(k.banks[:, n % 4, b * P:(b + 1) * P],
                                           source[:, b * width + tile * P:b * width + (tile + 1) * P],
                                           k.const("ident"))
            mm.then_inc(filled, 1)

    def reader(eng):
        for n in range(len(tiles)):
            eng.wait_ge(filled, n + 1)
            finish(eng, k.banks[:, n % 4, :], n).then_inc(free, 1)

    return Stage(tensor=tensor, **{engine: reader})


def feature_copy(k, memory):
    return lambda act, bank, n: k.nc.scalar.activation(cut(memory, n * 512, 512), bank, ACT.Copy)


def stick_breaking(k, queries, keys, values, value_width, out, out_width, arena):
    at = [0, 512, 896, 1152]
    size = [TOKENS - P * j for j in range(BLOCKS)]
    q_head, k_head = arena.take(512), arena.take(512)
    softplus_part = [arena.take(1280) for _ in range(2)]
    softplus = [arena.take(1280) for _ in range(2)]
    weights = [arena.take(1280) for _ in range(2)]
    (staged, scored, absolute, exped, logged, summed, raw_sum, exponent_ready, weights_done, attended, emptied) = (
        (k.sem_from_one if s in ("scored", "emptied") else k.sem)("stick_" + s) for s in ("staged", "scored", "absolute", "exp_neg", "log1p", "softplus", "softplus_raw",
                                      "exponent", "weights", "attended", "emptied"))
    pairs = SB_HEADS // 2
    order = [3, 2, 1, 0]

    def gpsimd(pool):
        with pool.Fori(0, pairs) as i:
            pool.wait_ge(scored, after(i * 8))
            k.nc.gpsimd.tensor_copy(q_head, cut(queries, i * 512, 512)).then_inc(staged, 1)
            k.nc.gpsimd.tensor_copy(k_head, cut(keys, i * 512, 512)).then_inc(staged, 1)

    def tensor(pe):
        with pe.Fori(0, pairs) as i:
            pe.wait_ge(staged, i * 2 + 2)
            for f in range(2):
                pe.wait_ge(emptied, after(i * 2))
                rows = slice(64 * f, 64 * f + 64)
                for j in order:
                    k.nc.tensor.matmul(k.banks[:, 4 * f + j, 0:size[j]], k_head[rows, j * P:(j + 1) * P],
                                       q_head[rows, j * P:TOKENS], start=True, stop=True,
                                       skip_group_check=True).then_inc(scored, 1)
            for f in range(2):
                for n, j in enumerate(order):
                    pe.wait_ge(summed, i * 8 + (4 * f + n + 1))
                    bank = k.banks[:, 4 * f + j, :]
                    own = softplus[f][:, at[j]:at[j] + size[j]]
                    k.nc.tensor.matmul(bank[:, 0:size[j]], k.const("neg_tri"), own, start=False, stop=False,
                                       skip_group_check=True)
                    for later in range(j + 1, BLOCKS):
                        k.nc.tensor.matmul(bank[:, (later - j) * P:size[j]], k.const("neg_ones"),
                                           softplus[f][:, at[later]:at[later] + size[later]], start=False,
                                           stop=False, skip_group_check=True)
                    k.nc.tensor.matmul(bank[:, 0:P], k.const("ident"), k.const("neg_mask"), start=False,
                                       stop=True, skip_group_check=True).then_inc(exponent_ready, 1)
            for f in range(2):
                pe.wait_ge(weights_done, i * 8 + (4 * f + 4))
                for n in range(BLOCKS):
                    for j in range(n + 1):
                        w = weights[f][:, at[j] + (n - j) * P:at[j] + (n - j + 1) * P]
                        mm = k.nc.tensor.matmul(k.banks[:, 4 * f + 3, n * 64:(n + 1) * 64], w,
                                                cut(values, j * value_width + i * 128 + f * 64, 64),
                                                start=j == 0, stop=j == n, skip_group_check=True)
                mm.then_inc(attended, 1)

    def vector(dve):
        with dve.Fori(0, pairs) as i:
            for f in range(2):
                for n, j in enumerate(order):
                    dve.wait_ge(logged, i * 8 + (4 * f + n + 1))
                    own = softplus[f][:, at[j]:at[j] + size[j]]
                    k.nc.vector.scalar_tensor_tensor(
                        out=own, in0=k.banks[:, 4 * f + j, 0:size[j]], scalar=0.0,
                        in1=softplus_part[f][:, at[j]:at[j] + size[j]], op0=ALU.max, op1=ALU.add).then_inc(raw_sum, 1)
                    dve.wait_ge(raw_sum, i * 8 + (4 * f + n + 1))
                    k.nc.vector.tensor_tensor(own[:, 0:P], own[:, 0:P], k.const("strict"), ALU.mult).then_inc(summed, 1)

    def scalar(act):
        with act.Fori(0, pairs) as i:
            for f in range(2):
                for n, j in enumerate(order):
                    part = softplus_part[f][:, at[j]:at[j] + size[j]]
                    act.wait_ge(scored, after(i * 8 + (4 * f + n + 1)))
                    k.nc.scalar.activation(part, k.banks[:, 4 * f + j, 0:size[j]], ACT.Abs).then_inc(absolute, 1)
                    act.wait_ge(absolute, i * 8 + (4 * f + n + 1))
                    k.nc.scalar.activation(part, part, ACT.Exp, scale=-1.0).then_inc(exped, 1)
                    act.wait_ge(exped, i * 8 + (4 * f + n + 1))
                    k.nc.scalar.activation(part, part, ACT.Ln, bias=1.0).then_inc(logged, 1)
            for f in range(2):
                for n, j in enumerate(order):
                    act.wait_ge(exponent_ready, i * 8 + (4 * f + n + 1))
                    k.nc.scalar.activation(weights[f][:, at[j]:at[j] + size[j]], k.banks[:, 4 * f + j, 0:size[j]],
                                           ACT.Exp).then_inc(weights_done, 1)
            for f in range(2):
                act.wait_ge(attended, i * 2 + (f + 1))
                k.nc.scalar.activation(out.rearrange("p (b n) -> p b n", b=BLOCKS)[:, :, bass.ds(i * 128 + f * 64, 64)],
                                       k.banks[:, 4 * f + 3, 0:256].rearrange("p (b n) -> p b n", b=BLOCKS),
                                       ACT.Copy).then_inc(emptied, 1)

    return Stage(tensor, vector, scalar, gpsimd)


def hgrn_gates(k, q, f, g, keep, decay, small):
    zero, e, inverse, share, lb, rest = (small[:, 4 * n:4 * n + 4] for n in range(6))
    activated, order, floors = k.sem("hgrn_activated"), k.sem("hgrn_gates_order"), k.sem("hgrn_lower_bound")
    logits = k.column("lb")

    def scalar(act):
        act.wait_ge(floors, 1)
        k.nc.scalar.activation(e, zero, ACT.Exp).then_inc(activated, 1)
        k.nc.scalar.activation(keep, f, ACT.Sigmoid, scale=-1.0).then_inc(activated, 1)
        act.wait_ge(activated, 2)
        k.nc.scalar.activation(f, f, ACT.Sigmoid).then_inc(activated, 1)
        k.nc.scalar.activation(q, q, ACT.Silu)
        k.nc.scalar.activation(g, g, ACT.Silu)
        act.wait_ge(order, 2 * HG_HEADS)
        k.nc.scalar.activation(f, f, ACT.Ln).then_inc(activated, 1)

    def vector(dve):
        v = k.nc.vector
        v.tensor_tensor(zero, logits, logits, ALU.subtract).then_inc(floors, 1)
        dve.wait_ge(activated, 1)
        v.reciprocal(inverse, e).then_inc(floors, 1)
        dve.wait_ge(floors, 2)
        v.tensor_tensor(share, e, inverse, ALU.mult).then_inc(floors, 1)
        dve.wait_ge(floors, 3)
        v.tensor_tensor(lb, share, share, ALU.subtract).then_inc(floors, 1)
        dve.wait_ge(floors, 4)
        v.tensor_scalar(rest, lb, -1.0, 1.0, ALU.mult, ALU.add).then_inc(floors, 1)
        dve.wait_ge(floors, 5)
        dve.wait_ge(activated, 3)
        for n in range(HG_HEADS):
            t = slice(n * 512, (n + 1) * 512)
            v.tensor_scalar(f[:, t], f[:, t], rest[:, n:n + 1], lb[:, n:n + 1], ALU.mult, ALU.add).then_inc(order, 1)
            v.tensor_scalar(keep[:, t], keep[:, t], rest[:, n:n + 1], None, ALU.mult).then_inc(order, 1)
        dve.wait_ge(activated, 4)
        for n in range(HG_HEADS):
            t = slice(n * 512, (n + 1) * 512)
            v.tensor_tensor_scan(decay[:, t], k.const("restart"), f[:, t], 0.0, ALU.mult, ALU.add)

    return Stage(vector=vector, scalar=scalar)


def hgrn_heads(k, q, keep, decay, values, value_width, value_at, out, out_width, out_at, arena):
    halves = [64, 32, 16, 8, 4, 2, 1]
    n_levels = len(halves)
    difference = [arena.take(512) for _ in range(2)]
    q_part = [arena.take(512) for _ in range(2)]
    k_part = [arena.take(512) for _ in range(2)]
    from_start, q_decayed, to_end, k_decayed, k_turned, scores = (arena.take(512) for _ in range(6))
    state = arena.take(P)
    (cleared, subtracted, exped, q_ready, k_ready, copied, scored, merged, turned, turned_copied, updated,
     state_ready, attended, emptied, end_order, q_dec, k_dec) = (
         (k.sem_from_one if s in ("attended", "scored", "merged", "emptied") else k.sem)("hgrn_" + s) for s in (
         "cleared", "subtracted", "exped", "q_ready", "k_ready", "diagonal_copied", "scored", "merged", "turned",
         "turned_copied", "updated", "state_ready", "attended", "emptied", "scores_cleared", "q_decayed", "k_decayed"))

    def split(ap, m):
        v = ap.rearrange("p (n m) -> p n m", m=2 * m)
        return v[:, :, 0:m], v[:, :, m:2 * m]

    def per_chunk(ap):
        return ap.rearrange("p (c t) -> p c t", c=BLOCKS)

    def vector(dve):
        v = k.nc.vector
        for n, buffer in enumerate(q_part + k_part):
            v.memset(buffer, 0.0).then_inc(cleared, 1)
        dve.wait_ge(cleared, 4)
        dve.sem_inc(merged, 1)
        with dve.Fori(0, HG_HEADS) as i:
            b, qh = cut(decay, i * 512, 512), cut(q, i * 512, 512)
            dve.wait_ge(attended, after(i * 4))
            v.memset(scores, 0.0).then_inc(end_order, 1)
            dve.wait_ge(end_order, i + 1)

            def subtract(level):
                if level == 8:
                    v.tensor_tensor(per_chunk(difference[0]), per_chunk(b)[:, :, P - 1:P].broadcast_to([P, BLOCKS, P]),
                                    per_chunk(b), ALU.subtract).then_inc(subtracted, 1)
                    return
                m = halves[level]
                first, second = split(b, m)
                ref = first[:, :, m - 1:m].broadcast_to([P, TOKENS // (2 * m), m])
                d_first, d_second = split(difference[level % 2], m)
                v.tensor_tensor(d_first, ref, first, ALU.subtract)
                v.tensor_tensor(d_second, second, ref, ALU.subtract).then_inc(subtracted, 1)

            def multiply(level):
                dve.wait_ge(exped, i * 9 + (level + 1))
                dve.wait_ge(scored, after(i * 8 + (level - 1) if level else i * 8))
                m = halves[level]
                v.tensor_tensor(split(q_part[level % 2], m)[1], split(qh, m)[1],
                                split(difference[level % 2], m)[1], ALU.mult).then_inc(q_ready, 1)

            def merge(level):
                dve.wait_ge(scored, after(i * 8 + (level + 1)))
                dve.wait_ge(merged, after(i * 8 + (level + 1)))
                k.hold(dve)
                mask = k.const("level_masks")[:, level * P:(level + 1) * P].bitcast(I32)
                v.copy_predicated(per_chunk(scores), mask.unsqueeze(1).broadcast_to([P, BLOCKS, P]),
                                  per_chunk(k.banks[:, level % 2, :])).then_inc(merged, 1)

            subtract(0)
            subtract(1)
            for level in range(n_levels):
                multiply(level)
                if level + 2 < n_levels:
                    dve.wait_ge(q_ready, i * 7 + (level + 1))
                    dve.wait_ge(k_ready, i * 7 + (level + 1))
                    subtract(level + 2)
                elif level == n_levels - 2:
                    pass
                if level >= 1:
                    merge(level - 1)
            dve.wait_ge(q_ready, i * 7 + 7)
            dve.wait_ge(k_ready, i * 7 + 7)
            subtract(8)
            dve.wait_ge(exped, i * 9 + 9)
            v.tensor_tensor(q_decayed, qh, from_start, ALU.mult).then_inc(q_dec, 1)
            merge(n_levels - 1)
            merge(n_levels)
            for c in range(BLOCKS - 1):
                dve.wait_ge(updated, i * 3 + (c + 1))
                if c == 0:
                    v.tensor_copy(state, k.banks[:, 4, 0:P]).then_inc(state_ready, 1)
                else:
                    dve.wait_ge(state_ready, i * 3 + c)
                    dve.wait_ge(attended, after(i * 4 + (c + 1)))
                    v.scalar_tensor_tensor(out=state, in0=state, scalar=from_start[:, c * P + P - 1:c * P + P],
                                           in1=k.banks[:, 4 + c % 2, 0:P], op0=ALU.mult,
                                           op1=ALU.add).then_inc(state_ready, 1)

    def gpsimd(pool):
        pool.wait_ge(cleared, 4)
        with pool.Fori(0, HG_HEADS) as i:
            kh = cut(keep, i * 512, 512)
            for level in range(n_levels):
                pool.wait_ge(exped, i * 9 + (level + 1))
                pool.wait_ge(scored, after(i * 8 + (level - 1) if level else i * 8))
                k.hold(pool)
                m = halves[level]
                k.nc.gpsimd.tensor_tensor(split(k_part[level % 2], m)[0], split(kh, m)[0],
                                          split(difference[level % 2], m)[0], ALU.mult).then_inc(k_ready, 1)
            pool.wait_ge(exped, i * 9 + 8)
            k.hold(pool)
            k.nc.gpsimd.tensor_tensor(k_decayed, kh, to_end, ALU.mult).then_inc(k_dec, 1)

    def scalar(act):
        s = k.nc.scalar
        with act.Fori(0, HG_HEADS) as i:
            for level in range(n_levels):
                act.wait_ge(subtracted, i * 8 + (level + 1))
                s.activation(difference[level % 2], difference[level % 2], ACT.Exp).then_inc(exped, 1)
            act.wait_ge(scored, after(i * 8 + 6))
            s.activation(q_part[1], cut(q, i * 512, 512), ACT.Copy).then_inc(copied, 1)
            s.activation(k_part[1], cut(keep, i * 512, 512), ACT.Copy).then_inc(copied, 1)
            act.wait_ge(subtracted, i * 8 + 8)
            act.wait_ge(attended, after(i * 4))
            s.activation(to_end, difference[0], ACT.Exp).then_inc(exped, 1)
            s.activation(from_start, cut(decay, i * 512, 512), ACT.Exp).then_inc(exped, 1)
            act.wait_ge(turned, i + 1)
            s.activation(k_turned, k.banks[:, 2, :], ACT.Copy).then_inc(turned_copied, 1)
            act.wait_ge(attended, after(i * 4 + 4))
            s.activation(per_chunk_out(i), per_chunk(k.banks[:, 3, :]), ACT.Copy).then_inc(emptied, 1)

    def per_chunk_out(i):
        return out.rearrange("p (b n) -> p b n", b=BLOCKS)[:, :, bass.ds(i * P + out_at, P)]

    def tensor(pe):
        mm = k.nc.tensor.matmul
        with pe.Fori(0, HG_HEADS) as i:
            for level in range(n_levels + 1):
                if level < n_levels:
                    pe.wait_ge(q_ready, i * 7 + (level + 1))
                    pe.wait_ge(k_ready, i * 7 + (level + 1))
                else:
                    pe.wait_ge(copied, i * 2 + 2)
                pe.wait_ge(merged, after(i * 8 + level))
                for c in range(BLOCKS):
                    t = slice(c * P, (c + 1) * P)
                    last = mm(k.banks[:, level % 2, t], k_part[level % 2][:, t], q_part[level % 2][:, t],
                              start=True, stop=True)
                last.then_inc(scored, 1)
            pe.wait_ge(k_dec, i + 1)
            for c in range(BLOCKS):
                t = slice(c * P, (c + 1) * P)
                last = k.nc.tensor.transpose(k.banks[:, 2, t], k_decayed[:, t], k.const("ident"))
            last.then_inc(turned, 1)
            pe.wait_ge(merged, after(i * 8 + 9))
            pe.wait_ge(q_dec, i + 1)
            pe.wait_ge(turned_copied, i + 1)
            pe.wait_ge(emptied, after(i))
            for c in range(BLOCKS):
                t = slice(c * P, (c + 1) * P)
                value = cut(values, i * P + (c * value_width + value_at), P)
                if c < BLOCKS - 1:
                    mm(k.banks[:, 4 + c % 2, 0:P], k_turned[:, t], value, start=True, stop=True).then_inc(updated, 1)
                last = mm(k.banks[:, 3, t], scores[:, t], value, start=True, stop=c == 0)
                if c:
                    pe.wait_ge(state_ready, i * 3 + c)
                    last = mm(k.banks[:, 3, t], q_decayed[:, t], state, start=False, stop=True)
                last.then_inc(attended, 1)

    return Stage(tensor, vector, scalar, gpsimd)


def token_norm(k, name, values, count, width, temp, small, scale):
    order, rooted = k.sem(name + "_order"), k.sem(name + "_rooted")
    v3 = values.rearrange("p (c n) -> p c n", n=width)
    sums, deviation, rstd = (small[:, n * count:(n + 1) * count] for n in range(3))

    def scalar(act):
        k.nc.scalar.activation(temp, values, ACT.Square).then_inc(rooted, 1)
        act.wait_ge(order, 1)
        k.nc.scalar.activation(deviation, sums, ACT.Sqrt, bias=k.const("eps"), scale=1.0 / width).then_inc(rooted, 1)

    def vector(dve):
        v = k.nc.vector
        dve.wait_ge(rooted, 1)
        v.tensor_reduce(sums, temp.rearrange("p (c n) -> p c n", n=width), AX.X, ALU.add).then_inc(order, 1)
        dve.wait_ge(rooted, 2)
        v.reciprocal(rstd, deviation).then_inc(order, 1)
        dve.wait_ge(order, 2)
        v.scalar_tensor_tensor(out=v3, in0=v3, scalar=scale, in1=rstd.unsqueeze(2).broadcast_to([P, count, width]),
                               op0=ALU.mult, op1=ALU.mult)

    return Stage(vector=vector, scalar=scalar)


def mixer_ab(k):
    arena = Arena(k.work)
    heads = arena.take(20 * 512)
    values = arena.take(BLOCKS * 1024)
    out = arena.take(BLOCKS * 1024)
    qa, ka, qb, fb, gb = (heads[:, n * 2048:(n + 1) * 2048] for n in range(5))
    source = tile_of(k.hn)

    def evacuate(act, bank, tile):
        return k.nc.scalar.activation(cut(heads, tile * TOKENS, TOKENS), bank, ACT.Copy)

    def scale_queries(act):
        k.nc.scalar.activation(qa, qa, ACT.Copy, scale=SB_DIM ** -0.5)

    stages = [projection(k, "ab_heads", 20, D_TILES, source, evacuate),
              token_projection(k, "ab_values", 4, source, values, 1024, meet=True),
              Stage(scalar=scale_queries),
              stick_breaking(k, qa, ka, values, 1024, out, 1024, Arena(k.work, arena.at))]
    keep, decay = heads[:, 0:2048], heads[:, 2048:4096]
    inner = Arena(k.work, arena.at)
    small = inner.take(64)
    stages += [hgrn_gates(k, qb, fb, gb, keep, decay, small),
               hgrn_heads(k, qb, keep, decay, values, 1024, 512, out, 1024, 512, inner)]
    gathered = heads[:, 0:2048]
    after = Arena(k.work, arena.at)
    squares, small2 = after.take(2048), after.take(64)

    def gather(act):
        k.nc.scalar.activation(gathered.rearrange("p (b n) -> p b n", b=BLOCKS),
                               out.rearrange("p (b n) -> p b n", b=BLOCKS)[:, :, 512:1024], ACT.Copy)

    mixed = Arena(k.work, after.at).take(8 * 512)
    gain = k.column("hg_norm", 0)

    def gated(dve, bank, n):
        return k.nc.vector.scalar_tensor_tensor(out=cut(mixed, (4 + n) * 512, 512), in0=bank, scalar=gain,
                                                in1=cut(gb, n * 512, 512), op0=ALU.mult, op1=ALU.mult)

    stages += [Stage(scalar=gather), token_norm(k, "hg_norm", gathered, 16, P, squares, small2, 1.0),
               turn(k, "stick_out", out, 1024, range(4), feature_copy(k, mixed)),
               turn(k, "hgrn_out", gathered, 512, range(4), gated, engine="vector"),
               projection(k, "ab_out", D_TILES, D_TILES, tile_of(mixed), add_to_residual(k), engine="vector",
                          meet=True)]
    return stages


def softmax_attention(k, name, repeats, units, load, value_of, value_cols, out, out_of, bias_of, scale,
                      span, arena, prepare=None, sink_of=None, minus=None):
    count = len(units)
    per = 2 if minus is not None else 1
    outs = count // per
    logits = [arena.take(span) for _ in range(3)]
    probs = [arena.take(span) for _ in range(3)]
    combined = [arena.take(span) for _ in range(2)] if per == 2 else None
    turned = [arena.take(span) for _ in range(2)]
    small = arena.take(8 * 3)
    largest, shift, total, sink_exp, sum_all, inverse, signed = (small[:, 3 * n:3 * n + 3] for n in range(7))
    (staged, scored, ready, maxed, shifted, exped, normed, joined, turned_done, copied, attended, emptied, order,
     prepared) = (
         (k.sem if s in ("staged", "maxed", "shift_ready", "inverse_ready", "order", "prepared")
          else k.sem_from_one)(f"{name}_{s}") for s in (
         "staged", "scored", "logits_ready", "maxed", "shift_ready", "exped", "inverse_ready", "joined", "turned",
         "turned_copied", "attended", "emptied", "order", "prepared"))
    loads = load(None, None)
    exps = 2 if sink_of else 1

    def gpsimd(pool):
        with pool.Fori(0, repeats) as i:
            pool.wait_ge(scored, after(i * count))
            for instruction in load(pool, i):
                instruction.then_inc(staged, 1)

    def tensor(pe):
        with pe.Fori(0, repeats) as i:
            pe.wait_ge(staged, i * loads + loads)

            def score(u):
                pe.wait_ge(ready, after(i * count + (u - 2) if u >= 3 else i * count))
                query, key, first, blocks = units[u]
                k.nc.tensor.matmul(k.banks[:, u % 3, 0:blocks * P], query, key, start=True,
                                   stop=True).then_inc(scored, 1)

            def turn_probs(v):
                u = v * per + per - 1
                _, _, first, blocks = units[u]
                if per == 2:
                    pe.wait_ge(joined, after(i * outs + (v + 1)))
                    source = combined[v % 2]
                else:
                    pe.wait_ge(exped, after(i * count * exps + (u * exps + exps)))
                    source = probs[u % 3]
                pe.wait_ge(copied, after(i * outs + (v - 1) if v >= 2 else i * outs))
                for b in range(blocks):
                    mm = k.nc.tensor.transpose(k.banks[:, 3 + v % 2, b * P:(b + 1) * P], source[:, b * P:(b + 1) * P],
                                               k.const("ident"))
                mm.then_inc(turned_done, 1)

            def apply(v):
                u = v * per + per - 1
                _, _, first, blocks = units[u]
                pe.wait_ge(copied, after(i * outs + (v + 1)))
                pe.wait_ge(emptied, after(i * outs + (v - 1) if v >= 2 else i * outs))
                for b in range(blocks):
                    mm = k.nc.tensor.matmul(k.banks[:, 5 + v % 2, 0:value_cols], turned[v % 2][:, b * P:(b + 1) * P],
                                            value_of(i, u, first + b), start=b == 0, stop=b == blocks - 1)
                mm.then_inc(attended, 1)

            lead = 2
            for step in range(0, count + 2 * per + lead + 1):
                if step < count:
                    score(step)
                behind = step - lead
                if behind >= 0 and behind % per == per - 1 and behind // per < outs:
                    turn_probs(behind // per)
                behind = step - lead - per
                if behind >= 0 and behind % per == per - 1 and behind // per < outs:
                    apply(behind // per)

    def vector(dve):
        v_ = k.nc.vector
        with dve.Fori(0, repeats) as i:
            if prepare:
                dve.wait_ge(prepared, i + 1)

            def logit(u):
                dve.wait_ge(scored, after(i * count + (u + 1)))
                dve.wait_ge(exped, after(i * count * exps + (u - 2) * exps if u >= 3 else i * count * exps))
                _, _, first, blocks = units[u]
                w = blocks * P
                s = u % 3
                v_.scalar_tensor_tensor(out=logits[s][:, 0:w], in0=k.banks[:, s, 0:w], scalar=scale,
                                        in1=bias_of(i, u, w), op0=ALU.mult, op1=ALU.add).then_inc(ready, 1)
                dve.wait_ge(ready, after(i * count + (u + 1)))
                v_.tensor_reduce(largest[:, s:s + 1], logits[s][:, 0:w], AX.X, ALU.max).then_inc(maxed, 1)
                dve.wait_ge(maxed, i * count + (u + 1))
                v_.tensor_scalar(shift[:, s:s + 1], largest[:, s:s + 1], sink_of(i, u) if sink_of else NEG, -1.0,
                                 ALU.max, ALU.mult).then_inc(shifted, 1)

            per_norm = (1 if sink_of else 0) + 1 + (1 if per == 2 else 0)

            def normalise(u):
                s = u % 3
                dve.wait_ge(exped, after(i * count * exps + (u * exps + exps)))
                base = i * (count * (exps) + (outs if per == 2 else 0))
                done = u * exps + (u // 2 if per == 2 else 0)
                if sink_of:
                    v_.tensor_tensor(sum_all[:, s:s + 1], total[:, s:s + 1], sink_exp[:, s:s + 1],
                                     ALU.add).then_inc(order, 1)
                    dve.wait_ge(order, base + (done + 1))
                    done += 1
                denominator = sum_all if sink_of else total
                v_.reciprocal(inverse[:, s:s + 1], denominator[:, s:s + 1]).then_inc(order, 1)
                done += 1
                dve.wait_ge(order, base + done)
                if per == 1:
                    return
                v = u // 2
                w = units[u][3] * P
                if u % 2 == 0:
                    dve.wait_ge(turned_done, after(i * outs + (v - 1) if v >= 2 else i * outs))
                    v_.tensor_scalar(combined[v % 2][:, 0:w], probs[s][:, 0:w], inverse[:, s:s + 1], None,
                                     ALU.mult).then_inc(normed, 1)
                else:
                    v_.tensor_tensor(signed[:, s:s + 1], inverse[:, s:s + 1], minus, ALU.mult).then_inc(order, 1)
                    dve.wait_ge(order, base + (done + 1))
                    dve.wait_ge(normed, i * outs + (v + 1))
                    v_.scalar_tensor_tensor(out=combined[v % 2][:, 0:w], in0=probs[s][:, 0:w],
                                            scalar=signed[:, s:s + 1], in1=combined[v % 2][:, 0:w], op0=ALU.mult,
                                            op1=ALU.add).then_inc(joined, 1)

            def finish(v):
                u = v * per + per - 1
                dve.wait_ge(attended, after(i * outs + (v + 1)))
                bank = k.banks[:, 5 + v % 2, 0:value_cols]
                if per == 2:
                    v_.tensor_copy(out_of(i, u), bank).then_inc(emptied, 1)
                else:
                    v_.tensor_scalar(out_of(i, u), bank, inverse[:, u % 3:u % 3 + 1], None, ALU.mult).then_inc(emptied, 1)

            for step in range(0, count + 5):
                if per == 1 and 0 <= step - 3 < count:
                    finish(step - 3)
                if step < count:
                    logit(step)
                if per == 2 and step - 6 >= 0 and step % 2 == 0 and (step - 6) // 2 < outs:
                    finish((step - 6) // 2)
                if 0 <= step - 1 < count:
                    normalise(step - 1)
            if per == 2:
                for v in range(max(0, (count + 4 - 6) // 2 + 1), outs):
                    finish(v)

    def scalar(act):
        a = k.nc.scalar
        with act.Fori(0, repeats) as i:
            if prepare:
                act.wait_ge(ready, after(i * count))
                prepare(act, i).then_inc(prepared, 1)

            def exponent(u):
                act.wait_ge(shifted, i * count + (u + 1))
                if per == 2:
                    act.wait_ge(joined, after(i * outs + (u - 3) // 2 + 1 if u >= 3 else i * outs))
                else:
                    act.wait_ge(turned_done, after(i * outs + (u - 2) if u >= 3 else i * outs))
                    act.wait_ge(emptied, after(i * outs + (u - 2) if u >= 3 else i * outs))
                _, _, first, blocks = units[u]
                w = blocks * P
                s = u % 3
                a.activation(probs[s][:, 0:w], logits[s][:, 0:w], ACT.Exp, bias=shift[:, s:s + 1],
                             accum_out=total[:, s:s + 1]).then_inc(exped, 1)
                if sink_of:
                    a.activation(sink_exp[:, s:s + 1], sink_of(i, u), ACT.Exp, bias=shift[:, s:s + 1]).then_inc(exped, 1)

            def copy(v):
                u = v * per + per - 1
                act.wait_ge(turned_done, after(i * outs + (v + 1)))
                act.wait_ge(attended, after(i * outs + (v - 1) if v >= 2 else i * outs))
                w = units[u][3] * P
                a.activation(turned[v % 2][:, 0:w], k.banks[:, 3 + v % 2, 0:w], ACT.Copy).then_inc(copied, 1)

            lead = 2
            for step in range(0, count + 2 * per + lead + 1):
                if step < count:
                    exponent(step)
                behind = step - lead
                if behind >= 0 and behind % per == per - 1 and behind // per < outs:
                    copy(behind // per)

    return Stage(tensor, vector, scalar, gpsimd)


def window_bias_table(k):
    arena = Arena(k.work)
    spread = arena.take(SW_HEADS * P)
    pitch = CONST_WIDTHS["bucket_rows"]
    row = [arena.take(pitch) for _ in range(2)]
    spread_done, made, copied, written = (k.sem("window_bias_" + s) for s in ("spread", "made", "copied", "written"))

    def vector(dve):
        v = k.nc.vector
        v.tensor_copy(spread[0:BUCKETS + 1, :].rearrange("p (h n) -> p h n", h=SW_HEADS),
                      k.column("rel_bias")[0:BUCKETS + 1, :].unsqueeze(2).broadcast_to([BUCKETS + 1, SW_HEADS, P])
                      ).then_inc(spread_done, 1)
        for h in range(SW_HEADS):
            dve.wait_ge(made, h + 1)
            if h >= 2:
                dve.wait_ge(written, 16 * (h - 1))
            v.tensor_copy(row[h % 2], k.banks[:, h % 2, 0:pitch]).then_inc(copied, 1)

    def tensor(pe):
        pe.wait_ge(spread_done, 1)
        for h in range(SW_HEADS):
            if h >= 2:
                pe.wait_ge(copied, h - 1)
            k.nc.tensor.matmul(k.banks[:, h % 2, 0:pitch], spread[0:BUCKETS + 1, h * P:(h + 1) * P],
                               k.const("bucket_rows")[0:BUCKETS + 1, :], start=True, stop=True).then_inc(made, 1)

    def scalar(act):
        for h in range(SW_HEADS):
            act.wait_ge(copied, h + 1)
            if h >= 1:
                act.wait_ge(written, 16 * h)
            act.dma_start(k.dram["window_rows"][h], row[h % 2]).then_inc(written, 16)
        act.wait_ge(written, 16 * SW_HEADS)

    return [Stage(tensor, vector, scalar)]


def chunk_bias_table(k):
    arena = Arena(k.work)
    table = arena.take(CH_HEADS * (2 * REL_CLIP + 1))
    pitch = TOKENS + P - 1
    rows = arena.take(CH_HEADS * pitch)
    loaded, built, written = (k.sem("chunk_bias_" + s) for s in ("loaded", "built", "written"))
    flat = TOKENS - 1 - REL_CLIP
    table3 = table.rearrange("p (h n) -> p h n", h=CH_HEADS)
    rows3 = rows.rearrange("p (h n) -> p h n", h=CH_HEADS)

    def vector(dve):
        dve.wait_ge(loaded, 16)
        k.nc.vector.tensor_copy(rows3[:, :, 0:flat], table3[:, :, 0:1].broadcast_to([P, CH_HEADS, flat])).then_inc(built, 1)
        k.nc.vector.tensor_copy(rows3[:, :, flat:pitch], table3[:, :, 0:pitch - flat]).then_inc(built, 1)

    def scalar(act):
        act.dma_start(table, k.dram["chunk_table"]).then_inc(loaded, 16)
        act.wait_ge(built, 2)
        act.dma_start(k.dram["chunk_rows"].rearrange("h p u -> p h u"), rows3).then_inc(written, 16)
        act.wait_ge(written, 16)

    return [Stage(vector=vector, scalar=scalar)]


def skewed(dram, heads, pitch, columns):
    flat = dram.rearrange("h p u -> h (p u)")[:, P - 1:P - 1 + P * (pitch - 1)]
    return flat.rearrange("h (p u) -> p h u", u=pitch - 1)[:, :, 0:columns]


def mixer_c(k):
    arena = Arena(k.work)
    heads = arena.take(10 * 512)
    key_pairs = arena.take(SW_KV * 512)
    values = arena.take(BLOCKS * 256)
    out = arena.take(BLOCKS * 1024)
    table = arena.take(SW_HEADS * 256)
    q_heads, k_head = arena.take(2 * 512), arena.take(512)
    squares, total, deviation = arena.take(2 * 512), arena.take(2 * 512), arena.take(2 * 512)
    squared, summed, rooted, inverted, table_in = (k.sem("qk_norm_" + s) for s in
                                                   ("squared", "summed", "rooted", "inverted", "table_in"))

    def norm_tensor(pe):
        for n in range(10):
            pe.wait_ge(squared, n + 1)
            if n >= 2:
                pe.wait_ge(rooted, n - 1)
            k.nc.tensor.matmul(k.banks[:, n % 2, :], k.const("head_pair"), squares[:, n % 2 * 512:n % 2 * 512 + 512],
                               start=True, stop=True).then_inc(summed, 1)

    def norm_vector(dve):
        v = k.nc.vector
        order = norm_order
        for n in range(10):
            s = slice(n % 2 * 512, n % 2 * 512 + 512)
            dve.wait_ge(rooted, n + 1)
            v.reciprocal(total[:, s], deviation[:, s]).then_inc(order, 1)
            dve.wait_ge(order, n + 1)
            tile = cut(heads, n * 512, 512)
            v.scalar_tensor_tensor(out=tile, in0=tile, scalar=k.column("q_norm" if n < 8 else "k_norm"), in1=total[:, s],
                                   op0=ALU.mult, op1=ALU.mult).then_inc(inverted, 1)

    norm_order = k.sem("qk_norm_order")
    paired = k.sem("qk_norm_keys_paired")

    def norm_scalar(act):
        a = k.nc.scalar
        act.dma_start(table.rearrange("p (h n) -> p h n", h=SW_HEADS),
                      skewed(k.dram["window_rows"], SW_HEADS, CONST_WIDTHS["bucket_rows"], 256)).then_inc(table_in, 16)
        for n in range(11):
            if n < 10:
                if n >= 2:
                    act.wait_ge(summed, n - 1)
                a.activation(squares[:, n % 2 * 512:n % 2 * 512 + 512], cut(heads, n * 512, 512),
                             ACT.Square).then_inc(squared, 1)
            if n >= 1:
                m = n - 1
                act.wait_ge(summed, m + 1)
                if m >= 2:
                    act.wait_ge(norm_order, m - 1)
                a.activation(deviation[:, m % 2 * 512:m % 2 * 512 + 512], k.banks[:, m % 2, :], ACT.Sqrt,
                             bias=k.const("eps"), scale=1.0 / 64).then_inc(rooted, 1)
        act.wait_ge(inverted, 10)
        for kv in range(SW_KV):
            rows = slice(64 * (kv % 2), 64 * (kv % 2) + 64)
            for half in range(2):
                a.activation(key_pairs[64 * half:64 * half + 64, kv * 512:(kv + 1) * 512],
                             heads[rows, (8 + kv // 2) * 512:(9 + kv // 2) * 512], ACT.Copy).then_inc(paired, 1)
        act.wait_ge(table_in, 16)

    units, which = [], []
    for tile in range(2):
        for half in range(2):
            for n in range(BLOCKS):
                rows = slice(64 * half, 64 * half + 64)
                first = max(n - 1, 0)
                units.append((q_heads[rows, tile * 512 + n * P:tile * 512 + (n + 1) * P],
                              k_head[rows, first * P:(n + 1) * P], first, n + 1 - first))
                which.append((2 * tile + half, n))

    def load(pool, i):
        if pool is None:
            return 2
        return [k.nc.gpsimd.tensor_copy(q_heads, cut(heads, i * 1024, 1024)),
                k.nc.gpsimd.tensor_copy(k_head, cut(key_pairs, i * 512, 512))]

    def value_of(i, u, block):
        return cut(values, i * 64 + block * 256, 64)

    def out_of(i, u):
        head, n = which[u]
        return cut(out, i * 256 + (n * 1024 + head * 64), 64)

    def bias_of(i, u, w):
        head, n = which[u]
        return cut(table, i * 1024 + (head * 256 + 256 - w), w)

    def sink_of(i, u):
        return k.column("sinks", i * 4 + which[u][0])

    attention = softmax_attention(k, "window", SW_KV, units, load, value_of, 64, out, out_of, bias_of, 64 ** -0.5,
                                  256, Arena(k.work, arena.at - 3072), sink_of=sink_of)
    mixed = heads[:, 0:8 * 512]
    return [projection(k, "c_heads", 10, D_TILES, tile_of(k.hn), copy_into(k, heads)),
            token_projection(k, "c_values", 1, tile_of(k.hn), values, 256, meet=True),
            Stage(norm_tensor, norm_vector, norm_scalar), attention,
            turn(k, "window_out", out, 1024, range(8), feature_copy(k, mixed)),
            projection(k, "c_out", D_TILES, D_TILES, tile_of(mixed), add_to_residual(k), engine="vector", meet=True)]


def branches(k):
    arena = Arena(k.work)
    heads = arena.take(24 * 512)
    values = arena.take(BLOCKS * 1536)
    out_d = arena.take(BLOCKS * 1024)
    q_head, k_head, bias = arena.take(512), arena.take(512), arena.take(512)
    minus = arena.take(8)
    scratch = arena.at
    qd, kd, qc, kc = heads[:, 0:4096], heads[:, 4096:8192], heads[:, 8192:10240], heads[:, 10240:12288]
    stages = [projection(k, "in_heads", 24, D_TILES, tile_of(k.hn), copy_into(k, heads)),
              token_projection(k, "in_values", 6, tile_of(k.hn), values, 1536, meet=True)]

    temp = Arena(k.work, scratch).take(64)
    made, exped = k.sem("lambda_made"), k.sem("lambda_exped")
    lambdas = k.column("lambdas")

    def lambda_vector(dve):
        v = k.nc.vector
        for n in range(2):
            v.tensor_tensor(temp, lambdas[:, 128 * n:128 * n + 64], lambdas[:, 128 * n + 64:128 * n + 128],
                            ALU.mult).then_inc(made, 1)
            dve.wait_ge(made, 2 * n + 1)
            v.tensor_reduce(minus[:, 1 + n:2 + n], temp, AX.X, ALU.add).then_inc(made, 1)
            dve.wait_ge(made, 2 * n + 2)
        dve.wait_ge(exped, 1)
        v.tensor_tensor(minus[:, 5:6], minus[:, 4:5], minus[:, 3:4], ALU.subtract).then_inc(made, 1)
        dve.wait_ge(made, 5)
        v.tensor_scalar(minus[:, 0:1], minus[:, 5:6], -LAM_INIT, None, ALU.add)

    def lambda_scalar(act):
        act.wait_ge(made, 4)
        k.nc.scalar.activation(minus[:, 3:5], minus[:, 1:3], ACT.Exp).then_inc(exped, 1)

    stages.append(Stage(vector=lambda_vector, scalar=lambda_scalar))

    units = []
    for n in range(BLOCKS):
        for half in range(2):
            rows = slice(64 * half, 64 * half + 64)
            units.append((q_head[rows, n * P:(n + 1) * P], k_head[rows, 0:(n + 1) * P], 0, n + 1))

    def load_d(pool, i):
        if pool is None:
            return 2
        return [k.nc.gpsimd.tensor_copy(q_head, cut(qd, i * 512, 512)),
                k.nc.gpsimd.tensor_copy(k_head, cut(kd, i * 512, 512))]

    def slope(act, i):
        return k.nc.scalar.activation(bias, k.const("distance"), ACT.Copy, scale=cut(k.const("slopes"), i, 1))

    stages.append(softmax_attention(
        k, "diff", DIFF_HEADS, units, load_d, lambda i, u, b: cut(values, i * P + b * 1536, P), P, out_d,
        lambda i, u: cut(out_d, i * P + (u // 2) * 1024, P), lambda i, u, w: bias[:, 512 - w:512], 64 ** -0.5,
        512, Arena(k.work, scratch), prepare=slope, minus=minus[:, 0:1]))

    squares = kd
    small = Arena(k.work, scratch).take(96)
    mixed_d = heads[:, 0:4096]

    def gained(act, bank, n):
        return k.nc.scalar.activation(cut(mixed_d, n * 512, 512), bank, ACT.Copy, scale=k.column("subln", 0))

    stages += [token_norm(k, "diff_norm", out_d, 32, P, squares, small, 1.0 - LAM_INIT),
               turn(k, "diff_out", out_d, 1024, range(8), gained)]

    table = kd
    out_c = out_d[:, 0:BLOCKS * 512]
    table_in, masked = k.sem("chunk_table_in"), k.sem("chunk_table_masked")

    def table_scalar(act):
        act.dma_start(table.rearrange("p (h n) -> p h n", h=CH_HEADS),
                      skewed(k.dram["chunk_rows"], CH_HEADS, TOKENS + P - 1, TOKENS)).then_inc(table_in, 16)

    def table_vector(dve):
        dve.wait_ge(table_in, 16)
        k.nc.vector.memset(table.rearrange("p (h n) -> p h n", h=CH_HEADS)[0:64, :, 448:512], NEG)

    stages.append(Stage(vector=table_vector, scalar=table_scalar))
    units_c, which = [], []
    for half in range(2):
        for n in range(BLOCKS):
            rows = slice(64 * half, 64 * half + 64)
            units_c.append((q_head[rows, n * P:(n + 1) * P], k_head[rows, 0:(n + 1) * P], 0, n + 1))
            which.append((half, n))

    def load_c(pool, i):
        if pool is None:
            return 2
        return [k.nc.gpsimd.tensor_copy(q_head, cut(qc, i * 512, 512)),
                k.nc.gpsimd.tensor_copy(k_head, cut(kc, i * 512, 512))]

    stages.append(softmax_attention(
        k, "chunk", CH_HEADS // 2, units_c, load_c,
        lambda i, u, b: cut(values, i * P + (b * 1536 + 1024 + which[u][0] * 64), 64), 64, out_c,
        lambda i, u: cut(out_c, i * P + (which[u][1] * 512 + which[u][0] * 64), 64),
        lambda i, u, w: cut(table, i * 1024 + (which[u][0] * 512 + 512 - w), w), 64 ** -0.5,
        512, Arena(k.work, scratch)))
    mixed_c = heads[:, 8192:10240]
    stages.append(turn(k, "chunk_out", out_c, 512, range(4), feature_copy(k, mixed_c)))

    after = Arena(k.work, 24 * 512)
    gates, merged, product = after.take(4096), after.take(4096), after.take(512)

    def gate(offset):
        return lambda act, bank, tile: k.nc.scalar.activation(cut(gates, tile * 512, 512), bank, ACT.Sigmoid,
                                                              bias=k.column("b_gate", tile + offset))

    def first(dve, bank, tile):
        return k.nc.vector.tensor_tensor(cut(merged, tile * 512, 512), bank, cut(gates, tile * 512, 512), ALU.mult)

    order = k.sem("merge_order")

    def second(dve, bank, tile):
        if tile:
            dve.wait_ge(order, 2 * tile)
        k.nc.vector.tensor_tensor(product, bank, cut(gates, tile * 512, 512), ALU.mult).then_inc(order, 1)
        dve.wait_ge(order, 2 * tile + 1)
        m = cut(merged, tile * 512, 512)
        k.nc.vector.tensor_tensor(m, product, m, ALU.add).then_inc(order, 1)
        return dve.drain()

    stages += [projection(k, "gate_d", 8, 8, tile_of(k.hn), gate(0), meet=True),
               projection(k, "branch_d", 8, 8, tile_of(mixed_d), first, engine="vector", meet=True),
               projection(k, "gate_c", 8, 8, tile_of(k.hn), gate(8), meet=True),
               projection(k, "branch_c", 8, 4, tile_of(mixed_c), second, engine="vector", meet=True),
               projection(k, "out", 8, 8, tile_of(merged), add_to_residual(k), engine="vector", meet=True)]
    return stages


def routing(k, queries, key_table, turned):
    arena = Arena(k.work, 8192 + 1024 + 3 * 512)
    lists = 2 * PEER_HEADS
    q_block = arena.take(D_TILES * P)
    scores = [arena.take(lists * P), arena.take(lists * P)]
    best = arena.take(lists * TOPK)
    index, index_f = arena.take(lists * TOPK), arena.take(lists * TOPK)
    sums = [arena.take(PEER_HEADS * TOPK * TOPK) for _ in range(2)]
    picked = arena.take(PEER_HEADS * TOPK)
    pick, row_col, row_col_f = arena.take(P), arena.take(2 * P), arena.take(2 * P)
    match, product = arena.take(2048), arena.take(2048)
    chosen = arena.take(3 * P)
    shifted, exped_s, total, inverse = arena.take(P), arena.take(P), arena.take(8), arena.take(8)
    (loaded, staged, scored, copied, order, exp_in, exp_out, ready, turned_up, emptied) = (
        (k.sem_from_one if s in ("scored", "chosen", "copied", "emptied", "turned") else k.sem)("route_" + s) for s in (
        "keys_in", "staged", "scored", "copied", "order", "to_exp", "exped", "chosen", "turned", "emptied"))
    best4 = best.rearrange("p (s h r) -> p h s r", h=PEER_HEADS, s=2)
    index4 = index_f.rearrange("p (s h r) -> p h s r", h=PEER_HEADS, s=2)
    quad = [P, PEER_HEADS, TOPK, TOPK]

    def scalar(act):
        a = k.nc.scalar
        act.dma_start(key_table, k.dram["peer_keys"]).then_inc(loaded, 16)
        with act.Fori(0, BLOCKS) as b:
            act.wait_ge(scored, after(b))
            a.activation(q_block.rearrange("p (h t) -> p h t", h=D_TILES),
                         queries.rearrange("p (h t) -> p h t", h=D_TILES)[:, :, bass.ds(b * P, P)],
                         ACT.Copy).then_inc(staged, 1)
            act.wait_ge(scored, after(b + 1))
            act.wait_ge(ready, after(b))
            for n in range(4):
                a.activation(scores[0][:, n * 512:(n + 1) * 512], k.banks[:, n, :], ACT.Copy).then_inc(copied, 1)
            act.wait_ge(exp_in, b + 1)
            a.activation(exped_s, shifted, ACT.Exp).then_inc(exp_out, 1)
            act.wait_ge(turned_up, after(b + 1))
            for n in range(3):
                a.activation(cut(turned, b * P + n * 512, P), k.banks[:, 4, n * P:(n + 1) * P],
                             ACT.Copy).then_inc(emptied, 1)

    def tensor(pe):
        pe.wait_ge(loaded, 16)
        with pe.Fori(0, BLOCKS) as b:
            pe.wait_ge(staged, b + 1)
            pe.wait_ge(copied, after(b * 4))
            for h in range(PEER_HEADS):
                for s in range(2):
                    rows = slice(64 * s, 64 * s + 64)
                    mm = k.nc.tensor.matmul(k.banks[:, 2 * s + h // 4, h % 4 * P:(h % 4 + 1) * P],
                                            q_block[rows, h * P:(h + 1) * P], key_table[rows, h * P:(h + 1) * P],
                                            start=True, stop=True)
            mm.then_inc(scored, 1)
            pe.wait_ge(ready, after(b + 1))
            pe.wait_ge(emptied, after(b * 3))
            for n in range(3):
                mm = k.nc.tensor.transpose(k.banks[:, 4, n * P:(n + 1) * P], chosen[:, n * P:(n + 1) * P],
                                           k.const("ident"))
            mm.then_inc(turned_up, 1)

    def vector(dve):
        v = k.nc.vector
        steps = 19

        with dve.Fori(0, BLOCKS) as b:
            done = [0]

            def then(instruction):
                done[0] += 1
                instruction.then_inc(order, 1)
                dve.wait_ge(order, b * steps + done[0])
                k.hold(dve)

            def ranked(count, width, values, spare, top, where):
                def of(memory, n, size):
                    return memory[:, n * size:(n + 1) * size]
                for n in range(count):
                    last = v.max(of(top, n, TOPK)[:, 0:8], of(values, n, width))
                then(last)
                for n in range(count):
                    v.max_index(of(where, n, TOPK)[:, 0:8].bitcast(U32), of(top, n, TOPK)[:, 0:8], of(values, n, width))
                    last = v.match_replace(of(spare, n, width), of(top, n, TOPK)[:, 0:8], of(values, n, width), -3e38)
                then(last)
                for n in range(count):
                    last = v.max(of(top, n, TOPK)[:, 8:16], of(spare, n, width))
                then(last)
                for n in range(count):
                    last = v.max_index(of(where, n, TOPK)[:, 8:16].bitcast(U32), of(top, n, TOPK)[:, 8:16],
                                       of(spare, n, width))
                then(last)

            dve.wait_ge(copied, after(b * 4 + 4))
            k.hold(dve)
            ranked(lists, P, scores[0], scores[1], best, index)
            then(v.tensor_copy(index_f, index.bitcast(U32)))
            then(v.tensor_tensor(sums[0].rearrange("p (h r c) -> p h r c", h=PEER_HEADS, r=TOPK),
                                 best4[:, :, 0, :].unsqueeze(3).broadcast_to(quad),
                                 best4[:, :, 1, :].unsqueeze(2).broadcast_to(quad), ALU.add))
            ranked(PEER_HEADS, TOPK * TOPK, sums[0], sums[1], picked, pick)
            v.tensor_scalar(row_col[:, 0:P].bitcast(U32), pick.bitcast(U32), 4, None, ALU.logical_shift_right)
            then(v.tensor_scalar(row_col[:, P:2 * P].bitcast(U32), pick.bitcast(U32), 15, None, ALU.bitwise_and))
            then(v.tensor_copy(row_col_f, row_col.bitcast(U32)))
            dve.wait_ge(turned_up, after(b))
            for s in range(2):
                rank = row_col_f[:, s * P:(s + 1) * P].rearrange("p (h r) -> p h r", h=PEER_HEADS)
                ranks = k.const("iota")[:, 0:TOPK].unsqueeze(1).unsqueeze(1).broadcast_to(quad)
                m4 = match.rearrange("p (h r c) -> p h r c", h=PEER_HEADS, r=TOPK)
                p4 = product.rearrange("p (h r c) -> p h r c", h=PEER_HEADS, r=TOPK)
                then(v.tensor_tensor(m4, rank.unsqueeze(3).broadcast_to(quad), ranks, ALU.is_equal))
                then(v.tensor_tensor(p4, m4, index4[:, :, s, :].unsqueeze(2).broadcast_to(quad), ALU.mult))
                last = v.tensor_reduce(chosen[:, s * P:(s + 1) * P], product.rearrange("p (n c) -> p n c", c=TOPK),
                                       AX.X, ALU.add)
            then(last)
            picked3 = picked.rearrange("p (h r) -> p h r", h=PEER_HEADS)
            by_head = [P, PEER_HEADS, TOPK]
            v.tensor_tensor(shifted.rearrange("p (h r) -> p h r", h=PEER_HEADS), picked3,
                            picked3[:, :, 0:1].broadcast_to(by_head), ALU.subtract).then_inc(exp_in, 1)
            dve.wait_ge(exp_out, b + 1)
            exps = exped_s.rearrange("p (h r) -> p h r", h=PEER_HEADS)
            then(v.tensor_reduce(total, exps, AX.X, ALU.add))
            then(v.reciprocal(inverse, total))
            v.tensor_tensor(chosen[:, 2 * P:3 * P].rearrange("p (h r) -> p h r", h=PEER_HEADS), exps,
                            inverse.unsqueeze(2).broadcast_to(by_head), ALU.mult).then_inc(ready, 1)
            assert done[0] == steps, done[0]

    return Stage(tensor, vector, scalar)


def routing_matrix(k, turned):
    arena = Arena(k.work, 8192 + 1024 + 3 * 512)
    batch = 4
    rows = [arena.take(batch * P) for _ in range(2)]
    cols = [arena.take(batch * P) for _ in range(2)]
    staging = arena.take(P * CHUNK_TOKENS)
    (rows_ready, cols_ready, made, emptied, stored) = (
        (k.sem_from_one if s in ("made", "stored") else k.sem)("matrix_" + s) for s in (
        "rows", "columns", "made", "emptied", "stored"))
    per_chunk = CHUNK_TOKENS // batch
    choice_i, choice_j, weight = (turned[:, n * 512:(n + 1) * 512] for n in range(3))
    three = [P, batch, P]

    def batches(eng, body):
        with eng.Fori(0, CHUNKS) as chunk:
            with eng.Fori(0, per_chunk // 2) as pair:
                for p in range(2):
                    body(chunk * per_chunk + pair * 2, p)

    def vector(dve):
        dve.sem_inc(made, 1)

        def body(base, p):
            dve.wait_ge(made, after(base + p))
            for t in range(batch):
                at = base * batch + (p * batch + t)
                last = k.nc.vector.tensor_scalar(rows[p][:, t * P:(t + 1) * P], k.const("iota"), cut(choice_i, at, 1),
                                                 cut(weight, at, 1), ALU.is_equal, ALU.mult)
            last.then_inc(rows_ready, 1)
            k.nc.vector.tensor_tensor(cols[p].rearrange("p (t n) -> p t n", t=batch),
                                      k.const("iota").unsqueeze(1).broadcast_to(three),
                                      cut(choice_j, base * batch + p * batch, batch).unsqueeze(2).broadcast_to(three),
                                      ALU.is_equal).then_inc(cols_ready, 1)
        batches(dve, body)

    def tensor(pe):
        def body(base, p):
            pe.wait_ge(rows_ready, base + (p + 1))
            pe.wait_ge(cols_ready, base + (p + 1))
            pe.wait_ge(emptied, base + (p + 1))
            for t in range(batch):
                s = slice(t * P, (t + 1) * P)
                mm = k.nc.tensor.matmul(k.banks[:, p, s], rows[p][:, s], cols[p][:, s], start=True, stop=True)
            mm.then_inc(made, 1)
        batches(pe, body)

    def scalar(act):
        act.sem_inc(emptied, 2)
        by_token = staging.rearrange("p (j t) -> p t j", t=CHUNK_TOKENS)

        with act.Fori(0, CHUNKS) as chunk:
            act.wait_ge(stored, after(chunk * 16))
            with act.Fori(0, per_chunk // 2) as pair:
                for p in range(2):
                    act.wait_ge(made, after(chunk * per_chunk + pair * 2 + (p + 2)))
                    k.nc.scalar.activation(by_token[:, bass.ds(pair * 2 * batch + p * batch, batch), :],
                                           k.banks[:, p, :].rearrange("p (t n) -> p t n", t=batch),
                                           ACT.Copy).then_inc(emptied, 1)
            act.wait_ge(emptied, chunk * per_chunk + (per_chunk + 2))
            act.dma_start(k.dram["routing"][bass.ds(chunk, 1)].rearrange("c p j t -> (c p) (j t)"),
                          staging).then_inc(stored, 16)
        act.wait_ge(stored, after(CHUNKS * 16))

    return Stage(tensor, vector, scalar)


def experts(k):
    arena = Arena(k.work)
    hidden = [arena.take(GROUP * 512) for _ in range(2)]
    gates = [arena.take(GROUP * 512) for _ in range(2)]
    activated = arena.take(2 * 512)
    first = k.take_slots(GROUPS * 8)
    (filled, free, gelu_done, ready, gates_in, out_filled, out_free) = (
        (k.sem_from_one if s in ("ready", "out_filled") else k.sem)("experts_" + s) for s in (
        "filled", "free", "gelu_done", "ready", "gates_in", "out_filled", "out_free"))

    def tensor(pe):
        mm = k.nc.tensor.matmul

        def slot(q, turn_base, body):
            place = (first + q) % RING
            k.slot_begins(pe, place, turn_base + (first + q) // RING)
            body(place)

        def hide(g, p, turn_base):
            for q in range(4):
                def body(place):
                    for n in range(2):
                        pe.wait_ge(free, g * GROUP + (2 * q + n + 1))
                        bank = k.banks[:, (2 * q + n) % 4, :]
                        for kk in range(D_TILES):
                            last = mm(bank, k.tile(place, n * D_TILES + kk), cut(k.hn, kk * 512, 512),
                                      start=kk == 0, stop=kk == D_TILES - 1)
                            if n == 0 and kk == 0:
                                k.release_previous(last, place)
                        last.then_inc(filled, 1)
                slot(q, turn_base, body)

        def give(g, p, turn_base):
            pe.wait_ge(ready, after(g * GROUP + GROUP))
            for q in range(4):
                def body(place):
                    for n in range(2):
                        pe.wait_ge(out_free, g * D_TILES + (2 * q + n + 1))
                        bank = k.banks[:, 4 + (2 * q + n) % 4, :]
                        for e in range(GROUP):
                            last = mm(bank, k.tile(place, n * GROUP + e), hidden[p][:, e * 512:(e + 1) * 512],
                                      start=e == 0, stop=e == GROUP - 1)
                            if n == 0 and e == 0:
                                k.release_previous(last, place)
                        last.then_inc(out_filled, 1)
                slot(q, turn_base, body)

        hide(0, 0, 0)
        with pe.Fori(0, GROUPS // 2 - 1) as r:
            for p in range(2):
                hide(r * 2 + (p + 1), 1 - p, r * 4 + (2 * p + 1))
                give(r * 2 + p, p, r * 4 + (2 * p + 2))
        hide(GROUPS - 1, 1, 2 * GROUPS - 3)
        give(GROUPS - 2, 0, 2 * GROUPS - 2)
        give(GROUPS - 1, 1, 2 * GROUPS - 1)

    def in_groups(eng, hide, give):
        hide(0, 0)
        with eng.Fori(0, GROUPS // 2 - 1) as r:
            for p in range(2):
                hide(r * 2 + (p + 1), 1 - p)
                give(r * 2 + p, p)
        hide(GROUPS - 1, 1)
        give(GROUPS - 2, 0)
        give(GROUPS - 1, 1)

    def scalar(act):
        def load(g, p):
            act.dma_start(gates[p].rearrange("p (c j t) -> p c (j t)", c=CHUNKS, j=GROUP),
                          k.dram["routing"].rearrange("c p j t -> p c (j t)")[
                              :, :, bass.ds(g * (GROUP * CHUNK_TOKENS), GROUP * CHUNK_TOKENS)]).then_inc(gates_in, 16)

        def hide(g, p):
            if not (isinstance(g, int) and g < 2):
                act.wait_ge(ready, after(g * GROUP - GROUP))
            load(g, p)
            for e in range(GROUP):
                act.wait_ge(filled, g * GROUP + (e + 1))
                act.wait_ge(ready, after(g * GROUP + (e - 1) if not (isinstance(g, int) and e < 2 and g == 0) else 0))
                k.nc.scalar.activation(activated[:, e % 2 * 512:e % 2 * 512 + 512], k.banks[:, e % 4, :],
                                       ACT.Gelu).then_inc(gelu_done, 1)
        in_groups(act, hide, lambda g, p: None)

    def vector(dve):
        dve.sem_inc(free, 4)
        dve.sem_inc(out_free, 4)

        def hide(g, p):
            dve.wait_ge(gates_in, g * 16 + 16)
            gate = gates[p].rearrange("p (c j t) -> p c j t", c=CHUNKS, j=GROUP)
            dve.wait_ge(out_filled, after(g * D_TILES - D_TILES if not (isinstance(g, int) and g < 2) else 0))
            for e in range(GROUP):
                dve.wait_ge(gelu_done, g * GROUP + (e + 1))
                dve.sem_inc(free, 1)
                k.nc.vector.tensor_tensor(
                    hidden[p][:, e * 512:(e + 1) * 512].rearrange("p (c t) -> p c t", c=CHUNKS),
                    activated[:, e % 2 * 512:e % 2 * 512 + 512].rearrange("p (c t) -> p c t", c=CHUNKS),
                    gate[:, :, e, :], ALU.mult).then_inc(ready, 1)

        def give(g, p):
            for n in range(D_TILES):
                dve.wait_ge(out_filled, after(g * D_TILES + (n + 1)))
                add_to_residual(k)(dve, k.banks[:, 4 + n % 4, :], n).then_inc(out_free, 1)
        in_groups(dve, hide, give)

    return Stage(tensor, vector, scalar)


def expert_layer(k):
    arena = Arena(k.work)
    queries = arena.take(8 * 512)
    arena.take(4096)
    key_table = arena.take(8 * P)
    turned = arena.take(3 * 512)
    return [projection(k, "peer_queries", 8, 8, tile_of(k.hn), copy_into(k, queries), meet=True),
            routing(k, queries, key_table, turned), routing_matrix(k, turned), experts(k)]


def load_inputs(k):
    def scalar(act):
        act.dma_start(k.consts[:, :], k.dram["consts"]).then_inc(k.inputs_in, 16)
        act.dma_start(k.columns[:, :], k.dram["columns"]).then_inc(k.inputs_in, 16)
        act.dma_start(k.h[:, :], k.dram["x"]).then_inc(k.inputs_in, 16)
        act.wait_ge(k.inputs_in, 48)
    return Stage(scalar=scalar)


def store(k, source):
    stored = k.sem("stored")

    def scalar(act):
        act.dma_start(k.dram["out"], source).then_inc(stored, 16)
        act.wait_ge(stored, 16)
    return Stage(scalar=scalar)


def program(nc, dram, stop=None):
    ctx = ExitStack()
    with ctx:
        k = Core(nc, ctx, dram)
        periods = [
            lambda: [load_inputs(k)], lambda: window_bias_table(k), lambda: chunk_bias_table(k),
            lambda: [norm(k, "mix0_norm", "mix0", k.work)], lambda: mixer_ab(k),
            lambda: [norm(k, "ffn0_norm", "ffn0", k.work)], lambda: feed_forward(k, 0), lambda: layer_embedding(k, 0),
            lambda: [norm(k, "mix1_norm", "mix1", k.work)], lambda: mixer_c(k),
            lambda: [norm(k, "ffn1_norm", "ffn1", k.work)], lambda: feed_forward(k, 1), lambda: layer_embedding(k, 1),
            lambda: [norm(k, "norm1", "norm1", k.work)], lambda: branches(k),
            lambda: [norm(k, "norm2", "norm2", k.work)], lambda: expert_layer(k)]
        if stop is not None:
            periods = periods[:stop] + [lambda: [store(k, k.h[:, :])]]
        else:
            periods += [lambda: [norm(k, "final_norm", "final", k.work), store(k, k.hn[:, :])]]
        stages = k.plan(periods)

        def run(eng, which):
            met = 0
            for stage in stages:
                part = {"tensor": stage.tensor, "vector": stage.vector, "scalar": stage.scalar,
                        "gpsimd": stage.gpsimd}[which]
                if part:
                    part(eng)
                if stage.meet:
                    eng.drain().then_inc(k.meetings, 1)
                    met += 1
                    eng.wait_ge(k.meetings, 4 * met)

        block = ctx.enter_context(nc.Block())

        @block.sync
        def _(sp):
            rounds = k.slots // RING

            def load(place, round_):
                sp.wait_ge(k.weights_used[place], round_ + 1)
                slot = round_ * RING + place
                sp.dma_start(k.ring[:, place * SLOT:(place + 1) * SLOT],
                             dram["weights"][bass.ds(slot, 1)].rearrange("s p n -> (s p) n")
                             ).then_inc(k.weights_in[place], 16)
            if rounds:
                with sp.Fori(0, rounds) as r:
                    for place in range(RING):
                        load(place, r)
            for place in range(k.slots % RING):
                load(place, rounds)

        @block.tensor
        def _(pe):
            for place in range(RING - 1):
                pe.sem_inc(k.weights_used[place], 1)
            run(pe, "tensor")

        @block.vector
        def _(dve):
            run(dve, "vector")

        @block.scalar
        def _(act):
            run(act, "scalar")

        @block.gpsimd
        def _(pool):
            run(pool, "gpsimd")
    return k


def weight_stream(a):
    def feature(w, ktiles):
        k_in, n_out = w.shape
        t = w.reshape(ktiles, P, n_out // P, P).transpose(2, 0, 1, 3).reshape(-1, P, P)
        return t

    def paired(w):
        t = feature(w, D_TILES).reshape(2, FF_TILES, D_TILES, P, P)
        return t.transpose(1, 0, 2, 3, 4).reshape(-1, P, P)

    def rows_first(w):
        return w.reshape(-1, P, D_TILES, P).transpose(0, 2, 1, 3).reshape(-1, P, P)

    ab, c, w2 = a["ab_w_in"][0], a["c_w_in"][0], a["w_in_2"][0]
    parts = [ab[:, n * 512:(n + 1) * 512] for n in range(7)]
    tiles = [feature(parts[n], 8) for n in (0, 1, 3, 4, 6, 2, 5)]
    tiles += [feature(a["ab_w_out"][0], 8)]

    def layer_rest(i):
        return [paired(a["ffn_up"][i]), rows_first(a["ffn_down"][i]), feature(a["ple_gate"][i], 8),
                feature(a["ple_proj"][i], 2)]
    tiles += layer_rest(0)
    tiles += [feature(c, 8), feature(a["c_w_out"][0], 8)] + layer_rest(1)
    qd, kd, vd, qc, kc, vc, gd, gc = np.split(w2, np.cumsum([1024] * 3 + [512] * 3 + [1024] * 2)[:-1], axis=1)
    tiles += [feature(w, 8) for w in (qd, kd, qc, kc, vd, vc, gd)]
    tiles += [feature(a["w_branch_diff_2"][0], 8), feature(gc, 8), feature(a["w_branch_chunk_2"][0], 4),
              feature(a["w_out_2"][0], 8), feature(a["peer_wq_2"][0], 8)]
    u = a["peer_u_2"][0].reshape(P, P, D_TILES, P).transpose(1, 2, 3, 0)
    v = a["peer_v_2"][0].reshape(P, P, D_TILES, P).transpose(1, 2, 0, 3)
    u_groups = u.reshape(GROUPS, GROUP * D_TILES, P, P)
    v_groups = v.reshape(GROUPS, GROUP, D_TILES, P, P).transpose(0, 2, 1, 3, 4).reshape(GROUPS, -1, P, P)
    tiles += [u_groups[0]]
    for g in range(1, GROUPS):
        tiles += [u_groups[g], v_groups[g - 1]]
    tiles += [v_groups[GROUPS - 1]]
    stream = np.concatenate(tiles)
    return np.ascontiguousarray(stream.reshape(-1, SLOT_TILES, P, P).transpose(0, 2, 1, 3)).reshape(-1, P, SLOT)


def column_array(a):
    def down(v):
        return v.reshape(-1, P).T

    def rows(v):
        return np.broadcast_to(v.reshape(1, -1), (P, v.size))
    c = {}
    for i in range(2):
        c[f"mix{i}"], c[f"ffn{i}"], c[f"ple{i}"] = (down(a[n][i]) for n in ("mix_norm", "ffn_norm", "ple_norm"))
        c[f"conv{i}"], c[f"conv_b{i}"] = down(a["ffn_conv"][i]), down(a["ffn_conv_b"][i])
    c["norm1"], c["norm2"], c["final"] = down(a["norm1_w_2"][0]), down(a["norm2_w_2"][0]), down(a["final_norm_w_2"])
    c["hg_norm"], c["subln"], c["lb"] = down(a["hg_out_norm"][0]), down(a["diff_subln_w_2"][0]), down(a["hg_lb_logits"][0])
    c["q_norm"], c["k_norm"] = (np.concatenate([a[n][0]] * 2)[:, None] for n in ("q_norm", "k_norm"))
    c["b_gate"], c["sinks"] = down(a["b_gate_2"][0]), rows(a["sinks"][0])
    c["lambdas"] = rows(np.concatenate([a[n][0] for n in ("diff_lq1_2", "diff_lk1_2", "diff_lq2_2", "diff_lk2_2")]))
    c["rel_bias"] = np.concatenate([a["rel_bias"], np.ones((P - BUCKETS, SW_HEADS), np.float32)])
    out = np.concatenate([c[n] for n in COLUMN_WIDTHS], axis=1)
    assert out.shape == (P, COLUMN_N)
    return np.ascontiguousarray(out)


def feature_major(x, tiles):
    return np.ascontiguousarray(x.reshape(TOKENS, tiles, P).transpose(2, 1, 0)).reshape(P, tiles * TOKENS)


def host_arrays(a):
    keys = a["peer_keys_2"][0].transpose(1, 3, 0, 2).reshape(P, PEER_HEADS * PEER_KEYS)
    table = a["chunk_rel_bias_2"][0][:, ::-1].reshape(1, -1)
    return {"x": feature_major(a["x"][0], D_TILES), "consts": constants(), "columns": column_array(a),
            "weights": weight_stream(a), "peer_keys": np.ascontiguousarray(keys),
            "p": np.stack([feature_major(a["p"][i, 0], PLE_TILES).reshape(P, PLE_TILES, TOKENS) for i in range(2)]),
            "chunk_table": np.ascontiguousarray(np.broadcast_to(table, (P, table.size)))}


def build(nc, shapes, stop=None):
    dram = {n: nc.dram_tensor(f"in_{n}", s, F32, kind="ExternalInput").ap() for n, s in shapes.items()}
    dram["out"] = nc.dram_tensor("out_0", (P, D_TILES * TOKENS), F32, kind="ExternalOutput").ap()
    dram["window_rows"] = nc.dram_tensor("window_rows", (SW_HEADS, P, CONST_WIDTHS["bucket_rows"]), F32).ap()
    dram["chunk_rows"] = nc.dram_tensor("chunk_rows", (CH_HEADS, P, TOKENS + P - 1), F32).ap()
    dram["routing"] = nc.dram_tensor("routing", (CHUNKS, P, PEER_KEYS, CHUNK_TOKENS), F32).ap()
    program(nc, dram, stop)


def kernel(**inputs):
    import concourse.bacc as bacc
    from concourse.bass_utils import run_bass_kernel_spmd
    arrays = host_arrays({n: np.asarray(v) for n, v in inputs.items()})
    nc = bacc.Bacc("TRN2", target_bir_lowering=False, num_devices=1)
    build(nc, {n: v.shape for n, v in arrays.items()})
    r = run_bass_kernel_spmd(nc, [{f"in_{n}": v for n, v in arrays.items()}], core_ids=[0])
    out = r.results[0]["out_0"]
    return np.ascontiguousarray(out.reshape(P, D_TILES, TOKENS).transpose(2, 1, 0)).reshape(1, TOKENS, D_MODEL)
```

```python
import math
from contextlib import ExitStack, contextmanager

import numpy as np

import concourse.bass as bass
import concourse.mybir as mybir

F32 = mybir.dt.float32
F32R = mybir.dt.float32r
U32 = mybir.dt.uint32
I32 = mybir.dt.int32
ACT = mybir.ActivationFunctionType
ALU = mybir.AluOpType
AX = mybir.AxisListType

P = 128
TOKENS = 512
BLOCKS = TOKENS // P
D_MODEL = 1024
D_TILES = D_MODEL // P
EPS = 1e-6

RING = 2
UNROLL = 4
SLOT_TILES = 16
SLOT = SLOT_TILES * P

SB_HEADS, SB_DIM = 8, 64
HG_HEADS = 4
SW_HEADS, SW_KV = 16, 4
BUCKETS, WINDOW, MAX_DISTANCE = 32, 128, 128
FF_TILES = 2816 // P
CONV = 3
PLE_TILES = 2
DIFF_HEADS = 8
CH_HEADS, REL_CLIP = 8, 128
PEER_HEADS, PEER_KEYS, TOPK = 8, 128, 16
GROUP = 8
GROUPS = PEER_KEYS // GROUP
CHUNK_TOKENS = 64
CHUNKS = TOKENS // CHUNK_TOKENS
ROUTING_PAIRS = 3
MATRIX_PAIRS = CHUNKS * 2
LAM_INIT = 0.8 - 0.6 * math.exp(-0.3 * 0)
NEG = -1e30

CONST_WIDTHS = dict(ident=P, ones=P, neg_tri=P, neg_ones=P, neg_mask=P, strict=P, head_pair=P, iota=P,
                    distance=TOKENS, level_masks=8 * P, slopes=DIFF_HEADS, eps=1,
                    bucket_rows=2 * WINDOW + P - 1)
COLUMN_WIDTHS = dict(mix0=8, mix1=8, ffn0=8, ffn1=8, ple0=8, ple1=8, norm1=8, norm2=8, final=8,
                     hg_norm=1, q_norm=1, k_norm=1, subln=1, lb=HG_HEADS, b_gate=16,
                     conv0=3 * 44, conv1=3 * 44, conv_b0=44, conv_b1=44,
                     sinks=SW_HEADS, lambdas=4 * 64, rel_bias=SW_HEADS)


def offsets(widths):
    at, out = 0, {}
    for name, width in widths.items():
        out[name] = (at, width)
        at += width
    return out, at


CONST_AT, CONST_N = offsets(CONST_WIDTHS)
COLUMN_AT, COLUMN_N = offsets(COLUMN_WIDTHS)


def t5_bucket(distance):
    exact = BUCKETS // 2
    large = exact + (np.log(np.maximum(distance, exact) / exact) / math.log(MAX_DISTANCE / exact)
                     * (BUCKETS - exact)).astype(np.int32)
    return np.where(distance < exact, np.maximum(distance, 0), np.minimum(large, BUCKETS - 1))


def constants():
    row, col = np.arange(P)[:, None], np.arange(P)[None, :]
    c = {}
    c["ident"] = row == col
    c["ones"] = np.ones((P, P))
    c["neg_tri"] = np.where(row >= col, -1.0, 0.0)
    c["neg_ones"] = -np.ones((P, P))
    c["neg_mask"] = np.where(row >= col, NEG, 0.0)
    c["strict"] = row < col
    c["head_pair"] = (row // 64) == (col // 64)
    c["iota"] = np.broadcast_to(col, (P, P))
    y = np.arange(TOKENS)[None, :]
    c["distance"] = np.where((row < 64) & (y >= 448), 1e32, np.abs(row + 384 - y))
    levels = [((row // (2 * m)) == (col // (2 * m))) & (row % (2 * m) < m) & (col % (2 * m) >= m)
              for m in (64, 32, 16, 8, 4, 2, 1)]
    c["level_masks"] = np.concatenate(levels + [row == col], axis=1)
    c["slopes"] = np.broadcast_to(-np.exp2(-8.0 * np.arange(1, 9) / DIFF_HEADS), (P, DIFF_HEADS))
    c["eps"] = np.full((P, 1), EPS)
    u = np.arange(2 * WINDOW + P - 1)[None, :]
    distance = 2 * WINDOW - 1 - u
    band = (distance >= 0) & (distance < WINDOW)
    c["bucket_rows"] = np.where(row < BUCKETS, (t5_bucket(distance) == row) & band,
                                np.where((row == BUCKETS) & ~band, NEG, 0.0))
    return np.concatenate([np.broadcast_to(c[n], (P, w)).astype(np.float32)
                           for n, w in CONST_WIDTHS.items()], axis=1)


class Stage:

    def __init__(self, tensor=None, vector=None, scalar=None, meet=True):
        self.tensor, self.vector, self.scalar, self.meet = tensor, vector, scalar, meet


class Split:

    def __init__(self, memory, tiles):
        self.memory, self.tiles = memory, tiles
        self.tile_made = None

    def await_tile(self, eng, n):
        if self.tile_made is not None:
            eng.wait_ge(self.tile_made, n + 1)

    def high(self, n):
        return cut(self.memory, n * TOKENS, TOKENS)

    def low(self, n):
        return cut(self.memory, n * TOKENS + self.tiles * TOKENS, TOKENS)

    def __call__(self, n):
        return self.high(n), self.low(n)


def cut(ap, start, size):
    return ap[:, bass.ds(start, size)]


def after(signals):
    return signals + 1


def over_slots(eng, first, count, step):
    rounds = count // UNROLL if count >= 2 * UNROLL else 0
    if rounds:
        with eng.Fori(0, rounds) as r:
            for j in range(UNROLL):
                step(j, r * UNROLL + j, (first + j) % RING, r * (UNROLL // RING) + (first + j) // RING)
    for j in range(UNROLL * rounds, count):
        step(j % UNROLL, j, (first + j) % RING, (first + j) // RING)


def split_product(k, out, left, right, start, stop):
    for n, (a, b) in enumerate(((0, 0), (1, 0), (0, 1))):
        last = k.nc.tensor.matmul(out, left[a], right[b], start=start and n == 0, stop=stop and n == 2,
                                  skip_group_check=True)
        if n == 0:
            begun = last
    return begun, last


class Core:

    def __init__(self, nc, ctx, dram):
        self.nc, self.ctx, self.dram = nc, ctx, dram
        self.period = None
        self.h = self.sbuf("residual", [P, D_TILES * TOKENS])
        self.raw = self.sbuf("weights_raw", [P, RING * SLOT])
        self.ring = ctx.enter_context(nc.sbuf_tensor("weights_split", [P, RING * 2 * SLOT], F32R))
        self.consts = self.sbuf("constants", [P, CONST_N])
        self.columns = self.sbuf("columns", [P, COLUMN_N])
        self.banks = ctx.enter_context(nc.psum_tensor("banks", [P, 8, 512], F32))
        self.raw_in = [self.sem(f"weights_raw_in_{i}") for i in range(RING)]
        self.high_made = self.sem("weights_high_made")
        self.weights_ready = [self.sem(f"weights_split_{i}") for i in range(RING)]
        self.weights_used = [self.sem(f"weights_used_{i}") for i in range(RING)]
        self.meetings = self.sem("meetings")
        self.inputs_in = self.sem("inputs_in")
        self.held = self.sem("held")
        self.slots = 0
        self.scopes, self.named = [], 0

    def sbuf(self, name, shape):
        return self.ctx.enter_context(self.nc.sbuf_tensor(name, shape, F32))

    @contextmanager
    def scope(self):
        with ExitStack() as stack:
            self.scopes.append(stack)
            yield
            self.scopes.pop()

    def take(self, columns, dtype=F32):
        self.named += 1
        name = f"memory_{self.named}"
        return self.scopes[-1].enter_context(self.nc.sbuf_tensor(name, [P, columns], dtype))[:, :]

    def take_split(self, tiles):
        return Split(self.take(2 * tiles * TOKENS, F32R), tiles)

    def sem(self, name):
        if self.period is None:
            return self.ctx.enter_context(self.nc.semaphore(name))
        self.period_sems.append(self.period.enter_context(self.nc.semaphore(name)))
        return self.period_sems[-1]

    def sem_from_one(self, name):
        self.from_one.append(self.sem(name))
        return self.from_one[-1]

    def plan(self, periods):
        stages, before = [], []
        for make in periods:
            if len(before) == 2:
                before.pop(0)[0].close()
            self.period, self.period_sems, self.from_one = ExitStack(), [], []
            with self.scope():
                made = make()
            made.insert(0, Stage(tensor=self.opening(before[-1][1] if before else [], self.from_one), meet=False))
            before.append((self.period, self.period_sems))
            stages += made
        for period, _ in before:
            period.close()
        self.period = None
        return stages

    @staticmethod
    def opening(cleared, from_one):
        def tensor(pe):
            for sem in cleared:
                pe.sem_clear(sem)
            for sem in from_one:
                pe.sem_inc(sem, 1)
        return tensor

    def const(self, name):
        at, width = CONST_AT[name]
        return self.consts[:, at:at + width]

    def column(self, name, index=None):
        at, width = COLUMN_AT[name]
        if index is None:
            return self.columns[:, at:at + width]
        return cut(self.columns, at + index, 1)

    def tile(self, place, n):
        at = place * 2 * SLOT + n * P
        return self.ring[:, at:at + P], self.ring[:, at + SLOT:at + SLOT + P]

    def hold(self, eng):
        eng.sem_inc(self.held, 1)

    def take_slots(self, count):
        first = self.slots
        self.slots += count
        return first

    def slot_begins(self, pe, place, turn):
        pe.wait_ge(self.weights_ready[place], turn + 1)

    def release_previous(self, matmul, place):
        matmul.then_inc(self.weights_used[(place - 1) % RING], 1)


def projection(k, name, n_tiles, ktiles, source, evacuate, engine="scalar", banks=(0, 1, 2, 3), meet=False):
    slots = n_tiles * ktiles // SLOT_TILES
    per_slot = SLOT_TILES // ktiles
    first = k.take_slots(slots)
    nb = len(banks)
    bank_filled, bank_free = k.sem(name + "_bank_filled"), k.sem(name + "_bank_free")

    early = isinstance(source, Split) and source.tile_made is not None

    def tensor(pe):
        if early:
            pe.sem_inc(bank_free, nb)

        def step(j, slot, place, turn):
            k.slot_begins(pe, place, turn)
            for n in range(per_slot):
                pe.wait_ge(bank_free, slot * per_slot + (n + 1))
                bank = k.banks[:, banks[(j * per_slot + n) % nb], :]
                for kk in range(ktiles):
                    if early and j == 0 and n == 0:
                        source.await_tile(pe, kk)
                    begun, mm = split_product(k, bank, k.tile(place, n * ktiles + kk), source(kk), kk == 0,
                                              kk == ktiles - 1)
                    if n == 0 and kk == 0:
                        k.release_previous(begun, place)
                mm.then_inc(bank_filled, 1)
        over_slots(pe, first, slots, step)

    def reader(eng):
        if not early:
            eng.sem_inc(bank_free, nb)

        def step(j, slot, place, turn):
            for n in range(per_slot):
                tile = slot * per_slot + n
                eng.wait_ge(bank_filled, tile + 1)
                evacuate(eng, k.banks[:, banks[(j * per_slot + n) % nb], :], tile).then_inc(bank_free, 1)
        over_slots(eng, first, slots, step)

    return Stage(tensor=tensor, meet=meet, **{engine: reader})


def token_projection(k, name, slots, source, out, width, meet=False):
    first = k.take_slots(slots)
    filled, free = k.sem(name + "_banks_filled"), k.sem(name + "_banks_free")
    both = [k.banks[:, 4 + 2 * i:6 + 2 * i, :].rearrange("p b (h n) -> p (b h) n", h=2) for i in range(2)]

    def tensor(pe):
        def step(j, slot, place, turn):
            k.slot_begins(pe, place, turn)
            pe.wait_ge(free, slot + 1)
            weights = [k.ring[:, (2 * place + part) * SLOT:(2 * place + part + 1) * SLOT].rearrange(
                "p (n k c) -> p n k c", n=2, k=D_TILES) for part in range(2)]
            for b in range(BLOCKS):
                for kk in range(D_TILES):
                    begun, mm = split_product(k, both[j % 2][:, b, :], [x[:, b * P:(b + 1) * P] for x in source(kk)],
                                              [w[:, :, kk, :] for w in weights], kk == 0, kk == D_TILES - 1)
                    if b == 0 and kk == 0:
                        k.release_previous(begun, place)
            mm.then_inc(filled, 1)
        over_slots(pe, first, slots, step)

    def scalar(act):
        act.sem_inc(free, 2)
        rows = out.rearrange("p (b n) -> p b n", b=BLOCKS)

        def step(j, slot, place, turn):
            act.wait_ge(filled, slot + 1)
            k.nc.scalar.activation(rows[:, :, bass.ds(slot * 256, 256)], both[j % 2][:, :, :],
                                   ACT.Copy).then_inc(free, 1)
        over_slots(act, first, slots, step)

    return Stage(tensor=tensor, scalar=scalar, meet=meet)


def tile_of(memory):
    return lambda n: cut(memory, n * TOKENS, TOKENS)


def copy_into(k, memory, scale=1.0):
    def evacuate(act, bank, tile):
        return k.nc.scalar.activation(cut(memory, tile * TOKENS, TOKENS), bank, ACT.Copy, scale=scale)
    return evacuate


def add_to_residual(k):
    def evacuate(dve, bank, tile):
        h = cut(k.h, tile * TOKENS, TOKENS)
        return k.nc.vector.tensor_tensor(h, bank, h, ALU.add)
    return evacuate


def norm(k, name, gain, out, meet=True):
    with k.scope():
        squares, total, deviation, rstd = k.take(8 * 512), k.take(512), k.take(512), k.take(512)
    split = isinstance(out, Split)
    squared, summed, totalled, rooted, ready, scaled, high_made = (
        k.sem(f"{name}_{s}") for s in ("squared", "summed", "totalled", "rooted", "ready", "scaled", "high_made"))
    if not meet:
        out.tile_made = k.sem(name + "_low_made")

    def scalar(act):
        for i in range(D_TILES):
            k.nc.scalar.activation(cut(squares, i * 512, 512), cut(k.h, i * 512, 512), ACT.Square).then_inc(squared, 1)
        act.wait_ge(totalled, 1)
        k.nc.scalar.activation(deviation, k.banks[:, 0, :], ACT.Sqrt, bias=k.const("eps"),
                               scale=1.0 / D_MODEL).then_inc(rooted, 1)
        if split:
            for i in range(D_TILES):
                act.wait_ge(scaled, i + 1)
                k.nc.scalar.activation(out.high(i), cut(squares, i * 512, 512), ACT.Copy).then_inc(high_made, 1)

    def vector(dve):
        v = k.nc.vector
        for i in range(1, D_TILES):
            dve.wait_ge(squared, i + 1)
            if i > 1:
                dve.wait_ge(summed, i - 1)
            other = cut(squares, 0, 512) if i == 1 else total
            v.tensor_tensor(total, other, cut(squares, i * 512, 512), ALU.add).then_inc(summed, 1)
        dve.wait_ge(rooted, 1)
        v.reciprocal(rstd, deviation).then_inc(ready, 1)
        dve.wait_ge(ready, 1)
        for i in range(D_TILES + 1):
            if i < D_TILES:
                y = cut(squares if split else out, i * 512, 512)
                v.scalar_tensor_tensor(out=y, in0=cut(k.h, i * 512, 512), scalar=k.column(gain, i), in1=rstd,
                                       op0=ALU.mult, op1=ALU.mult).then_inc(scaled, 1)
            if i >= 1 and split:
                dve.wait_ge(high_made, i)
                low = v.tensor_tensor(out.low(i - 1), cut(squares, (i - 1) * 512, 512),
                                      out.high(i - 1).bitcast(F32), ALU.subtract)
                if not meet:
                    low.then_inc(out.tile_made, 1)

    def tensor(pe):
        pe.wait_ge(summed, D_TILES - 1)
        k.nc.tensor.matmul(k.banks[:, 0, :], k.const("ones"), total, start=True, stop=True).then_inc(totalled, 1)

    return Stage(tensor=tensor, vector=vector, scalar=scalar, meet=meet)


def split_stage(k, name, source, tiles, out):
    high_made = k.sem(name + "_high_made")

    def scalar(act):
        for n in range(tiles):
            k.nc.scalar.activation(out.high(n), cut(source, n * 512, 512), ACT.Copy).then_inc(high_made, 1)

    def vector(dve):
        for n in range(tiles):
            dve.wait_ge(high_made, n + 1)
            k.nc.vector.tensor_tensor(out.low(n), cut(source, n * 512, 512), out.high(n).bitcast(F32), ALU.subtract)

    return Stage(vector=vector, scalar=scalar)


def collect(k, slots, operand, filled, ready=None, used=None):
    first = k.take_slots(slots)

    def tensor(pe):
        def step(position, slot, place, turn, begins=False, ends=False):
            k.slot_begins(pe, place, turn)
            for kk in range(2):
                if ready:
                    ready(pe, slot, kk)
                for n in range(D_TILES):
                    begun, last = split_product(k, k.banks[:, n, :], k.tile(place, kk * D_TILES + n),
                                                operand(slot, kk, position), kk == 0 and begins, kk == 1 and ends)
                    if kk == 0 and n == 0:
                        k.release_previous(begun, place)
                    if kk == 1 and ends:
                        last.then_inc(filled, 1)
                if used and not (kk == 1 and ends):
                    last.then_inc(used, 1)

        step(0, 0, first % RING, first // RING, begins=True)
        rounds = (slots - 2) // UNROLL
        with pe.Fori(0, rounds) as r:
            for j in range(UNROLL):
                g = first + 1 + j
                step((1 + j) % UNROLL, r * UNROLL + (1 + j), g % RING, r * (UNROLL // RING) + g // RING)
        for s in range(1 + rounds * UNROLL, slots):
            step(s % UNROLL, s, (first + s) % RING, (first + s) // RING, ends=s == slots - 1)
    return tensor


def feed_forward(k, layer):
    name = f"ffn{layer}"
    hn = k.take_split(D_TILES)
    stages = [norm(k, name + "_norm", name, hn, meet=False)]
    act_in = k.take_split(FF_TILES)
    gate, up = k.take(2 * 512), k.take(2 * 512)
    filled, free = k.sem(name + "_pair_filled"), k.sem(name + "_pair_free")
    conv_done, silu_done, multiplied, high_made, low_made, dve_order = (k.sem(f"{name}_{s}") for s in (
        "conv_done", "silu_done", "multiplied", "high_made", "low_made", "vector_order"))
    first = k.take_slots(FF_TILES)
    taps, bias = f"conv{layer}", f"conv_b{layer}"

    def tensor(pe):
        pe.sem_inc(free, 2)

        def step(j, slot, place, turn):
            k.slot_begins(pe, place, turn)
            pe.wait_ge(free, slot + 1)
            for n in range(2):
                for kk in range(D_TILES):
                    if j == 0 and n == 0:
                        hn.await_tile(pe, kk)
                    begun, mm = split_product(k, k.banks[:, 2 * (j % 2) + n, :], k.tile(place, n * D_TILES + kk),
                                              hn(kk), kk == 0, kk == D_TILES - 1)
                    if n == 0 and kk == 0:
                        k.release_previous(begun, place)
            mm.then_inc(filled, 1)
        over_slots(pe, first, FF_TILES, step)

    def vector(dve):
        def step(j, slot, place, turn):
            dve.wait_ge(filled, slot + 1)
            p = j % 2
            for tap in (2, 1, 0):
                s = CONV - 1 - tap
                for half, (buffer, at) in enumerate(((gate, 0), (up, FF_TILES))):
                    bank = k.banks[:, 2 * p + half, :]
                    y = buffer[:, p * 512 + s:(p + 1) * 512]
                    weight = k.column(taps, slot + (tap * 2 * FF_TILES + at))
                    if s == 0:
                        ins = k.nc.vector.tensor_scalar(y, bank, weight, k.column(bias, slot + at), ALU.mult, ALU.add)
                    else:
                        ins = k.nc.vector.scalar_tensor_tensor(out=y, in0=bank[:, 0:512 - s], scalar=weight, in1=y,
                                                               op0=ALU.mult, op1=ALU.add)
                    if s < 2:
                        ins.then_inc(dve_order, 1)
                    elif half == 1:
                        ins.then_inc(conv_done, 1)
                if s < 2:
                    dve.wait_ge(dve_order, slot * 4 + (2 * s + 2))
            dve.wait_ge(conv_done, slot + 1)
            dve.sem_inc(free, 1)
            dve.wait_ge(silu_done, slot + 1)
            half = slice(p * 512, (p + 1) * 512)
            k.nc.vector.tensor_tensor(up[:, half], gate[:, half], up[:, half], ALU.mult).then_inc(multiplied, 1)
            dve.wait_ge(high_made, slot + 1)
            k.nc.vector.tensor_tensor(act_in.low(slot), up[:, half], act_in.high(slot).bitcast(F32),
                                      ALU.subtract).then_inc(low_made, 1)
            dve.wait_ge(low_made, slot + 1)
        over_slots(dve, first, FF_TILES, step)

    def scalar(act):
        def step(j, slot, place, turn):
            p = j % 2
            act.wait_ge(conv_done, slot + 1)
            half = slice(p * 512, (p + 1) * 512)
            k.nc.scalar.activation(gate[:, half], gate[:, half], ACT.Silu).then_inc(silu_done, 1)
            act.wait_ge(multiplied, slot + 1)
            k.nc.scalar.activation(act_in.high(slot), up[:, half], ACT.Copy).then_inc(high_made, 1)
        over_slots(act, first, FF_TILES, step)

    up_stage = Stage(tensor=tensor, vector=vector, scalar=scalar)

    down_filled = k.sem(name + "_down_filled")
    down_tensor = collect(k, FF_TILES // 2, lambda slot, kk, at: act_in(slot * 2 + kk), down_filled)

    def down_vector(dve):
        for n in range(D_TILES):
            dve.wait_ge(down_filled, n + 1)
            add_to_residual(k)(dve, k.banks[:, n, :], n)

    return stages + [up_stage, Stage(tensor=down_tensor, vector=down_vector)]


def layer_embedding(k, layer):
    name = f"ple{layer}"
    hn = k.take_split(D_TILES)
    embedding, gates, product = k.take(PLE_TILES * 512), k.take(D_TILES * 512), k.take(512)
    embedding_split = k.take_split(PLE_TILES)
    loaded, order = k.sem(name + "_embedding_in"), k.sem(name + "_product_order")

    def load(act):
        act.dma_start(embedding.rearrange("p (c t) -> p c t", c=PLE_TILES), k.dram["p"][layer]).then_inc(loaded, 16)

    def gate(act, bank, tile):
        return k.nc.scalar.activation(cut(gates, tile * 512, 512), bank, ACT.Sigmoid)

    def add(dve, bank, tile):
        if tile >= 1:
            dve.wait_ge(order, 2 * tile)
        k.nc.vector.tensor_tensor(product, bank, cut(gates, tile * 512, 512), ALU.mult).then_inc(order, 1)
        dve.wait_ge(order, 2 * tile + 1)
        h = cut(k.h, tile * 512, 512)
        k.nc.vector.tensor_tensor(h, product, h, ALU.add).then_inc(order, 1)
        return dve.drain()

    normed = norm(k, name + "_norm", f"ple{layer}", hn)
    loading = Stage(scalar=load, vector=lambda dve: dve.wait_ge(loaded, 16), meet=False)
    gated = projection(k, name + "_gate", D_TILES, D_TILES, hn, gate, meet=True)
    mixed = projection(k, name + "_mix", D_TILES, PLE_TILES, embedding_split, add, engine="vector", meet=True)
    return [loading, normed, split_stage(k, name + "_embedding", embedding, PLE_TILES, embedding_split), gated, mixed]


def turn(k, name, source, width, tiles, finish, engine="scalar"):
    filled, free = k.sem(name + "_turned"), k.sem(name + "_turn_free")

    def tensor(pe):
        for n, tile in enumerate(tiles):
            if n >= 4:
                pe.wait_ge(free, n - 3)
            for b in range(BLOCKS):
                mm = k.nc.tensor.transpose(k.banks[:, n % 4, b * P:(b + 1) * P],
                                           source[:, b * width + tile * P:b * width + (tile + 1) * P],
                                           k.const("ident"))
            mm.then_inc(filled, 1)

    def reader(eng):
        for n in range(len(tiles)):
            eng.wait_ge(filled, n + 1)
            finish(eng, k.banks[:, n % 4, :], n).then_inc(free, 1)

    return Stage(tensor=tensor, **{engine: reader})


def turn_split(k, name, source, width, tiles, out, scale=1.0, gain=None, gate=None):
    filled, high_made, low_made, scaled = (k.sem(f"{name}_{s}") for s in ("turned", "high_made", "low_made", "scaled"))
    gated = k.take(len(tiles) * 512) if gate is not None else None

    def tensor(pe):
        for n, tile in enumerate(tiles):
            if n >= 4:
                pe.wait_ge(low_made, n - 3)
            for b in range(BLOCKS):
                mm = k.nc.tensor.transpose(k.banks[:, n % 4, b * P:(b + 1) * P],
                                           source[:, b * width + tile * P:b * width + (tile + 1) * P],
                                           k.const("ident"))
            mm.then_inc(filled, 1)

    def scalar(act):
        for n in range(len(tiles)):
            high = out[n][0]
            if gate is None:
                act.wait_ge(filled, n + 1)
                k.nc.scalar.activation(high, k.banks[:, n % 4, :], ACT.Copy, scale=scale).then_inc(high_made, 1)
            else:
                act.wait_ge(scaled, n + 1)
                k.nc.scalar.activation(high, cut(gated, n * 512, 512), ACT.Copy).then_inc(high_made, 1)

    def vector(dve):
        v = k.nc.vector
        for n in range(len(tiles)):
            high, low = out[n]
            if gate is None:
                dve.wait_ge(high_made, n + 1)
                v.scalar_tensor_tensor(out=low, in0=k.banks[:, n % 4, :], scalar=scale, in1=high.bitcast(F32),
                                       op0=ALU.mult, op1=ALU.subtract).then_inc(low_made, 1)
            else:
                y = cut(gated, n * 512, 512)
                dve.wait_ge(filled, n + 1)
                v.scalar_tensor_tensor(out=y, in0=k.banks[:, n % 4, :], scalar=gain, in1=cut(gate, n * 512, 512),
                                       op0=ALU.mult, op1=ALU.mult).then_inc(scaled, 1)
                dve.wait_ge(high_made, n + 1)
                v.tensor_tensor(low, y, high.bitcast(F32), ALU.subtract).then_inc(low_made, 1)

    return Stage(tensor, vector, scalar)


def feature_copy(k, memory):
    return lambda act, bank, n: k.nc.scalar.activation(cut(memory, n * 512, 512), bank, ACT.Copy)


def stick_breaking(k, queries, keys, values, value_width, out):
    at = [0, 512, 896, 1152]
    size = [TOKENS - P * j for j in range(BLOCKS)]
    q_head, k_head = k.take(512), k.take(512)
    softplus_part = [k.take(1280) for _ in range(2)]
    softplus = [k.take(1280) for _ in range(2)]
    weights = [k.take(1280) for _ in range(2)]
    (staged, scored, absolute, exped, logged, summed, raw_sum, exponent_ready, weights_done, attended, emptied) = (
        (k.sem_from_one if s in ("scored", "emptied") else k.sem)("stick_" + s) for s in ("staged", "scored", "absolute", "exp_neg", "log1p", "softplus", "softplus_raw",
                                      "exponent", "weights", "attended", "emptied"))
    pairs = SB_HEADS // 2
    order = [3, 2, 1, 0]

    def tensor(pe):
        with pe.Fori(0, pairs) as i:
            pe.wait_ge(staged, i * 2 + 2)
            for f in range(2):
                pe.wait_ge(emptied, after(i * 2))
                rows = slice(64 * f, 64 * f + 64)
                for j in order:
                    k.nc.tensor.matmul(k.banks[:, 4 * f + j, 0:size[j]], k_head[rows, j * P:(j + 1) * P],
                                       q_head[rows, j * P:TOKENS], start=True, stop=True,
                                       skip_group_check=True).then_inc(scored, 1)
            for f in range(2):
                for n, j in enumerate(order):
                    pe.wait_ge(summed, i * 8 + (4 * f + n + 1))
                    bank = k.banks[:, 4 * f + j, :]
                    own = softplus[f][:, at[j]:at[j] + size[j]]
                    k.nc.tensor.matmul(bank[:, 0:size[j]], k.const("neg_tri"), own, start=False, stop=False,
                                       skip_group_check=True)
                    for later in range(j + 1, BLOCKS):
                        k.nc.tensor.matmul(bank[:, (later - j) * P:size[j]], k.const("neg_ones"),
                                           softplus[f][:, at[later]:at[later] + size[later]], start=False,
                                           stop=False, skip_group_check=True)
                    k.nc.tensor.matmul(bank[:, 0:P], k.const("ident"), k.const("neg_mask"), start=False,
                                       stop=True, skip_group_check=True).then_inc(exponent_ready, 1)
            for f in range(2):
                pe.wait_ge(weights_done, i * 8 + (4 * f + 4))
                for n in range(BLOCKS):
                    for j in range(n + 1):
                        w = weights[f][:, at[j] + (n - j) * P:at[j] + (n - j + 1) * P]
                        mm = k.nc.tensor.matmul(k.banks[:, 4 * f + 3, n * 64:(n + 1) * 64], w,
                                                cut(values, j * value_width + i * 128 + f * 64, 64),
                                                start=j == 0, stop=j == n, skip_group_check=True)
                mm.then_inc(attended, 1)

    def vector(dve):
        with dve.Fori(0, pairs) as i:
            dve.wait_ge(scored, after(i * 8))
            k.nc.vector.tensor_copy(q_head, cut(queries, i * 512, 512)).then_inc(staged, 1)
            k.nc.vector.tensor_copy(k_head, cut(keys, i * 512, 512)).then_inc(staged, 1)
            for f in range(2):
                for n, j in enumerate(order):
                    dve.wait_ge(logged, i * 8 + (4 * f + n + 1))
                    own = softplus[f][:, at[j]:at[j] + size[j]]
                    k.nc.vector.scalar_tensor_tensor(
                        out=own, in0=k.banks[:, 4 * f + j, 0:size[j]], scalar=0.0,
                        in1=softplus_part[f][:, at[j]:at[j] + size[j]], op0=ALU.max, op1=ALU.add).then_inc(raw_sum, 1)
                    dve.wait_ge(raw_sum, i * 8 + (4 * f + n + 1))
                    k.nc.vector.tensor_tensor(own[:, 0:P], own[:, 0:P], k.const("strict"), ALU.mult).then_inc(summed, 1)

    def scalar(act):
        with act.Fori(0, pairs) as i:
            tiles = [(4 * f + n + 1, 4 * f + j, softplus_part[f][:, at[j]:at[j] + size[j]])
                     for f in range(2) for n, j in enumerate(order)]
            for n, bank, part in tiles:
                act.wait_ge(scored, after(i * 8 + n))
                k.nc.scalar.activation(part, k.banks[:, bank, 0:size[bank % 4]], ACT.Abs).then_inc(absolute, 1)
            for n, bank, part in tiles:
                act.wait_ge(absolute, i * 8 + n)
                k.nc.scalar.activation(part, part, ACT.Exp, scale=-1.0).then_inc(exped, 1)
            for n, bank, part in tiles:
                act.wait_ge(exped, i * 8 + n)
                k.nc.scalar.activation(part, part, ACT.Ln, bias=1.0).then_inc(logged, 1)
            for f in range(2):
                for n, j in enumerate(order):
                    act.wait_ge(exponent_ready, i * 8 + (4 * f + n + 1))
                    k.nc.scalar.activation(weights[f][:, at[j]:at[j] + size[j]], k.banks[:, 4 * f + j, 0:size[j]],
                                           ACT.Exp).then_inc(weights_done, 1)
            for f in range(2):
                act.wait_ge(attended, i * 2 + (f + 1))
                k.nc.scalar.activation(out.rearrange("p (b n) -> p b n", b=BLOCKS)[:, :, bass.ds(i * 128 + f * 64, 64)],
                                       k.banks[:, 4 * f + 3, 0:256].rearrange("p (b n) -> p b n", b=BLOCKS),
                                       ACT.Copy).then_inc(emptied, 1)

    return Stage(tensor, vector, scalar)


def hgrn_gates(k, q, f, g, keep, decay, small):
    zero, e, inverse, share, lb, rest = (small[:, 4 * n:4 * n + 4] for n in range(6))
    activated, order, floors = k.sem("hgrn_activated"), k.sem("hgrn_gates_order"), k.sem("hgrn_lower_bound")
    logits = k.column("lb")

    def scalar(act):
        act.wait_ge(floors, 1)
        k.nc.scalar.activation(e, zero, ACT.Exp).then_inc(activated, 1)
        k.nc.scalar.activation(keep, f, ACT.Sigmoid, scale=-1.0).then_inc(activated, 1)
        act.wait_ge(activated, 2)
        k.nc.scalar.activation(f, f, ACT.Sigmoid).then_inc(activated, 1)
        k.nc.scalar.activation(q, q, ACT.Silu)
        k.nc.scalar.activation(g, g, ACT.Silu)
        act.wait_ge(order, 2 * HG_HEADS)
        k.nc.scalar.activation(f, f, ACT.Ln).then_inc(activated, 1)

    def vector(dve):
        v = k.nc.vector
        v.tensor_tensor(zero, logits, logits, ALU.subtract).then_inc(floors, 1)
        dve.wait_ge(activated, 1)
        v.reciprocal(inverse, e).then_inc(floors, 1)
        dve.wait_ge(floors, 2)
        v.tensor_tensor(share, e, inverse, ALU.mult).then_inc(floors, 1)
        dve.wait_ge(floors, 3)
        v.tensor_tensor(lb, share, share, ALU.subtract).then_inc(floors, 1)
        dve.wait_ge(floors, 4)
        v.tensor_scalar(rest, lb, -1.0, 1.0, ALU.mult, ALU.add).then_inc(floors, 1)
        dve.wait_ge(floors, 5)
        dve.wait_ge(activated, 3)
        for n in range(HG_HEADS):
            t = slice(n * 512, (n + 1) * 512)
            v.tensor_scalar(f[:, t], f[:, t], rest[:, n:n + 1], lb[:, n:n + 1], ALU.mult, ALU.add).then_inc(order, 1)
            v.tensor_scalar(keep[:, t], keep[:, t], rest[:, n:n + 1], None, ALU.mult).then_inc(order, 1)
        dve.wait_ge(activated, 4)
        for n in range(HG_HEADS * BLOCKS):
            t = slice(n * P, (n + 1) * P)
            v.tensor_tensor_scan(decay[:, t], k.const("ones"), f[:, t], 0.0, ALU.mult, ALU.add)

    return Stage(vector=vector, scalar=scalar)


def hgrn_heads(k, q, keep, decay, values, value_width, value_at, out, out_at):
    halves = [64, 32, 16, 8, 4, 2, 1]
    n_levels = len(halves)
    difference = [k.take(512) for _ in range(2)]
    q_part = [k.take(512) for _ in range(2)]
    k_part = [k.take(512) for _ in range(2)]
    from_start, q_decayed, to_end, k_decayed, k_turned, scores = (k.take(512) for _ in range(6))
    state = k.take(P)
    (cleared, subtracted, exped, q_ready, k_ready, copied, scored, merged, turned, turned_copied, updated,
     state_ready, attended, emptied, end_order, q_dec, k_dec) = (
         (k.sem_from_one if s in ("attended", "scored", "merged", "emptied") else k.sem)("hgrn_" + s) for s in (
         "cleared", "subtracted", "exped", "q_ready", "k_ready", "diagonal_copied", "scored", "merged", "turned",
         "turned_copied", "updated", "state_ready", "attended", "emptied", "scores_cleared", "q_decayed", "k_decayed"))

    def split(ap, m):
        v = ap.rearrange("p (n m) -> p n m", m=2 * m)
        return v[:, :, 0:m], v[:, :, m:2 * m]

    def per_chunk(ap):
        return ap.rearrange("p (c t) -> p c t", c=BLOCKS)

    def vector(dve):
        v = k.nc.vector
        for n, buffer in enumerate(q_part + k_part):
            v.memset(buffer, 0.0).then_inc(cleared, 1)
        dve.wait_ge(cleared, 4)
        dve.sem_inc(merged, 1)
        with dve.Fori(0, HG_HEADS) as i:
            b, qh, kh = (cut(memory, i * 512, 512) for memory in (decay, q, keep))
            dve.wait_ge(attended, after(i * 4))
            v.memset(scores, 0.0).then_inc(end_order, 1)
            dve.wait_ge(end_order, i + 1)

            def subtract(level):
                if level == 8:
                    v.tensor_tensor(per_chunk(difference[0]), per_chunk(b)[:, :, P - 1:P].broadcast_to([P, BLOCKS, P]),
                                    per_chunk(b), ALU.subtract).then_inc(subtracted, 1)
                    return
                m = halves[level]
                first, second = split(b, m)
                ref = first[:, :, m - 1:m].broadcast_to([P, TOKENS // (2 * m), m])
                d_first, d_second = split(difference[level % 2], m)
                v.tensor_tensor(d_first, ref, first, ALU.subtract)
                v.tensor_tensor(d_second, second, ref, ALU.subtract).then_inc(subtracted, 1)

            def multiply(level):
                dve.wait_ge(exped, i * 9 + (level + 1))
                dve.wait_ge(scored, after(i * 8 + (level - 1) if level else i * 8))
                m = halves[level]
                v.tensor_tensor(split(q_part[level % 2], m)[1], split(qh, m)[1],
                                split(difference[level % 2], m)[1], ALU.mult).then_inc(q_ready, 1)
                v.tensor_tensor(split(k_part[level % 2], m)[0], split(kh, m)[0],
                                split(difference[level % 2], m)[0], ALU.mult).then_inc(k_ready, 1)

            def merge(level):
                dve.wait_ge(scored, after(i * 8 + (level + 1)))
                dve.wait_ge(merged, after(i * 8 + (level + 1)))
                k.hold(dve)
                mask = k.const("level_masks")[:, level * P:(level + 1) * P].bitcast(I32)
                v.copy_predicated(per_chunk(scores), mask.unsqueeze(1).broadcast_to([P, BLOCKS, P]),
                                  per_chunk(k.banks[:, level % 2, :])).then_inc(merged, 1)

            subtract(0)
            subtract(1)
            for level in range(n_levels):
                multiply(level)
                if level + 2 < n_levels:
                    dve.wait_ge(q_ready, i * 7 + (level + 1))
                    dve.wait_ge(k_ready, i * 7 + (level + 1))
                    subtract(level + 2)
                if level >= 1:
                    merge(level - 1)
            dve.wait_ge(q_ready, i * 7 + 7)
            dve.wait_ge(k_ready, i * 7 + 7)
            subtract(8)
            dve.wait_ge(exped, i * 9 + 8)
            v.tensor_tensor(k_decayed, kh, to_end, ALU.mult).then_inc(k_dec, 1)
            dve.wait_ge(exped, i * 9 + 9)
            v.tensor_tensor(q_decayed, qh, from_start, ALU.mult).then_inc(q_dec, 1)
            merge(n_levels - 1)
            merge(n_levels)
            for c in range(BLOCKS - 1):
                dve.wait_ge(updated, i * 3 + (c + 1))
                if c == 0:
                    v.tensor_copy(state, k.banks[:, 4, 0:P]).then_inc(state_ready, 1)
                else:
                    dve.wait_ge(state_ready, i * 3 + c)
                    dve.wait_ge(attended, after(i * 4 + (c + 1)))
                    v.scalar_tensor_tensor(out=state, in0=state, scalar=from_start[:, c * P + P - 1:c * P + P],
                                           in1=k.banks[:, 4 + c % 2, 0:P], op0=ALU.mult,
                                           op1=ALU.add).then_inc(state_ready, 1)

    def scalar(act):
        s = k.nc.scalar
        with act.Fori(0, HG_HEADS) as i:
            for level in range(n_levels):
                act.wait_ge(subtracted, i * 8 + (level + 1))
                s.activation(difference[level % 2], difference[level % 2], ACT.Exp).then_inc(exped, 1)
            act.wait_ge(scored, after(i * 8 + 6))
            s.activation(q_part[1], cut(q, i * 512, 512), ACT.Copy).then_inc(copied, 1)
            s.activation(k_part[1], cut(keep, i * 512, 512), ACT.Copy).then_inc(copied, 1)
            act.wait_ge(subtracted, i * 8 + 8)
            act.wait_ge(attended, after(i * 4))
            s.activation(to_end, difference[0], ACT.Exp).then_inc(exped, 1)
            s.activation(from_start, cut(decay, i * 512, 512), ACT.Exp).then_inc(exped, 1)
            act.wait_ge(turned, i + 1)
            s.activation(k_turned, k.banks[:, 2, :], ACT.Copy).then_inc(turned_copied, 1)
            act.wait_ge(attended, after(i * 4 + 4))
            s.activation(per_chunk_out(i), per_chunk(k.banks[:, 3, :]), ACT.Copy).then_inc(emptied, 1)

    def per_chunk_out(i):
        return out.rearrange("p (b n) -> p b n", b=BLOCKS)[:, :, bass.ds(i * P + out_at, P)]

    def tensor(pe):
        mm = k.nc.tensor.matmul
        with pe.Fori(0, HG_HEADS) as i:
            for level in range(n_levels + 1):
                if level < n_levels:
                    pe.wait_ge(q_ready, i * 7 + (level + 1))
                    pe.wait_ge(k_ready, i * 7 + (level + 1))
                else:
                    pe.wait_ge(copied, i * 2 + 2)
                pe.wait_ge(merged, after(i * 8 + level))
                for c in range(BLOCKS):
                    t = slice(c * P, (c + 1) * P)
                    last = mm(k.banks[:, level % 2, t], k_part[level % 2][:, t], q_part[level % 2][:, t],
                              start=True, stop=True)
                last.then_inc(scored, 1)
            pe.wait_ge(k_dec, i + 1)
            for c in range(BLOCKS):
                t = slice(c * P, (c + 1) * P)
                last = k.nc.tensor.transpose(k.banks[:, 2, t], k_decayed[:, t], k.const("ident"))
            last.then_inc(turned, 1)
            pe.wait_ge(merged, after(i * 8 + 9))
            pe.wait_ge(q_dec, i + 1)
            pe.wait_ge(turned_copied, i + 1)
            pe.wait_ge(emptied, after(i))
            for c in range(BLOCKS):
                t = slice(c * P, (c + 1) * P)
                value = cut(values, i * P + (c * value_width + value_at), P)
                if c < BLOCKS - 1:
                    mm(k.banks[:, 4 + c % 2, 0:P], k_turned[:, t], value, start=True, stop=True).then_inc(updated, 1)
                last = mm(k.banks[:, 3, t], scores[:, t], value, start=True, stop=c == 0)
                if c:
                    pe.wait_ge(state_ready, i * 3 + c)
                    last = mm(k.banks[:, 3, t], q_decayed[:, t], state, start=False, stop=True)
                last.then_inc(attended, 1)

    return Stage(tensor, vector, scalar)


def token_norm(k, name, values, count, width, temp, small, scale):
    order, rooted = k.sem(name + "_order"), k.sem(name + "_rooted")
    v3 = values.rearrange("p (c n) -> p c n", n=width)
    sums, deviation, rstd = (small[:, n * count:(n + 1) * count] for n in range(3))

    def scalar(act):
        k.nc.scalar.activation(temp, values, ACT.Square).then_inc(rooted, 1)
        act.wait_ge(order, 1)
        k.nc.scalar.activation(deviation, sums, ACT.Sqrt, bias=k.const("eps"), scale=1.0 / width).then_inc(rooted, 1)

    def vector(dve):
        v = k.nc.vector
        dve.wait_ge(rooted, 1)
        v.tensor_reduce(sums, temp.rearrange("p (c n) -> p c n", n=width), AX.X, ALU.add).then_inc(order, 1)
        dve.wait_ge(rooted, 2)
        v.reciprocal(rstd, deviation).then_inc(order, 1)
        dve.wait_ge(order, 2)
        v.scalar_tensor_tensor(out=v3, in0=v3, scalar=scale, in1=rstd.unsqueeze(2).broadcast_to([P, count, width]),
                               op0=ALU.mult, op1=ALU.mult)

    return Stage(vector=vector, scalar=scalar)


def mixer_ab(k):
    with k.scope():
        heads = k.take(20 * 512)
        values = k.take(BLOCKS * 1024)
        qa, ka, qb, fb, gb = (heads[:, n * 2048:(n + 1) * 2048] for n in range(5))

        def evacuate(act, bank, tile):
            return k.nc.scalar.activation(cut(heads, tile * TOKENS, TOKENS), bank, ACT.Copy)

        def scale_queries(act):
            k.nc.scalar.activation(qa, qa, ACT.Copy, scale=SB_DIM ** -0.5)

        with k.scope():
            hn = k.take_split(D_TILES)
            stages = [norm(k, "mix0_norm", "mix0", hn, meet=False),
                      projection(k, "ab_heads", 20, D_TILES, hn, evacuate),
                      token_projection(k, "ab_values", 4, hn, values, 1024, meet=True)]
        out = k.take(BLOCKS * 1024)
        with k.scope():
            stages += [Stage(scalar=scale_queries), stick_breaking(k, qa, ka, values, 1024, out)]
        keep, decay = heads[:, 0:2048], heads[:, 2048:4096]
        with k.scope():
            stages += [hgrn_gates(k, qb, fb, gb, keep, decay, k.take(64)),
                       hgrn_heads(k, qb, keep, decay, values, 1024, 512, out, 512)]
        gathered = heads[:, 0:2048]

        def gather(act):
            k.nc.scalar.activation(gathered.rearrange("p (b n) -> p b n", b=BLOCKS),
                                   out.rearrange("p (b n) -> p b n", b=BLOCKS)[:, :, 512:1024], ACT.Copy)

        stages.append(Stage(scalar=gather))
        with k.scope():
            stages.append(token_norm(k, "hg_norm", gathered, 16, P, k.take(2048), k.take(64), 1.0))
        mixed = k.take_split(D_TILES)
        stages += [turn_split(k, "stick_out", out, 1024, range(4), [mixed(n) for n in range(4)]),
                   turn_split(k, "hgrn_out", gathered, 512, range(4), [mixed(4 + n) for n in range(4)],
                              gain=k.column("hg_norm", 0), gate=gb),
                   projection(k, "ab_out", D_TILES, D_TILES, mixed, add_to_residual(k), engine="vector", meet=True)]
    return stages


def softmax_attention(k, name, repeats, units, load, value_of, value_cols, out, out_of, bias_of, scale,
                      span, prepare=None, prepares=1, sink_of=None, minus=None):
    count = len(units)
    per = 2 if minus is not None else 1
    outs = count // per
    logits = [k.take(span) for _ in range(3)]
    probs = [k.take(span) for _ in range(3)]
    combined = [k.take(span) for _ in range(2)] if per == 2 else None
    turned = [k.take(span) for _ in range(2)]
    small = k.take(6 * 4 + 8)
    largest, shift, total, sink_exp, sum_all, signed = (small[:, 4 * n:4 * n + 4] for n in range(6))
    inverse = small[:, 24:32]
    lead = 3
    (staged, scored, ready, maxed, shifted, exped, normed, joined, turned_done, copied, attended, emptied, order,
     prepared) = (
         (k.sem if s in ("staged", "maxed", "shift_ready", "inverse_ready", "prepared")
          else k.sem_from_one)(f"{name}_{s}") for s in (
         "staged", "scored", "logits_ready", "maxed", "shift_ready", "exped", "inverse_ready", "joined", "turned",
         "turned_copied", "attended", "emptied", "order", "prepared"))
    loads = load(None, None)
    exps = 2 if sink_of else 1

    def tensor(pe):
        with pe.Fori(0, repeats) as i:
            pe.wait_ge(staged, i * loads + loads)

            def score(u):
                pe.wait_ge(ready, after(i * count + (u - 2) if u >= 3 else i * count))
                query, key, first, blocks = units[u]
                k.nc.tensor.matmul(k.banks[:, u % 3, 0:blocks * P], query, key, start=True,
                                   stop=True).then_inc(scored, 1)

            def turn_probs(v):
                u = v * per + per - 1
                _, _, first, blocks = units[u]
                if per == 2:
                    pe.wait_ge(joined, after(i * outs + (v + 1)))
                    source = combined[v % 2]
                else:
                    pe.wait_ge(exped, after(i * count * exps + (u * exps + exps)))
                    source = probs[u % 3]
                pe.wait_ge(copied, after(i * outs + (v - 1) if v >= 2 else i * outs))
                for b in range(blocks):
                    mm = k.nc.tensor.transpose(k.banks[:, 3 + v % 2, b * P:(b + 1) * P], source[:, b * P:(b + 1) * P],
                                               k.const("ident"))
                mm.then_inc(turned_done, 1)

            def apply(v):
                u = v * per + per - 1
                _, _, first, blocks = units[u]
                pe.wait_ge(copied, after(i * outs + (v + 1)))
                pe.wait_ge(emptied, after(i * outs + (v - 1) if v >= 2 else i * outs))
                for b in range(blocks):
                    mm = k.nc.tensor.matmul(k.banks[:, 5 + v % 2, 0:value_cols], turned[v % 2][:, b * P:(b + 1) * P],
                                            value_of(i, u, first + b), start=b == 0, stop=b == blocks - 1)
                mm.then_inc(attended, 1)

            for step in range(0, count + 2 * per + lead + 1):
                if step < count:
                    score(step)
                behind = step - lead
                if behind >= 0 and behind % per == per - 1 and behind // per < outs:
                    turn_probs(behind // per)
                behind = step - lead - per
                if behind >= 0 and behind % per == per - 1 and behind // per < outs:
                    apply(behind // per)

    def vector(dve):
        v_ = k.nc.vector
        with dve.Fori(0, repeats) as i:
            dve.wait_ge(scored, after(i * count))
            for instruction in load(dve, i):
                instruction.then_inc(staged, 1)
            if prepare:
                dve.wait_ge(prepared, i * prepares + prepares)

            def biased(u):
                dve.wait_ge(scored, after(i * count + (u + 1)))
                dve.wait_ge(exped, after(i * count * exps + (u - 2) * exps if u >= 3 else i * count * exps))
                _, _, first, blocks = units[u]
                w = blocks * P
                s = u % 3
                v_.scalar_tensor_tensor(out=logits[s][:, 0:w], in0=k.banks[:, s, 0:w], scalar=scale,
                                        in1=bias_of(i, u, w), op0=ALU.mult, op1=ALU.add).then_inc(ready, 1)

            def maximum(u):
                s, w = u % 3, units[u][3] * P
                dve.wait_ge(ready, after(i * count + (u + 1)))
                v_.tensor_reduce(largest[:, s:s + 1], logits[s][:, 0:w], AX.X, ALU.max).then_inc(maxed, 1)

            def negate(u):
                s = u % 3
                dve.wait_ge(maxed, i * count + (u + 1))
                v_.tensor_scalar(shift[:, s:s + 1], largest[:, s:s + 1], sink_of(i, u) if sink_of else NEG, -1.0,
                                 ALU.max, ALU.mult).then_inc(shifted, 1)

            def invert(u, begin=True, end=True):
                s = u % 3
                base = i * (count * exps + (outs if per == 2 else 0))
                done = u * exps + (u // 2 if per == 2 else 0)
                if begin:
                    dve.wait_ge(exped, after(i * count * exps + (u * exps + exps)))
                    if sink_of:
                        v_.tensor_tensor(sum_all[:, s:s + 1], total[:, s:s + 1], sink_exp[:, s:s + 1],
                                         ALU.add).then_inc(order, 1)
                if not end:
                    return
                if sink_of:
                    dve.wait_ge(order, after(base + (done + 1)))
                denominator = sum_all if sink_of else total
                v_.reciprocal(inverse[:, u % 8:u % 8 + 1], denominator[:, s:s + 1]).then_inc(order, 1)

            def normalise(u):
                invert(u)
                s = u % 3
                base = i * (count + outs)
                done = u + u // 2 + 1
                dve.wait_ge(order, after(base + done))
                v = u // 2
                w = units[u][3] * P
                if u % 2 == 0:
                    dve.wait_ge(turned_done, after(i * outs + (v - 1) if v >= 2 else i * outs))
                    v_.tensor_scalar(combined[v % 2][:, 0:w], probs[s][:, 0:w], inverse[:, u % 8:u % 8 + 1], None,
                                     ALU.mult).then_inc(normed, 1)
                else:
                    v_.tensor_tensor(signed[:, s:s + 1], inverse[:, u % 8:u % 8 + 1], minus, ALU.mult).then_inc(order, 1)
                    dve.wait_ge(order, after(base + (done + 1)))
                    dve.wait_ge(normed, i * outs + (v + 1))
                    v_.scalar_tensor_tensor(out=combined[v % 2][:, 0:w], in0=probs[s][:, 0:w],
                                            scalar=signed[:, s:s + 1], in1=combined[v % 2][:, 0:w], op0=ALU.mult,
                                            op1=ALU.add).then_inc(joined, 1)

            def finish(v):
                u = v * per + per - 1
                dve.wait_ge(attended, after(i * outs + (v + 1)))
                bank = k.banks[:, 5 + v % 2, 0:value_cols]
                if per == 2:
                    v_.tensor_copy(out_of(i, u), bank).then_inc(emptied, 1)
                else:
                    v_.tensor_scalar(out_of(i, u), bank, inverse[:, u % 8:u % 8 + 1], None, ALU.mult).then_inc(emptied, 1)

            for step in range(0, count + 5):
                if step < count:
                    biased(step)
                if per == 1 and 0 <= step - 5 < count:
                    finish(step - 5)
                if step < count:
                    maximum(step)
                if per == 1 and 0 <= step - 2 < count:
                    invert(step - 2, end=False)
                if step < count:
                    negate(step)
                if per == 1 and 0 <= step - 2 < count:
                    invert(step - 2, begin=False)
                if per == 2 and step - 6 >= 0 and step % 2 == 0 and (step - 6) // 2 < outs:
                    finish((step - 6) // 2)
                if per == 2 and 0 <= step - 1 < count:
                    normalise(step - 1)
            if per == 2:
                for v in range(max(0, (count + 4 - 6) // 2 + 1), outs):
                    finish(v)

    def scalar(act):
        a = k.nc.scalar
        with act.Fori(0, repeats) as i:
            if prepare:
                act.wait_ge(ready, after(i * count))
                for instruction in prepare(act, i):
                    instruction.then_inc(prepared, 1)

            def exponent(u):
                act.wait_ge(shifted, i * count + (u + 1))
                if per == 2:
                    act.wait_ge(joined, after(i * outs + (u - 3) // 2 + 1 if u >= 3 else i * outs))
                else:
                    act.wait_ge(turned_done, after(i * outs + (u - 2) if u >= 3 else i * outs))
                    act.wait_ge(order, after((i * count + (u - 2)) * exps if u >= 3 else i * count * exps))
                _, _, first, blocks = units[u]
                w = blocks * P
                s = u % 3
                a.activation(probs[s][:, 0:w], logits[s][:, 0:w], ACT.Exp, bias=shift[:, s:s + 1],
                             accum_out=total[:, s:s + 1]).then_inc(exped, 1)
                if sink_of:
                    a.activation(sink_exp[:, s:s + 1], sink_of(i, u), ACT.Exp, bias=shift[:, s:s + 1]).then_inc(exped, 1)

            def copy(v):
                u = v * per + per - 1
                act.wait_ge(turned_done, after(i * outs + (v + 1)))
                act.wait_ge(attended, after(i * outs + (v - 1) if v >= 2 else i * outs))
                w = units[u][3] * P
                a.activation(turned[v % 2][:, 0:w], k.banks[:, 3 + v % 2, 0:w], ACT.Copy).then_inc(copied, 1)

            for step in range(0, count + 2 * per + lead + 1):
                if step < count:
                    exponent(step)
                behind = step - lead
                if behind >= 0 and behind % per == per - 1 and behind // per < outs:
                    copy(behind // per)

    return Stage(tensor, vector, scalar)


def bias_tables(k):
    spread = k.take(SW_HEADS * P)
    pitch = CONST_WIDTHS["bucket_rows"]
    rows = k.take(SW_HEADS * pitch).rearrange("p (h n) -> p h n", h=SW_HEADS)
    together = 4
    spread_done, made, copied, written = (k.sem("window_bias_" + s) for s in ("spread", "made", "copied", "written"))
    table = k.take(CH_HEADS * (2 * REL_CLIP + 1))
    chunk_pitch = TOKENS + P - 1
    chunk_rows = k.take(CH_HEADS * chunk_pitch)
    loaded, built = (k.sem("chunk_bias_" + s) for s in ("loaded", "built"))
    flat = TOKENS - 1 - REL_CLIP
    table3 = table.rearrange("p (h n) -> p h n", h=CH_HEADS)
    chunk_rows3 = chunk_rows.rearrange("p (h n) -> p h n", h=CH_HEADS)

    def vector(dve):
        v = k.nc.vector
        v.tensor_copy(spread[0:BUCKETS + 1, :].rearrange("p (h n) -> p h n", h=SW_HEADS),
                      k.column("rel_bias")[0:BUCKETS + 1, :].unsqueeze(2).broadcast_to([BUCKETS + 1, SW_HEADS, P])
                      ).then_inc(spread_done, 1)
        dve.wait_ge(loaded, 16)
        v.tensor_copy(chunk_rows3[:, :, 0:flat], table3[:, :, 0:1].broadcast_to([P, CH_HEADS, flat])).then_inc(built, 1)
        v.tensor_copy(chunk_rows3[:, :, flat:chunk_pitch], table3[:, :, 0:chunk_pitch - flat]).then_inc(built, 1)
        for h in range(SW_HEADS):
            dve.wait_ge(made, h + 1)
            v.tensor_copy(rows[:, h, :], k.banks[:, h % 4, 0:pitch]).then_inc(copied, 1)

    def tensor(pe):
        pe.wait_ge(spread_done, 1)
        for h in range(SW_HEADS):
            if h >= 4:
                pe.wait_ge(copied, h - 3)
            k.nc.tensor.matmul(k.banks[:, h % 4, 0:pitch], spread[0:BUCKETS + 1, h * P:(h + 1) * P],
                               k.const("bucket_rows")[0:BUCKETS + 1, :], start=True, stop=True).then_inc(made, 1)

    def scalar(act):
        act.dma_start(table, k.dram["chunk_table"]).then_inc(loaded, 16)
        act.wait_ge(built, 2)
        act.dma_start(k.dram["chunk_rows"].rearrange("h p u -> p h u"), chunk_rows3).then_inc(written, 16)
        for h in range(0, SW_HEADS, together):
            act.wait_ge(copied, h + together)
            act.dma_start(k.dram["window_rows"][h:h + together].rearrange("h p u -> p h u"),
                          rows[:, h:h + together, :]).then_inc(written, 16)
        act.wait_ge(written, 16 * (1 + SW_HEADS // together))

    return [Stage(tensor, vector, scalar)]


def skewed(dram, heads, pitch, columns):
    flat = dram.rearrange("h p u -> h (p u)")[:, P - 1:P - 1 + P * (pitch - 1)]
    return flat.rearrange("h (p u) -> p h u", u=pitch - 1)[:, :, 0:columns]


def mixer_c(k):
    heads = k.take(10 * 512)
    key_pairs = k.take(SW_KV * 512)
    values = k.take(BLOCKS * 256)
    with k.scope():
        hn = k.take_split(D_TILES)
        stages = [norm(k, "mix1_norm", "mix1", hn, meet=False),
                  projection(k, "c_heads", 10, D_TILES, hn, copy_into(k, heads)),
                  token_projection(k, "c_values", 1, hn, values, 256, meet=True)]
    out = k.take(BLOCKS * 1024)
    table = k.take(SW_HEADS * 256)
    q_heads, k_head = k.take(2 * 512), k.take(512)
    with k.scope():
        squares, total, deviation = k.take(2 * 512), k.take(2 * 512), k.take(2 * 512)
    squared, summed, rooted, inverted, table_in = (k.sem("qk_norm_" + s) for s in
                                                   ("squared", "summed", "rooted", "inverted", "table_in"))

    def norm_tensor(pe):
        for n in range(10):
            pe.wait_ge(squared, n + 1)
            if n >= 2:
                pe.wait_ge(rooted, n - 1)
            k.nc.tensor.matmul(k.banks[:, n % 2, :], k.const("head_pair"), squares[:, n % 2 * 512:n % 2 * 512 + 512],
                               start=True, stop=True).then_inc(summed, 1)

    def norm_vector(dve):
        v = k.nc.vector
        order = norm_order
        for n in range(10):
            s = slice(n % 2 * 512, n % 2 * 512 + 512)
            dve.wait_ge(rooted, n + 1)
            v.reciprocal(total[:, s], deviation[:, s]).then_inc(order, 1)
            dve.wait_ge(order, n + 1)
            tile = cut(heads, n * 512, 512)
            v.scalar_tensor_tensor(out=tile, in0=tile, scalar=k.column("q_norm" if n < 8 else "k_norm"), in1=total[:, s],
                                   op0=ALU.mult, op1=ALU.mult).then_inc(inverted, 1)

    norm_order = k.sem("qk_norm_order")
    paired = k.sem("qk_norm_keys_paired")

    def norm_scalar(act):
        a = k.nc.scalar
        act.dma_start(table.rearrange("p (h n) -> p h n", h=SW_HEADS),
                      skewed(k.dram["window_rows"], SW_HEADS, CONST_WIDTHS["bucket_rows"], 256)).then_inc(table_in, 16)
        for n in range(11):
            if n < 10:
                if n >= 2:
                    act.wait_ge(summed, n - 1)
                a.activation(squares[:, n % 2 * 512:n % 2 * 512 + 512], cut(heads, n * 512, 512),
                             ACT.Square).then_inc(squared, 1)
            if n >= 1:
                m = n - 1
                act.wait_ge(summed, m + 1)
                if m >= 2:
                    act.wait_ge(norm_order, m - 1)
                a.activation(deviation[:, m % 2 * 512:m % 2 * 512 + 512], k.banks[:, m % 2, :], ACT.Sqrt,
                             bias=k.const("eps"), scale=1.0 / 64).then_inc(rooted, 1)
        act.wait_ge(inverted, 10)
        for kv in range(SW_KV):
            rows = slice(64 * (kv % 2), 64 * (kv % 2) + 64)
            for half in range(2):
                a.activation(key_pairs[64 * half:64 * half + 64, kv * 512:(kv + 1) * 512],
                             heads[rows, (8 + kv // 2) * 512:(9 + kv // 2) * 512], ACT.Copy).then_inc(paired, 1)
        act.wait_ge(table_in, 16)

    units, which = [], []
    for tile in range(2):
        for half in range(2):
            for n in range(BLOCKS):
                rows = slice(64 * half, 64 * half + 64)
                first = max(n - 1, 0)
                units.append((q_heads[rows, tile * 512 + n * P:tile * 512 + (n + 1) * P],
                              k_head[rows, first * P:(n + 1) * P], first, n + 1 - first))
                which.append((2 * tile + half, n))

    def load(dve, i):
        if dve is None:
            return 2
        return [k.nc.vector.tensor_copy(q_heads, cut(heads, i * 1024, 1024)),
                k.nc.vector.tensor_copy(k_head, cut(key_pairs, i * 512, 512))]

    def value_of(i, u, block):
        return cut(values, i * 64 + block * 256, 64)

    def out_of(i, u):
        head, n = which[u]
        return cut(out, i * 256 + (n * 1024 + head * 64), 64)

    def bias_of(i, u, w):
        head, n = which[u]
        return cut(table, i * 1024 + (head * 256 + 256 - w), w)

    def sink_of(i, u):
        return k.column("sinks", i * 4 + which[u][0])

    with k.scope():
        attention = softmax_attention(k, "window", SW_KV, units, load, value_of, 64, out, out_of, bias_of,
                                      64 ** -0.5, 256, sink_of=sink_of)
    mixed = k.take_split(D_TILES)
    return stages + [
        Stage(norm_tensor, norm_vector, norm_scalar), attention,
        turn_split(k, "window_out", out, 1024, range(8), [mixed(n) for n in range(8)]),
        projection(k, "c_out", D_TILES, D_TILES, mixed, add_to_residual(k), engine="vector", meet=True)]


def branches(k):
    heads = k.take(24 * 512)
    attending = ExitStack()
    k.scopes.append(attending)
    values = k.take(BLOCKS * 1536)
    with k.scope():
        hn = k.take_split(D_TILES)
        stages = [norm(k, "norm1", "norm1", hn, meet=False),
                  projection(k, "in_heads", 24, D_TILES, hn, copy_into(k, heads)),
                  token_projection(k, "in_values", 6, hn, values, 1536, meet=True)]
    out_d = k.take(BLOCKS * 1024)
    q_head, k_head, bias = k.take(2 * 512), k.take(2 * 512), k.take(2 * 512)
    minus = k.take(8)
    qd, kd, qc, kc = heads[:, 0:4096], heads[:, 4096:8192], heads[:, 8192:10240], heads[:, 10240:12288]
    with k.scope():
        temp = k.take(64)
    made, exped = k.sem("lambda_made"), k.sem("lambda_exped")
    lambdas = k.column("lambdas")

    def lambda_vector(dve):
        v = k.nc.vector
        for n in range(2):
            v.tensor_tensor(temp, lambdas[:, 128 * n:128 * n + 64], lambdas[:, 128 * n + 64:128 * n + 128],
                            ALU.mult).then_inc(made, 1)
            dve.wait_ge(made, 2 * n + 1)
            v.tensor_reduce(minus[:, 1 + n:2 + n], temp, AX.X, ALU.add).then_inc(made, 1)
            dve.wait_ge(made, 2 * n + 2)
        dve.wait_ge(exped, 1)
        v.tensor_tensor(minus[:, 5:6], minus[:, 4:5], minus[:, 3:4], ALU.subtract).then_inc(made, 1)
        dve.wait_ge(made, 5)
        v.tensor_scalar(minus[:, 0:1], minus[:, 5:6], -LAM_INIT, None, ALU.add)

    def lambda_scalar(act):
        act.wait_ge(made, 4)
        k.nc.scalar.activation(minus[:, 3:5], minus[:, 1:3], ACT.Exp).then_inc(exped, 1)

    stages.append(Stage(vector=lambda_vector, scalar=lambda_scalar))

    units, which_d = [], []
    for head in range(2):
        for n in range(BLOCKS):
            for half in range(2):
                rows = slice(64 * half, 64 * half + 64)
                units.append((q_head[rows, head * 512 + n * P:head * 512 + (n + 1) * P],
                              k_head[rows, head * 512:head * 512 + (n + 1) * P], 0, n + 1))
                which_d.append((head, n))

    def load_d(dve, i):
        if dve is None:
            return 2
        return [k.nc.vector.tensor_copy(q_head, cut(qd, i * 1024, 1024)),
                k.nc.vector.tensor_copy(k_head, cut(kd, i * 1024, 1024))]

    def slope(act, i):
        return [k.nc.scalar.activation(cut(bias, n * 512, 512), k.const("distance"), ACT.Copy,
                                       scale=cut(k.const("slopes"), i * 2 + n, 1)) for n in range(2)]

    with k.scope():
        stages.append(softmax_attention(
            k, "diff", DIFF_HEADS // 2, units, load_d,
            lambda i, u, b: cut(values, i * 2 * P + (which_d[u][0] * P + b * 1536), P), P, out_d,
            lambda i, u: cut(out_d, i * 2 * P + (which_d[u][0] * P + which_d[u][1] * 1024), P),
            lambda i, u, w: bias[:, (which_d[u][0] + 1) * 512 - w:(which_d[u][0] + 1) * 512], 64 ** -0.5,
            512, prepare=slope, prepares=2, minus=minus[:, 0:1]))

    squares = kd
    with k.scope():
        small = k.take(96)
    mixed_d = heads[:, 0:4096]

    def gained(act, bank, n):
        return k.nc.scalar.activation(cut(mixed_d, n * 512, 512), bank, ACT.Copy, scale=k.column("subln", 0))

    stages += [token_norm(k, "diff_norm", out_d, 32, P, squares, small, 1.0 - LAM_INIT),
               turn(k, "diff_out", out_d, 1024, range(8), gained)]

    table = kd
    out_c = out_d[:, 0:BLOCKS * 512]
    table_in, masked = k.sem("chunk_table_in"), k.sem("chunk_table_masked")

    def table_scalar(act):
        act.dma_start(table.rearrange("p (h n) -> p h n", h=CH_HEADS),
                      skewed(k.dram["chunk_rows"], CH_HEADS, TOKENS + P - 1, TOKENS)).then_inc(table_in, 16)

    def table_vector(dve):
        dve.wait_ge(table_in, 16)
        k.nc.vector.memset(table.rearrange("p (h n) -> p h n", h=CH_HEADS)[0:64, :, 448:512], NEG)

    stages.append(Stage(vector=table_vector, scalar=table_scalar))
    units_c, which = [], []
    for head in range(4):
        rows, pair = slice(64 * (head % 2), 64 * (head % 2) + 64), head // 2 * 512
        for n in range(BLOCKS):
            units_c.append((q_head[rows, pair + n * P:pair + (n + 1) * P], k_head[rows, pair:pair + (n + 1) * P],
                            0, n + 1))
            which.append((head, n))

    def load_c(dve, i):
        if dve is None:
            return 2
        return [k.nc.vector.tensor_copy(q_head, cut(qc, i * 1024, 1024)),
                k.nc.vector.tensor_copy(k_head, cut(kc, i * 1024, 1024))]

    with k.scope():
        stages.append(softmax_attention(
            k, "chunk", CH_HEADS // 4, units_c, load_c,
            lambda i, u, b: cut(values, i * 2 * P + (b * 1536 + 1024 + which[u][0] * 64), 64), 64, out_c,
            lambda i, u: cut(out_c, i * 2 * P + (which[u][1] * 512 + which[u][0] * 64), 64),
            lambda i, u, w: cut(table, i * 2048 + (which[u][0] * 512 + 512 - w), w), 64 ** -0.5,
            512))
    mixed_c = heads[:, 8192:10240]
    stages.append(turn(k, "chunk_out", out_c, 512, range(4), feature_copy(k, mixed_c)))

    attending.close()
    k.scopes.pop()

    operand = k.take_split(D_TILES)
    norm_again = norm(k, "norm1_again", "norm1", operand, meet=False)
    gates, product = k.take(2 * 4096), k.take(512)
    merged = kd

    def gate(offset):
        return lambda act, bank, tile: k.nc.scalar.activation(cut(gates, (tile + offset) * 512, 512), bank,
                                                              ACT.Sigmoid, bias=k.column("b_gate", tile + offset))

    def first(dve, bank, tile):
        return k.nc.vector.tensor_tensor(cut(merged, tile * 512, 512), bank, cut(gates, tile * 512, 512), ALU.mult)

    order = k.sem("merge_order")

    def second(dve, bank, tile):
        if tile:
            dve.wait_ge(order, 2 * tile)
        k.nc.vector.tensor_tensor(product, bank, cut(gates, (tile + 8) * 512, 512), ALU.mult).then_inc(order, 1)
        dve.wait_ge(order, 2 * tile + 1)
        m = cut(merged, tile * 512, 512)
        k.nc.vector.tensor_tensor(m, product, m, ALU.add).then_inc(order, 1)
        return dve.drain()

    chunk_operand = Split(operand.memory, 4)
    stages += [norm_again,
               projection(k, "gate_d", 8, 8, operand, gate(0)),
               projection(k, "gate_c", 8, 8, operand, gate(8), banks=(4, 5, 6, 7), meet=True),
               split_stage(k, "branch_d_operand", mixed_d, 8, operand),
               projection(k, "branch_d", 8, 8, operand, first, engine="vector", meet=True),
               split_stage(k, "branch_c_operand", mixed_c, 4, chunk_operand),
               projection(k, "branch_c", 8, 4, chunk_operand, second, engine="vector", meet=True),
               split_stage(k, "out_operand", merged, 8, operand),
               projection(k, "out", 8, 8, operand, add_to_residual(k), engine="vector", meet=True)]
    return stages


def routing(k, queries, key_table, turned, units):
    pairs = ROUTING_PAIRS
    lists = 2 * PEER_HEADS
    q_block = k.take(D_TILES * P)
    scores = [k.take(lists * P), k.take(lists * P)]
    best = k.take(lists * TOPK)
    index, index_f = k.take(lists * TOPK), k.take(lists * TOPK)
    sums = [k.take(PEER_HEADS * TOPK * TOPK) for _ in range(2)]
    picked = k.take(PEER_HEADS * TOPK)
    pick, row_col, row_col_f = k.take(P), k.take(2 * P), k.take(2 * P)
    match, product = k.take(2048), k.take(2048)
    chosen = k.take(3 * P)
    shifted, exped_s, total, inverse = k.take(P), k.take(P), k.take(8), k.take(8)
    (loaded, staged, scored, copied, order, exp_in, exp_out, ready, turned_up, emptied) = (
        (k.sem_from_one if s in ("scored", "chosen", "copied", "emptied", "turned") else k.sem)("route_" + s) for s in (
        "keys_in", "staged", "scored", "copied", "order", "to_exp", "exped", "chosen", "turned", "emptied"))
    best4 = best.rearrange("p (s h r) -> p h s r", h=PEER_HEADS, s=2)
    index4 = index_f.rearrange("p (s h r) -> p h s r", h=PEER_HEADS, s=2)
    quad = [P, PEER_HEADS, TOPK, TOPK]

    def scalar(act):
        a = k.nc.scalar
        units.start(act)
        act.dma_start(key_table, k.dram["peer_keys"]).then_inc(loaded, 16)
        with act.Fori(0, BLOCKS) as b:
            act.wait_ge(scored, after(b))
            a.activation(q_block.rearrange("p (h t) -> p h t", h=D_TILES),
                         queries.rearrange("p (h t) -> p h t", h=D_TILES)[:, :, bass.ds(b * P, P)],
                         ACT.Copy).then_inc(staged, 1)
            act.wait_ge(scored, after(b + 1))
            act.wait_ge(ready, after(b))
            for n in range(4):
                a.activation(scores[0][:, n * 512:(n + 1) * 512], k.banks[:, n, :], ACT.Copy).then_inc(copied, 1)
            with act.Fori(0, pairs - 1) as pair:
                for q in range(RING):
                    units.activate(act, b * pairs + pair, q)
            act.wait_ge(exp_in, b + 1)
            a.activation(exped_s, shifted, ACT.Exp).then_inc(exp_out, 1)
            for q in range(RING):
                units.activate(act, b * pairs + (pairs - 1), q)
            act.wait_ge(turned_up, after(b + 1))
            for n in range(3):
                a.activation(cut(turned, b * P + n * 512, P), k.banks[:, 4, n * P:(n + 1) * P],
                             ACT.Copy).then_inc(emptied, 1)

    def tensor(pe):
        pe.wait_ge(loaded, 16)
        with pe.Fori(0, BLOCKS) as b:
            pe.wait_ge(staged, b + 1)
            pe.wait_ge(copied, after(b * 4))
            for h in range(PEER_HEADS):
                for s in range(2):
                    rows = slice(64 * s, 64 * s + 64)
                    mm = k.nc.tensor.matmul(k.banks[:, 2 * s + h // 4, h % 4 * P:(h % 4 + 1) * P],
                                            q_block[rows, h * P:(h + 1) * P], key_table[rows, h * P:(h + 1) * P],
                                            start=True, stop=True)
            mm.then_inc(scored, 1)
            with pe.Fori(0, pairs) as pair:
                for q in range(RING):
                    units.product(pe, b * pairs + pair, q)
            pe.wait_ge(ready, after(b + 1))
            pe.wait_ge(emptied, after(b * 3))
            for n in range(3):
                mm = k.nc.tensor.transpose(k.banks[:, 4, n * P:(n + 1) * P], chosen[:, n * P:(n + 1) * P],
                                           k.const("ident"))
            mm.then_inc(turned_up, 1)

    def vector(dve):
        v = k.nc.vector
        steps = 19

        with dve.Fori(0, BLOCKS) as b:
            done = [0]

            def then(instruction):
                done[0] += 1
                instruction.then_inc(order, 1)
                dve.wait_ge(order, b * steps + done[0])
                k.hold(dve)

            def ranked(count, width, values, spare, top, where):
                def of(memory, n, size):
                    return memory[:, n * size:(n + 1) * size]
                for n in range(count):
                    last = v.max(of(top, n, TOPK)[:, 0:8], of(values, n, width))
                then(last)
                for n in range(count):
                    v.max_index(of(where, n, TOPK)[:, 0:8].bitcast(U32), of(top, n, TOPK)[:, 0:8], of(values, n, width))
                    last = v.match_replace(of(spare, n, width), of(top, n, TOPK)[:, 0:8], of(values, n, width), -3e38)
                then(last)
                for n in range(count):
                    last = v.max(of(top, n, TOPK)[:, 8:16], of(spare, n, width))
                then(last)
                for n in range(count):
                    last = v.max_index(of(where, n, TOPK)[:, 8:16].bitcast(U32), of(top, n, TOPK)[:, 8:16],
                                       of(spare, n, width))
                then(last)

            dve.wait_ge(copied, after(b * 4 + 4))
            k.hold(dve)
            ranked(lists, P, scores[0], scores[1], best, index)
            then(v.tensor_copy(index_f, index.bitcast(U32)))
            then(v.tensor_tensor(sums[0].rearrange("p (h r c) -> p h r c", h=PEER_HEADS, r=TOPK),
                                 best4[:, :, 0, :].unsqueeze(3).broadcast_to(quad),
                                 best4[:, :, 1, :].unsqueeze(2).broadcast_to(quad), ALU.add))
            ranked(PEER_HEADS, TOPK * TOPK, sums[0], sums[1], picked, pick)
            v.tensor_scalar(row_col[:, 0:P].bitcast(U32), pick.bitcast(U32), 4, None, ALU.logical_shift_right)
            then(v.tensor_scalar(row_col[:, P:2 * P].bitcast(U32), pick.bitcast(U32), 15, None, ALU.bitwise_and))
            then(v.tensor_copy(row_col_f, row_col.bitcast(U32)))
            dve.wait_ge(turned_up, after(b))
            for s in range(2):
                rank = row_col_f[:, s * P:(s + 1) * P].rearrange("p (h r) -> p h r", h=PEER_HEADS)
                ranks = k.const("iota")[:, 0:TOPK].unsqueeze(1).unsqueeze(1).broadcast_to(quad)
                m4 = match.rearrange("p (h r c) -> p h r c", h=PEER_HEADS, r=TOPK)
                p4 = product.rearrange("p (h r c) -> p h r c", h=PEER_HEADS, r=TOPK)
                then(v.tensor_tensor(m4, rank.unsqueeze(3).broadcast_to(quad), ranks, ALU.is_equal))
                then(v.tensor_tensor(p4, m4, index4[:, :, s, :].unsqueeze(2).broadcast_to(quad), ALU.mult))
                last = v.tensor_reduce(chosen[:, s * P:(s + 1) * P], product.rearrange("p (n c) -> p n c", c=TOPK),
                                       AX.X, ALU.add)
            then(last)
            picked3 = picked.rearrange("p (h r) -> p h r", h=PEER_HEADS)
            by_head = [P, PEER_HEADS, TOPK]
            v.tensor_tensor(shifted.rearrange("p (h r) -> p h r", h=PEER_HEADS), picked3,
                            picked3[:, :, 0:1].broadcast_to(by_head), ALU.subtract).then_inc(exp_in, 1)
            dve.wait_ge(exp_out, b + 1)
            exps = exped_s.rearrange("p (h r) -> p h r", h=PEER_HEADS)
            then(v.tensor_reduce(total, exps, AX.X, ALU.add))
            then(v.reciprocal(inverse, total))
            v.tensor_tensor(chosen[:, 2 * P:3 * P].rearrange("p (h r) -> p h r", h=PEER_HEADS), exps,
                            inverse.unsqueeze(2).broadcast_to(by_head), ALU.mult).then_inc(ready, 1)
            assert done[0] == steps, done[0]

    return Stage(tensor, vector, scalar)


def routing_matrix(k, turned, units):
    batch = 4
    depth = 4
    rows = [k.take(batch * P) for _ in range(depth)]
    cols = [k.take(batch * P) for _ in range(depth)]
    staging = k.take(P * CHUNK_TOKENS)
    (rows_ready, cols_ready, made, emptied, stored) = (
        (k.sem_from_one if s in ("made", "stored") else k.sem)("matrix_" + s) for s in (
        "rows", "columns", "made", "emptied", "stored"))
    per_chunk = CHUNK_TOKENS // batch
    halves = per_chunk // (RING * depth)
    choice_i, choice_j, weight = (turned[:, n * 512:(n + 1) * 512] for n in range(3))
    three = [P, batch, P]
    before = BLOCKS * ROUTING_PAIRS

    def vector(dve):
        dve.sem_inc(made, depth - 1)
        with dve.Fori(0, CHUNKS * per_chunk // depth) as four:
            for p in range(depth):
                base = four * depth + p
                dve.wait_ge(made, after(base))
                for t in range(batch):
                    at = four * (depth * batch) + (p * batch + t)
                    last = k.nc.vector.tensor_scalar(rows[p][:, t * P:(t + 1) * P], k.const("iota"),
                                                     cut(choice_i, at, 1), cut(weight, at, 1), ALU.is_equal, ALU.mult)
                last.then_inc(rows_ready, 1)
                k.nc.vector.tensor_tensor(cols[p].rearrange("p (t n) -> p t n", t=batch),
                                          k.const("iota").unsqueeze(1).broadcast_to(three),
                                          cut(choice_j, four * (depth * batch) + p * batch, batch).unsqueeze(
                                              2).broadcast_to(three), ALU.is_equal).then_inc(cols_ready, 1)

    def tensor(pe):
        with pe.Fori(0, CHUNKS * halves) as pair:
            for q in range(RING):
                units.product(pe, pair + before, q)
                for p in range(depth):
                    base = pair * (RING * depth) + (q * depth + p)
                    pe.wait_ge(rows_ready, base + 1)
                    pe.wait_ge(cols_ready, base + 1)
                    pe.wait_ge(emptied, base + 1)
                    for t in range(batch):
                        s = slice(t * P, (t + 1) * P)
                        mm = k.nc.tensor.matmul(k.banks[:, p, s], rows[p][:, s], cols[p][:, s], start=True, stop=True)
                    mm.then_inc(made, 1)

    def scalar(act):
        act.sem_inc(emptied, depth)
        by_token = staging.rearrange("p (j t) -> p t j", t=CHUNK_TOKENS)

        with act.Fori(0, CHUNKS) as chunk:
            with act.Fori(0, halves) as half:
                for q in range(RING):
                    units.activate(act, chunk * halves + half + before, q)
                    act.wait_ge(stored, after(chunk * 16))
                    for p in range(depth):
                        base = half * (RING * depth) + (q * depth + p)
                        act.wait_ge(made, after(chunk * per_chunk + base + depth))
                        k.nc.scalar.activation(by_token[:, bass.ds(half * (RING * depth * batch)
                                                                   + (q * depth + p) * batch, batch), :],
                                               k.banks[:, p, :].rearrange("p (t n) -> p t n", t=batch),
                                               ACT.Copy).then_inc(emptied, 1)
            act.wait_ge(emptied, chunk * per_chunk + (per_chunk + depth))
            act.dma_start(k.dram["routing"][bass.ds(chunk, 1)].rearrange("c p j t -> (c p) (j t)"),
                          staging).then_inc(stored, 16)
        act.wait_ge(stored, after(CHUNKS * 16))

    return Stage(tensor, vector, scalar)


class HiddenUnits:

    def __init__(self, k, hn, buffers):
        self.k, self.hn, self.buffers = k, hn, buffers
        self.first = k.take_slots(PEER_KEYS // 2)
        self.filled, self.activated = k.sem("hidden_filled"), k.sem("hidden_activated")
        self.written = [k.sem_from_one(f"hidden_written_{q}") for q in range(RING)]

    def product(self, pe, pair, q):
        k = self.k
        place = (self.first + q) % RING
        k.slot_begins(pe, place, pair + (self.first + q) // RING)
        for n in range(2):
            pe.wait_ge(self.activated, pair * 4 + (2 * q + n + 1))
            for kk in range(D_TILES):
                begun, last = split_product(k, k.banks[:, 6 + n, :], k.tile(place, n * D_TILES + kk), self.hn(kk),
                                            kk == 0, kk == D_TILES - 1)
                if n == 0 and kk == 0:
                    k.release_previous(begun, place)
            last.then_inc(self.filled, 1)

    def start(self, act):
        act.sem_inc(self.activated, 2)

    def activate(self, act, pair, q):
        k = self.k
        act.wait_ge(self.written[q], after(pair * 16))
        for n in range(2):
            act.wait_ge(self.filled, pair * 4 + (2 * q + n + 1))
            k.nc.scalar.activation(self.buffers[q][:, n * TOKENS:(n + 1) * TOKENS], k.banks[:, 6 + n, :],
                                   ACT.Gelu).then_inc(self.activated, 1)
        act.wait_ge(self.activated, pair * 4 + (2 * q + 4))
        act.dma_start(k.dram["hidden"][bass.ds(pair * RING + q, 1)].rearrange("s p n -> (s p) n"),
                      self.buffers[q]).then_inc(self.written[q], 16)


def experts(k, units):
    gates = [k.take(GROUP * TOKENS) for _ in range(2)]
    loaded = [k.take(GROUP * TOKENS) for _ in range(2)]
    gated = k.take(2 * TOKENS)
    operand = k.take_split(4)
    before, pairs = BLOCKS * ROUTING_PAIRS + MATRIX_PAIRS, PEER_KEYS // 4
    (group_in, multiplied, high_made, ready, used, out_filled) = (
        (k.sem_from_one if s == "ready" else k.sem)("experts_" + s) for s in (
            "group_in", "multiplied", "high_made", "ready", "used", "out_filled"))
    group_in = [group_in, k.sem("experts_group_in_1")]
    collected = collect(k, PEER_KEYS // 2, lambda slot, kk, at: operand((2 * at + kk) % 4), out_filled,
                        ready=lambda pe, slot, kk: pe.wait_ge(ready, after(slot * 2 + (kk + 1))), used=used)

    def tensor(pe):
        with pe.Fori(before, pairs) as pair:
            for q in range(RING):
                units.product(pe, pair, q)
        for n in range(2):
            pe.wait_ge(units.activated, 2 * 2 * pairs + (n + 1))
        collected(pe)

    def vector(dve):
        v = k.nc.vector

        def low(p, e, tile):
            dve.wait_ge(high_made, tile + 1)
            v.tensor_tensor(operand.low(e % 4), gated[:, e % 2 * 512:e % 2 * 512 + 512],
                            operand.high(e % 4).bitcast(F32), ALU.subtract).then_inc(ready, 1)
            dve.wait_ge(ready, after(tile + 1))

        with dve.Fori(0, GROUPS // 2) as r:
            for p in range(2):
                dve.wait_ge(group_in[p], r * 32 + 32)
                gate = gates[p].rearrange("p (c j t) -> p c j t", c=CHUNKS, j=GROUP)
                for e in range(GROUP + 1):
                    tile = r * (2 * GROUP) + (p * GROUP + e)
                    if e < GROUP:
                        v.tensor_tensor(gated[:, e % 2 * 512:e % 2 * 512 + 512].rearrange("p (c t) -> p c t", c=CHUNKS),
                                        loaded[p][:, e * 512:(e + 1) * 512].rearrange("p (c t) -> p c t", c=CHUNKS),
                                        gate[:, :, e, :], ALU.mult).then_inc(multiplied, 1)
                    if e >= 1:
                        low(p, e - 1, r * (2 * GROUP) + (p * GROUP + e - 1))
        for n in range(D_TILES):
            dve.wait_ge(out_filled, n + 1)
            add_to_residual(k)(dve, k.banks[:, n, :], n)

    def scalar(act):
        def load(p, group):
            act.dma_start(gates[p].rearrange("p (c n) -> p c n", c=CHUNKS),
                          k.dram["routing"].rearrange("c p j t -> p c (j t)")[
                              :, :, bass.ds(group * (GROUP * CHUNK_TOKENS), GROUP * CHUNK_TOKENS)]
                          ).then_inc(group_in[p], 16)
            act.dma_start(loaded[p].rearrange("p (s n) -> p s n", s=GROUP // 2),
                          k.dram["hidden"].rearrange("s p n -> p s n")[:, bass.ds(group * (GROUP // 2), GROUP // 2), :]
                          ).then_inc(group_in[p], 16)

        def groups(r, more):
            for p in range(2):
                for e in range(GROUP):
                    tile = r * (2 * GROUP) + (p * GROUP + e)
                    act.wait_ge(multiplied, tile + 1)
                    act.wait_ge(used, tile + 1)
                    k.nc.scalar.activation(operand.high(e % 4), gated[:, e % 2 * 512:e % 2 * 512 + 512],
                                           ACT.Copy).then_inc(high_made, 1)
                if more:
                    load(p, r * 2 + (p + 2))

        act.sem_inc(used, 4)
        for q in range(RING):
            act.wait_ge(units.written[q], after(before * 16))
        load(0, 0)
        load(1, 1)
        with act.Fori(before, pairs) as pair:
            for q in range(RING):
                units.activate(act, pair, q)
        for q in range(RING):
            act.wait_ge(units.written[q], after(pairs * 16))
        with act.Fori(0, GROUPS // 2 - 1) as r:
            groups(r, True)
        groups(GROUPS // 2 - 1, False)

    return Stage(tensor, vector, scalar)


def expert_layer(k):
    hn = k.take_split(D_TILES)
    buffers = [k.take(2 * TOKENS) for _ in range(RING)]
    with k.scope():
        turned = k.take(3 * 512)
        with k.scope():
            queries, key_table = k.take(8 * 512), k.take(8 * P)
            stages = [norm(k, "norm2", "norm2", hn, meet=False),
                      projection(k, "peer_queries", 8, 8, hn, copy_into(k, queries), meet=True)]
            units = HiddenUnits(k, hn, buffers)
            stages.append(routing(k, queries, key_table, turned, units))
        stages.append(routing_matrix(k, turned, units))
    return stages + [experts(k, units)]


def last_norm(k):
    out = k.take(8 * 512)
    return [norm(k, "final_norm", "final", out), store(k, out)]


def load_inputs(k):
    def scalar(act):
        act.dma_start(k.consts[:, :], k.dram["consts"]).then_inc(k.inputs_in, 16)
        act.dma_start(k.columns[:, :], k.dram["columns"]).then_inc(k.inputs_in, 16)
        act.dma_start(k.h[:, :], k.dram["x"]).then_inc(k.inputs_in, 16)
        act.wait_ge(k.inputs_in, 48)
    return Stage(scalar=scalar)


def store(k, source):
    stored = k.sem("stored")

    def scalar(act):
        act.dma_start(k.dram["out"], source).then_inc(stored, 16)
        act.wait_ge(stored, 16)
    return Stage(scalar=scalar)


def program(nc, dram, stop=None):
    ctx = ExitStack()
    with ctx:
        k = Core(nc, ctx, dram)
        periods = [
            lambda: [load_inputs(k)], lambda: bias_tables(k),
            lambda: mixer_ab(k), lambda: feed_forward(k, 0), lambda: layer_embedding(k, 0),
            lambda: mixer_c(k), lambda: feed_forward(k, 1), lambda: layer_embedding(k, 1),
            lambda: branches(k), lambda: expert_layer(k)]
        if stop is not None:
            periods = periods[:stop] + [lambda: [store(k, k.h[:, :])]]
        else:
            periods += [lambda: last_norm(k)]
        stages = k.plan(periods)

        def run(eng, which):
            met = 0
            for stage in stages:
                part = {"tensor": stage.tensor, "vector": stage.vector, "scalar": stage.scalar}[which]
                if part:
                    part(eng)
                if stage.meet:
                    eng.drain().then_inc(k.meetings, 1)
                    met += 1
                    eng.wait_ge(k.meetings, 3 * met)

        block = ctx.enter_context(nc.Block())

        @block.sync
        def _(sp):
            def load(place, slot, turn):
                if turn is not None:
                    sp.wait_ge(k.weights_ready[place], turn)
                sp.dma_start(k.raw[:, place * SLOT:(place + 1) * SLOT],
                             dram["weights"][bass.ds(slot, 1)].rearrange("s p n -> (s p) n")
                             ).then_inc(k.raw_in[place], 16)
            for place in range(RING):
                load(place, place, None)
            with sp.Fori(1, k.slots // RING) as turn:
                for place in range(RING):
                    load(place, turn * RING + place, turn)
            for place in range(k.slots % RING):
                load(place, k.slots - 1, k.slots // RING)

        @block.gpsimd
        def _(pool):
            def split(place, turn):
                raw = k.raw[:, place * SLOT:(place + 1) * SLOT]
                high = k.ring[:, place * 2 * SLOT:place * 2 * SLOT + SLOT]
                low = k.ring[:, place * 2 * SLOT + SLOT:(place + 1) * 2 * SLOT]
                pool.wait_ge(k.raw_in[place], turn * 16 + 16)
                pool.wait_ge(k.weights_used[place], turn + 1)
                k.hold(pool)
                k.nc.gpsimd.tensor_scalar(high, raw, 1.0, 1.0, ALU.mult, ALU.mult).then_inc(k.high_made, 1)
                pool.wait_ge(k.high_made, turn * RING + (place + 1))
                k.nc.gpsimd.tensor_tensor(low, raw, high.bitcast(F32), ALU.subtract).then_inc(k.weights_ready[place], 1)
            with pool.Fori(0, k.slots // RING) as turn:
                for place in range(RING):
                    split(place, turn)
            for place in range(k.slots % RING):
                split(place, k.slots // RING)

        @block.tensor
        def _(pe):
            for place in range(RING - 1):
                pe.sem_inc(k.weights_used[place], 1)
            run(pe, "tensor")

        @block.vector
        def _(dve):
            run(dve, "vector")

        @block.scalar
        def _(act):
            run(act, "scalar")
    return k


def weight_stream(a):
    def feature(w, ktiles):
        k_in, n_out = w.shape
        t = w.reshape(ktiles, P, n_out // P, P).transpose(2, 0, 1, 3).reshape(-1, P, P)
        return t

    def paired(w):
        t = feature(w, D_TILES).reshape(2, FF_TILES, D_TILES, P, P)
        return t.transpose(1, 0, 2, 3, 4).reshape(-1, P, P)

    def rows_first(w):
        return w.reshape(-1, P, D_TILES, P).transpose(0, 2, 1, 3).reshape(-1, P, P)

    ab, c, w2 = a["ab_w_in"][0], a["c_w_in"][0], a["w_in_2"][0]
    parts = [ab[:, n * 512:(n + 1) * 512] for n in range(7)]
    tiles = [feature(parts[n], 8) for n in (0, 1, 3, 4, 6, 2, 5)]
    tiles += [feature(a["ab_w_out"][0], 8)]

    def layer_rest(i):
        return [paired(a["ffn_up"][i]), rows_first(a["ffn_down"][i]), feature(a["ple_gate"][i], 8),
                feature(a["ple_proj"][i], 2)]
    tiles += layer_rest(0)
    tiles += [feature(c, 8), feature(a["c_w_out"][0], 8)] + layer_rest(1)
    qd, kd, vd, qc, kc, vc, gd, gc = np.split(w2, np.cumsum([1024] * 3 + [512] * 3 + [1024] * 2)[:-1], axis=1)
    tiles += [feature(w, 8) for w in (qd, kd, qc, kc, vd, vc, gd, gc)]
    tiles += [feature(a["w_branch_diff_2"][0], 8), feature(a["w_branch_chunk_2"][0], 4),
              feature(a["w_out_2"][0], 8), feature(a["peer_wq_2"][0], 8)]
    u = a["peer_u_2"][0].reshape(P, P, D_TILES, P).transpose(1, 2, 3, 0)
    v = a["peer_v_2"][0].reshape(P, P, D_TILES, P).transpose(1, 2, 0, 3)
    tiles += [u.reshape(-1, P, P), v.reshape(-1, P, P)]
    stream = np.concatenate(tiles)
    return np.ascontiguousarray(stream.reshape(-1, SLOT_TILES, P, P).transpose(0, 2, 1, 3)).reshape(-1, P, SLOT)


def column_array(a):
    def down(v):
        return v.reshape(-1, P).T

    def rows(v):
        return np.broadcast_to(v.reshape(1, -1), (P, v.size))
    c = {}
    for i in range(2):
        c[f"mix{i}"], c[f"ffn{i}"], c[f"ple{i}"] = (down(a[n][i]) for n in ("mix_norm", "ffn_norm", "ple_norm"))
        c[f"conv{i}"], c[f"conv_b{i}"] = down(a["ffn_conv"][i]), down(a["ffn_conv_b"][i])
    c["norm1"], c["norm2"], c["final"] = down(a["norm1_w_2"][0]), down(a["norm2_w_2"][0]), down(a["final_norm_w_2"])
    c["hg_norm"], c["subln"], c["lb"] = down(a["hg_out_norm"][0]), down(a["diff_subln_w_2"][0]), down(a["hg_lb_logits"][0])
    c["q_norm"], c["k_norm"] = (np.concatenate([a[n][0]] * 2)[:, None] for n in ("q_norm", "k_norm"))
    c["b_gate"], c["sinks"] = down(a["b_gate_2"][0]), rows(a["sinks"][0])
    c["lambdas"] = rows(np.concatenate([a[n][0] for n in ("diff_lq1_2", "diff_lk1_2", "diff_lq2_2", "diff_lk2_2")]))
    c["rel_bias"] = np.concatenate([a["rel_bias"], np.ones((P - BUCKETS, SW_HEADS), np.float32)])
    out = np.concatenate([c[n] for n in COLUMN_WIDTHS], axis=1)
    assert out.shape == (P, COLUMN_N)
    return np.ascontiguousarray(out)


def feature_major(x, tiles):
    return np.ascontiguousarray(x.reshape(TOKENS, tiles, P).transpose(2, 1, 0)).reshape(P, tiles * TOKENS)


def host_arrays(a):
    keys = a["peer_keys_2"][0].transpose(1, 3, 0, 2).reshape(P, PEER_HEADS * PEER_KEYS)
    table = a["chunk_rel_bias_2"][0][:, ::-1].reshape(1, -1)
    return {"x": feature_major(a["x"][0], D_TILES), "consts": constants(), "columns": column_array(a),
            "weights": weight_stream(a), "peer_keys": np.ascontiguousarray(keys),
            "p": np.stack([feature_major(a["p"][i, 0], PLE_TILES).reshape(P, PLE_TILES, TOKENS) for i in range(2)]),
            "chunk_table": np.ascontiguousarray(np.broadcast_to(table, (P, table.size)))}


def build(nc, shapes, stop=None):
    dram = {n: nc.dram_tensor(f"in_{n}", s, F32, kind="ExternalInput").ap() for n, s in shapes.items()}
    dram["out"] = nc.dram_tensor("out_0", (P, D_TILES * TOKENS), F32, kind="ExternalOutput").ap()
    dram["window_rows"] = nc.dram_tensor("window_rows", (SW_HEADS, P, CONST_WIDTHS["bucket_rows"]), F32).ap()
    dram["chunk_rows"] = nc.dram_tensor("chunk_rows", (CH_HEADS, P, TOKENS + P - 1), F32).ap()
    dram["hidden"] = nc.dram_tensor("hidden", (PEER_KEYS // 2, P, 2 * TOKENS), F32).ap()
    dram["routing"] = nc.dram_tensor("routing", (CHUNKS, P, PEER_KEYS, CHUNK_TOKENS), F32).ap()
    program(nc, dram, stop)


def kernel(**inputs):
    import concourse.bacc as bacc
    from concourse.bass_utils import run_bass_kernel_spmd
    arrays = host_arrays({n: np.asarray(v) for n, v in inputs.items()})
    nc = bacc.Bacc("TRN2", target_bir_lowering=False, num_devices=1)
    build(nc, {n: v.shape for n, v in arrays.items()})
    r = run_bass_kernel_spmd(nc, [{f"in_{n}": v for n, v in arrays.items()}], core_ids=[0])
    out = r.results[0]["out_0"]
    return np.ascontiguousarray(out.reshape(P, D_TILES, TOKENS).transpose(2, 1, 0)).reshape(1, TOKENS, D_MODEL)
```
